# Optimizing a Trainium2 kernel written in Bass

```python
import math
import jax, jax.numpy as jnp
from jax import lax
import numpy as np

D_MODEL = 1024
BATCH = 1
SEQ = 512
DEPTH = 2
DEC_BATCH = 1
DEC_SEQ = 512
PAST_LEN = 128

MLA_HEADS = 8
MLA_NOPE = 64
MLA_ROPE = 32
MLA_V = 64
Q_LORA = 256
KV_LORA = 128
ROPE_THETA = 10000.0
Q_BLOCK = 128
GDN_HEADS = 8
GDN_DK = 64
GDN_DV = 64
CONV_WIDTH = 3
CHUNK = 64
D_FF = -(-8 * D_MODEL // (3 * 256)) * 256
NORM_EPS = 1e-6

MIX_WIDTH = MLA_HEADS * MLA_V + GDN_HEADS * GDN_DV
QKV_CH = GDN_HEADS * (2 * GDN_DK + GDN_DV)
IN_SPLITS = (Q_LORA, KV_LORA, MLA_ROPE, QKV_CH, GDN_HEADS * GDN_DV, 2 * GDN_HEADS, 2 * GDN_HEADS)
IN_COLS = sum(IN_SPLITS)
IN_SPLIT_POINTS = tuple(int(v) for v in np.cumsum(IN_SPLITS)[:-1])

kernel_name = "hymba_mla_gdn_bidir_encoder"

def rms_norm(x, g):
    xf = x.astype(jnp.float32)
    y = xf * lax.rsqrt(jnp.mean(xf * xf, axis=-1, keepdims=True) + NORM_EPS)
    return (y * g.astype(jnp.float32)).astype(x.dtype)

def l2_normalize(x):
    xf = x.astype(jnp.float32)
    return xf * lax.rsqrt(jnp.sum(xf * xf, axis=-1, keepdims=True) + NORM_EPS)

def rope_tables(seq):
    pos = jnp.arange(seq, dtype=jnp.float32)
    inv = ROPE_THETA ** (-jnp.arange(0, MLA_ROPE, 2, dtype=jnp.float32) / MLA_ROPE)
    ang = pos[:, None] * inv[None, :]
    return jnp.cos(ang), jnp.sin(ang)

def apply_rope(x, cos, sin):
    c = cos[None, :, None, :].astype(x.dtype)
    s = sin[None, :, None, :].astype(x.dtype)
    x1, x2 = x[..., : MLA_ROPE // 2], x[..., MLA_ROPE // 2:]
    return jnp.concatenate([x1 * c - x2 * s, x2 * c + x1 * s], axis=-1)

def mla_mixer(q_lat, kv_lat, k_rope, q_norm, w_q_up, kv_norm, w_kv_up, cos, sin):
    B, S, _ = q_lat.shape
    q = (rms_norm(q_lat, q_norm) @ w_q_up).reshape(B, S, MLA_HEADS, MLA_NOPE + MLA_ROPE)
    q = jnp.concatenate([q[..., :MLA_NOPE], apply_rope(q[..., MLA_NOPE:], cos, sin)], axis=-1)
    kv = (rms_norm(kv_lat, kv_norm) @ w_kv_up).reshape(B, S, MLA_HEADS, MLA_NOPE + MLA_V)
    k_nope, v = kv[..., :MLA_NOPE], kv[..., MLA_NOPE:]
    k_pe = apply_rope(k_rope[:, :, None, :], cos, sin)
    k = jnp.concatenate([k_nope, jnp.broadcast_to(k_pe, (B, S, MLA_HEADS, MLA_ROPE))], axis=-1)
    scale = (MLA_NOPE + MLA_ROPE) ** -0.5
    nb = S // Q_BLOCK
    qb = jnp.moveaxis(q.reshape(B, nb, Q_BLOCK, MLA_HEADS, MLA_NOPE + MLA_ROPE), 1, 0)

    def attend(q_blk):
        s = jnp.einsum('bqhd,bkhd->bhqk', q_blk, k).astype(jnp.float32) * scale
        p = jax.nn.softmax(s, axis=-1).astype(v.dtype)
        return jnp.einsum('bhqk,bkhv->bqhv', p, v)

    o = lax.map(attend, qb)
    return jnp.moveaxis(o, 0, 1).reshape(B, S, MLA_HEADS * MLA_V)

def depthwise_conv_centred(x, w):
    C = x.shape[-1]
    return lax.conv_general_dilated(
        x, w[:, None, :].astype(x.dtype), window_strides=(1,),
        padding=[(CONV_WIDTH // 2, CONV_WIDTH // 2)],
        dimension_numbers=('NWC', 'WIO', 'NWC'), feature_group_count=C)

def gated_delta_chunked(q, k, v, g, beta):
    B, S, H, DK = q.shape
    DV = v.shape[-1]
    n = S // CHUNK

    def to_chunks(t):
        t = jnp.moveaxis(t.astype(jnp.float32), 2, 1)
        return t.reshape((B, H, n, CHUNK) + t.shape[3:])

    q = to_chunks(q) * (DK ** -0.5)
    k = to_chunks(k)
    v = to_chunks(v)
    g = to_chunks(g)
    beta = to_chunks(beta)
    gc = jnp.cumsum(g, axis=-1)
    idx = jnp.arange(CHUNK)
    incl = idx[:, None] >= idx[None, :]
    strict = idx[:, None] > idx[None, :]
    decay = jnp.exp(jnp.where(incl, gc[..., :, None] - gc[..., None, :], -jnp.inf))
    kb = k * beta[..., None]
    m = jnp.where(strict, jnp.einsum('bhnid,bhnjd->bhnij', kb, k) * decay, 0.0)
    rhs = jnp.concatenate([v * beta[..., None], kb * jnp.exp(gc)[..., None]], axis=-1)
    sol = lax.linalg.triangular_solve(m, rhs, left_side=True, lower=True, unit_diagonal=True)
    u, w = sol[..., :DV], sol[..., DV:]
    attn = jnp.einsum('bhnid,bhnjd->bhnij', q, k) * decay
    qg = q * jnp.exp(gc)[..., None]
    kg = k * jnp.exp(gc[..., -1:] - gc)[..., None]
    g_last = jnp.exp(gc[..., -1])
    xs = tuple(jnp.moveaxis(t, 2, 0) for t in (qg, kg, u, w, attn, g_last))

    def step(state, inp):
        qg_c, kg_c, u_c, w_c, attn_c, gl_c = inp
        v_new = u_c - jnp.einsum('bhcd,bhdv->bhcv', w_c, state)
        o = jnp.einsum('bhcd,bhdv->bhcv', qg_c, state) + jnp.einsum('bhij,bhjv->bhiv', attn_c, v_new)
        state = state * gl_c[..., None, None] + jnp.einsum('bhcd,bhcv->bhdv', kg_c, v_new)
        return state, o

    _, o = lax.scan(step, jnp.zeros((B, H, DK, DV), jnp.float32), xs)
    o = jnp.moveaxis(o, 0, 2).reshape(B, H, S, DV)
    return jnp.moveaxis(o, 1, 2)

def gdn_mixer(qkv, z, a, b, conv_w, a_log, dt_bias, gdn_norm):
    B, S, _ = qkv.shape
    qkv = jax.nn.silu(depthwise_conv_centred(qkv, conv_w))
    qd = GDN_HEADS * GDN_DK
    q = l2_normalize(qkv[..., :qd].reshape(B, S, GDN_HEADS, GDN_DK))
    k = l2_normalize(qkv[..., qd:2 * qd].reshape(B, S, GDN_HEADS, GDN_DK))
    v = qkv[..., 2 * qd:].reshape(B, S, GDN_HEADS, GDN_DV)
    a = a.astype(jnp.float32).reshape(B, S, 2, GDN_HEADS)
    b = b.astype(jnp.float32).reshape(B, S, 2, GDN_HEADS)
    g = -jnp.exp(a_log.astype(jnp.float32)) * jax.nn.softplus(a + dt_bias.astype(jnp.float32))
    beta = jax.nn.sigmoid(b)
    o_fwd = gated_delta_chunked(q, k, v, g[:, :, 0], beta[:, :, 0])
    flip = lambda t: jnp.flip(t, axis=1)
    o_bwd = flip(gated_delta_chunked(flip(q), flip(k), flip(v), flip(g[:, :, 1]), flip(beta[:, :, 1])))
    o = (o_fwd + o_bwd).astype(qkv.dtype)
    o = rms_norm(o, gdn_norm) * jax.nn.silu(z.reshape(B, S, GDN_HEADS, GDN_DV))
    return o.reshape(B, S, GDN_HEADS * GDN_DV)

def trunk(x, norm_attn, w_in, q_norm, w_q_up, kv_norm, w_kv_up, conv_w, a_log, dt_bias,
          gdn_norm, w_out, norm_ffn, w_gate, w_up, w_down, norm_final):
    cos, sin = rope_tables(x.shape[1])
    for l in range(DEPTH):
        h = rms_norm(x, norm_attn[l]) @ w_in[l]
        q_lat, kv_lat, k_rope, qkv, z, a, b = jnp.split(h, IN_SPLIT_POINTS, axis=-1)
        y_mla = mla_mixer(q_lat, kv_lat, k_rope, q_norm[l], w_q_up[l], kv_norm[l], w_kv_up[l], cos, sin)
        y_gdn = gdn_mixer(qkv, z, a, b, conv_w[l], a_log[l], dt_bias[l], gdn_norm[l])
        x = x + jnp.concatenate([y_mla, y_gdn], axis=-1) @ w_out[l]
        hn = rms_norm(x, norm_ffn[l])
        x = x + (jax.nn.silu(hn @ w_gate[l]) * (hn @ w_up[l])) @ w_down[l]
    return rms_norm(x, norm_final)

def setup_inputs(seed: int = 0) -> dict:
    key = jax.random.key(seed)
    ks = jax.random.split(key, 20)
    f32 = jnp.float32

    def w(k, shape, fan_in):
        return jax.random.normal(k, shape, f32) * (fan_in ** -0.5)

    def gain(k, shape):
        return 1.0 + 0.02 * jax.random.normal(k, shape, f32)

    dt = jnp.exp(jax.random.uniform(ks[12], (DEPTH, 2, GDN_HEADS), f32, math.log(1e-3), math.log(1e-1)))
    return {
        "x_prompt": jax.random.normal(ks[0], (BATCH, SEQ, D_MODEL), f32),
        "x_sample": jax.random.normal(ks[1], (DEC_BATCH, DEC_SEQ, D_MODEL), f32),
        "norm_attn": gain(ks[2], (DEPTH, D_MODEL)),
        "w_in": w(ks[3], (DEPTH, D_MODEL, IN_COLS), D_MODEL),
        "q_norm": gain(ks[4], (DEPTH, Q_LORA)),
        "w_q_up": w(ks[5], (DEPTH, Q_LORA, MLA_HEADS * (MLA_NOPE + MLA_ROPE)), Q_LORA),
        "kv_norm": gain(ks[6], (DEPTH, KV_LORA)),
        "w_kv_up": w(ks[7], (DEPTH, KV_LORA, MLA_HEADS * (MLA_NOPE + MLA_V)), KV_LORA),
        "conv_w": w(ks[8], (DEPTH, CONV_WIDTH, QKV_CH), CONV_WIDTH),
        "a_log": jnp.log(jax.random.uniform(ks[9], (DEPTH, 2, GDN_HEADS), f32, 1.0, 16.0)),
        "dt_bias": dt + jnp.log(-jnp.expm1(-dt)),
        "gdn_norm": gain(ks[10], (DEPTH, GDN_DV)),
        "w_out": w(ks[11], (DEPTH, MIX_WIDTH, D_MODEL), MIX_WIDTH),
        "norm_ffn": gain(ks[13], (DEPTH, D_MODEL)),
        "w_gate": w(ks[14], (DEPTH, D_MODEL, D_FF), D_MODEL),
        "w_up": w(ks[15], (DEPTH, D_MODEL, D_FF), D_MODEL),
        "w_down": w(ks[16], (DEPTH, D_FF, D_MODEL), D_FF),
        "norm_final": gain(ks[17], (D_MODEL,)),
    }

def reference(x_prompt, x_sample, norm_attn, w_in, q_norm, w_q_up, kv_norm, w_kv_up, conv_w,
              a_log, dt_bias, gdn_norm, w_out, norm_ffn, w_gate, w_up, w_down, norm_final):
    y_prompt = trunk(x_prompt, norm_attn, w_in, q_norm, w_q_up, kv_norm, w_kv_up, conv_w, a_log,
                     dt_bias, gdn_norm, w_out, norm_ffn, w_gate, w_up, w_down, norm_final)
    y_sample = trunk(x_sample, norm_attn, w_in, q_norm, w_q_up, kv_norm, w_kv_up, conv_w, a_log,
                     dt_bias, gdn_norm, w_out, norm_ffn, w_gate, w_up, w_down, norm_final)
    return (y_prompt, y_sample)


_drawn_inputs = setup_inputs


def setup_inputs(seed=0):
    import zlib

    import numpy as np

    out = dict(_drawn_inputs(seed))
    spreads = {}
    factors = {'q_norm': 8.0, 'kv_norm': 8.0, 'gdn_norm': 3.859, 'norm_ffn': 2.701, 'norm_final': 2.867}
    for name, (base, spread) in spreads.items():
        noise = np.random.default_rng([zlib.crc32(name.encode()), seed]).standard_normal(out[name].shape)
        drawn = base * np.exp(spread * noise) if base else spread * noise
        out[name] = __import__('jax').numpy.asarray(drawn.astype(out[name].dtype))
    for name, factor in factors.items():
        out[name] = (out[name] * factor).astype(out[name].dtype)
    return out
```

```python
from contextlib import ExitStack

import numpy as np
import concourse.bass as bass
from concourse import mybir

F32 = mybir.dt.float32
F32R = mybir.dt.float32r
ALU = mybir.AluOpType
ACT = mybir.ActivationFunctionType
AX_X = mybir.AxisListType.X

P = 128
D = 1024
KD = D // P
S = 512
NSEQ = 2
DEPTH = 2
HEADS = 8
NOPE, ROPE, DV = 64, 32, 64
QK = NOPE + ROPE
Q_LORA, KV_LORA = 256, 128
FF = 2816
NF = FF // P
EPS = 1e-6
ATT_SCALE = float(QK) ** -0.5
CH = 64
NCH = S // CH
PAIRS = HEADS // 2
SW = PAIRS * CH
LEVELS = 6
DOWN_K = (8, 7, 7)

W_IN, W_Q, W_KV, W_OUT, W_GU, W_DOWN = 20, 2, 2, KD, 2 * NF, 3 * KD
B_Q = W_IN
B_KV = B_Q + W_Q
B_OUT = B_KV + W_KV
B_GU = B_OUT + W_OUT
B_DOWN = B_GU + W_GU
BLOCKS = B_DOWN + W_DOWN
BW = KD * P

T_Q = W_IN
T_KN = T_Q + HEADS
T_V = T_KN + HEADS
T_OUT = T_V + S // P
T_GU = T_OUT + KD
T_DOWN = T_GU + 2 * NF
TILES = T_DOWN + KD

L_LAT, L_Y, L_FFN, L_A = KD, KD + 3, KD + 7, 2 * KD + 7
SPLITS = L_A + NF
TMPS = L_A

N_LAT, N_L2, N_Y, N_FFN, SUMS = 1, 3, 11, 15, 16
Q_LAT, Q_L2, Q_Y, Q_FFN, SQUARES = KD, KD + 3, KD + 11, KD + 15, 2 * KD + 15

PT_QLAT, PT_KVLAT, PT_MISC, PT_Q, PT_K, PT_V, PT_Z = 0, 2, 3, 4, 8, 12, 16
ROW_B = 32

C_NA, C_NF, C_QN, C_KVN, C_CONV, C_DT, C_ALOG, C_GN = 0, 8, 16, 18, 19, 55, 56, 57
NPAR = 58


def constants():
    t = np.arange(CH)
    cols, at = [], {}

    def add(name, m):
        full = np.zeros((P, m.shape[1]), np.float32)
        full[:m.shape[0]] = m
        at[name] = (sum(c.shape[1] for c in cols), m.shape[1])
        cols.append(full)

    def two(m):
        return np.kron(np.eye(2), m)

    le, ge = t[:, None] <= t[None, :], t[:, None] >= t[None, :]
    gt, lt = t[:, None] > t[None, :], t[:, None] < t[None, :]
    add("ones", np.ones((P, P)))
    add("ones_pair", two(np.ones((CH, CH))))
    add("eye", np.eye(P))
    add("after0", two(gt))
    add("after1", two(lt))
    add("upto0", np.tile(le, (2, 1)))
    add("upto1", np.tile(ge, (2, 1)))
    add("eye_pair", np.tile(np.eye(CH), (2, 1)))
    for d in range(2):
        for l in range(LEVELS):
            s = 1 << l
            j, i = t[:, None], t[None, :]
            if d:
                j, i = i, j
            m = (i // (2 * s) == j // (2 * s)) & (i % (2 * s) >= s) & (j % (2 * s) < s)
            add(f"join{d}{l}", np.tile(m, (2, 1)))
    for p in range(2):
        m = np.zeros((48, 16))
        for d in range(2):
            for q in range(PAIRS):
                m[d * HEADS + 2 * q + p, d * PAIRS + q] = 1
                m[ROW_B + d * HEADS + 2 * q + p, 8 + d * PAIRS + q] = 1
        add(f"pick{p}", m)
    pos = np.arange(S, dtype=np.float32)
    inv = np.float32(10000.0) ** (-np.arange(0, ROPE, 2, dtype=np.float32) / np.float32(ROPE))
    ang = pos[:, None] * inv[None, :].astype(np.float32)
    cos, sin = np.cos(ang).T, np.sin(ang).T
    rope = np.zeros((P, S))
    rope[64:96] = np.concatenate([cos, cos])
    rope[96:128] = np.concatenate([-sin, sin])
    add("rope", rope)
    add("eps", np.full((P, 1), EPS))
    return np.concatenate(cols, 1).astype(np.float32), at


def build(nc, xT, w_in, w_q, w_kv, w_out, w_gu, w_down, par, gfin, const, out):
    _, at = constants()
    with ExitStack() as ctx:
        base = 17536
        total = (229344 - base) // 4
        pos = 0

        def take(name, shape, dt=F32):
            nonlocal pos
            n = int(np.prod(shape[1:]))
            assert pos + n <= total, (name, pos + n, total)
            t = nc.alloc_sbuf_tensor_at(name, shape, dt, offset=base + 4 * pos)
            pos += (n + 7) // 8 * 8
            return t

        X = take("X", [P, NSEQ, KD, S])
        H_hi = take("H_hi", [P, KD, S], F32R)
        H_lo = take("H_lo", [P, KD, S], F32R)
        Wraw = take("Wraw", [P, 2, BW])
        Whi = take("Whi", [P, 2, BW], F32R)
        Wlo = take("Wlo", [P, 2, BW], F32R)
        C = take("C", [P, const.shape[1]])
        PAR = take("PAR", [P, NPAR])
        GFIN = take("GFIN", [P, KD])
        NEGA = take("NEGA", [P, 1])
        stat = take("stat", [P, 4, 4])
        sq = take("sq", [P, 2, S])
        rstd = take("rstd", [P, S])
        tmp = take("tmp", [P, 2, S])
        region = pos
        PRJ = take("PRJ", [P, W_IN, S])
        O = PRJ[:, 0:4, :]
        work = pos
        QN_hi = take("QN_hi", [P, 3, S], F32R)
        QN_lo = take("QN_lo", [P, 3, S], F32R)
        KH = take("KH", [QK, HEADS, S])
        QH = take("QH", [QK, HEADS, S])
        V = take("V", [P, S // P, HEADS * DV])
        VS = take("VS", [P, 2, S // P, DV])
        RT = take("RT", [P, 2, S])
        pos = work
        PEXP = take("PEXP", [P, 2, S])
        PT = take("PT", [P, S // P, S])
        pos = work
        GT = take("GT", [P, NCH, 16])
        G = take("G", [P, S])
        G2 = take("G2", [P, 2, S])
        gdn = []
        for d in range(2):
            g = {n: take(f"{n}{d}", [P, SW])
                 for n in "kc qc vc r1 rb dtm db wk kbe qg mt at ys r vn st ssc".split()}
            g["dte"] = take(f"dte{d}", [P, 2 * SW])
            g["ttt"] = take(f"ttt{d}", [P, 2, SW])
            g["ml"] = take(f"ml{d}", [P, 2, SW])
            g["kv"] = take(f"kv{d}", [P, 2 * SW])
            g["col"] = take(f"col{d}", [P, 16])
            gdn.append(g)
        pos = region
        A_hi = take("A_hi", [P, NF, S], F32R)
        A_lo = take("A_lo", [P, NF, S], F32R)
        SG = take("SG", [P, 2, S])

        def c(name, rows=slice(0, P)):
            a, n = at[name]
            return C[rows, a:a + n]

        def pairs(ap):
            return ap.rearrange("p (q t) -> p q t", q=PAIRS)

        def spread(ap, n, w=CH):
            return ap.unsqueeze(2).to_broadcast([P, n, w])

        def each(ap, n=PAIRS, w=CH):
            return ap.unsqueeze(1).to_broadcast([P, n, w])

        def tile_of(t, i, rows=slice(0, P)):
            return t[rows, bass.ds(i, 1), :].rearrange("p o t -> p (o t)")

        def x_tile(s, k):
            return X[:, bass.ds(s, 1), k, :].rearrange("p o t -> p (o t)")

        bank = [ctx.enter_context(nc.psum_tensor(f"bank{i}", [P, S], F32)) for i in range(8)]
        ss_bank = bank[7]

        def sem(name):
            return ctx.enter_context(nc.semaphore(name))

        const_loaded, x_loaded, par_loaded = sem("const_loaded"), sem("x_loaded"), sem("par_loaded")
        out_written = [sem("out_written0"), sem("out_written1")]
        w_loaded = [sem("w_loaded0"), sem("w_loaded1")]
        w_hi, w_lo, down_part = sem("w_hi_ready"), sem("w_lo_ready"), sem("down_part_used")
        sq_ready, sq_used, ln_ready, rstd_ready = (
            sem("sq_ready"), sem("sq_used"), sem("ln_ready"), sem("rstd_ready"))
        tmp_ready, hi_ready, lo_ready = sem("tmp_ready"), sem("hi_ready"), sem("lo_ready")
        tile_ready = sem("tile_ready")
        tile_free = [sem("tile_free0"), sem("tile_free1")]
        conv_step, silu_ready = sem("conv_step"), sem("silu_ready")
        krope_parts, krope_ready = sem("krope_parts"), sem("krope_ready")
        qrope_parts, qrope_ready = sem("qrope_parts"), sem("qrope_ready")
        head_staged = sem("head_staged")
        sc_ready, max_ready, bias_ready, exp_ready, rsum_ready, prob_ready = (
            sem("scores_ready"), sem("max_ready"), sem("bias_ready"), sem("exp_ready"), sem("rsum_ready"),
            sem("prob_ready"))
        pt_psum, pt_ready, yhi_ready, ylo_ready = (
            sem("pt_psum_ready"), sem("pt_ready"), sem("yhi_ready"),
            sem("ylo_ready"))
        pv_done = [sem("pv_done_even"), sem("pv_done_odd")]
        g_zero, gate_step, decay_step = sem("g_zero"), sem("gate_step"), sem("decay_step")
        gt_psum, gt_ready, l2_ready, o_zero = sem("gt_psum_ready"), sem("gt_ready"), sem("l2_ready"), sem("o_zero")
        gated_step, fin_ready = sem("gated_step"), sem("fin_ready")
        idle = {str(x.engine): sem(f"idle_{i}") for i, x in enumerate((nc.tensor, nc.vector, nc.scalar, nc.gpsimd))}
        per_dir = ("staged decay_rhs decay_psum beta_psum cols_psum decay_exp cols_exp dtm db kbe_qg kk_psum "
                   "mt_at nat_psum kv masked b1_psum y_psum y_ready z_psum t_ready ks_psum r_ready vn_psum "
                   "vn_ready su_psum o_psum scaled state_new o_added").split()
        gs = [{n: sem(f"{n}{d}") for n in per_dir} for d in range(2)]
        B = [bank[0:3], bank[3:6]]


        def wait_x(e, it, half):
            for b in range(2):
                e.wait_ge(tile_free[b], it * (TILES // 2) + (half * (T_GU // 2) + 1))

        def wait_tile_out(e, it, t):
            e.wait_ge(tile_free[t % 2], it * (TILES // 2) + (t // 2 + 2))

        def alone(e):
            e.sem_inc(idle[str(e.engine)], 1)

        block = ctx.enter_context(nc.Block())

        @block.sync
        def _(e):
            for s_, n in ((lo_ready, 2), (w_lo, 2), (sq_used, 2), (tile_free[0], 1), (tile_free[1], 1),
                          (ln_ready, 1), (ylo_ready, 1), (pv_done[0], 1), (pv_done[1], 1), (gs[0]["o_added"], 1), (gs[1]["o_added"], 1)):
                e.sem_inc(s_, n)
            e.dma_start(C[:, :], const).then_inc(const_loaded, 16)
            e.dma_start(GFIN[:, :], gfin).then_inc(const_loaded, 16)
            for s in range(NSEQ):
                e.dma_start(X[:, s, :, :], xT[s].rearrange("k p t -> p k t")).then_inc(x_loaded, 16)
            with e.Fori(0, DEPTH) as L, e.Fori(0, NSEQ) as s:
                it = L * NSEQ + s
                wait_x(e, it, 0)
                e.dma_start(PAR[:, :], par[bass.ds(L, 1), :, :].rearrange("o p n -> p (o n)")).then_inc(par_loaded, 16)

                def load(b, slot, src, width):
                    e.wait_ge(w_lo, it * BLOCKS + (b + 1))
                    e.dma_start(Wraw[:, slot, 0:width], src).then_inc(w_loaded[slot], 16)

                def loads(b0, n, w, width):
                    with e.Fori(0, n // 2) as half:
                        i = half * 2
                        for j in range(2):
                            load(i + (b0 + j), j, w[bass.ds(L * n + i + j, 1), :, :].rearrange("o p n -> p (o n)"),
                                 width)

                loads(0, W_IN, w_in, BW)
                loads(B_Q, W_Q, w_q, BW)
                loads(B_KV, W_KV, w_kv, S)
                loads(B_OUT, W_OUT, w_out, BW)
                loads(B_GU, W_GU, w_gu, BW)
                with e.Fori(0, KD // 2) as half:
                    j = half * 2
                    for jj in range(2):
                        at_k = 0
                        for r, nk in enumerate(DOWN_K):
                            src = w_down[bass.ds(L * KD + j + jj, 1), :, at_k * P:(at_k + nk) * P]
                            load(j * 3 + (B_DOWN + 3 * jj + r), (3 * jj + r) % 2,
                                 src.rearrange("o p n -> p (o n)"), nk * P)
                            at_k += nk
            for s in range(NSEQ):
                for k in range(KD):
                    e.wait_ge(fin_ready, s * KD + k + 1)
                    e.dma_start(out[s, k], tmp[:, k % 2, :]).then_inc(out_written[k % 2], 16)
            for slot in range(2):
                e.wait_ge(out_written[slot], 16 * NSEQ * KD // 2)

        @block.scalar
        def _(e):
            e.wait_ge(const_loaded, 32)
            e.wait_ge(x_loaded, 16 * NSEQ)

            def square(inp, q0, k):
                e.wait_ge(sq_used, q0 + (k + 1 + (k == 0)))
                alone(e)
                e.activation(sq[:, k % 2, :], inp, ACT.Square).then_inc(sq_ready, 1)

            def root(n0, n, q0, k, width):
                e.wait_ge(sq_used, q0 + (k + 2))
                e.activation(rstd[:, :], ss_bank[:, :], ACT.Ln, scale=1.0 / width, bias=c("eps"))\
                    .then_inc(ln_ready, 1)
                e.wait_ge(ln_ready, n0 + (n + 2))
                e.activation(rstd[:, :], rstd[:, :], ACT.Exp, scale=-0.5).then_inc(rstd_ready, 1)

            with e.Fori(0, DEPTH) as L, e.Fori(0, NSEQ) as s:
                it = e.snap(L * NSEQ + s)
                n0, q0, l0, m0 = it * SUMS, it * SQUARES, it * SPLITS, it * TMPS
                b0, t0 = it * BLOCKS, it * TILES

                def split_w(b, slot, width, used):
                    e.wait_ge(w_loaded[slot], b0 * 8 + ((b - slot) * 8 + 16))
                    if used is not None:
                        e.wait_ge(used[0], used[1])
                    e.activation(Whi[:, slot, 0:width], Wraw[:, slot, 0:width], ACT.Copy).then_inc(w_hi, 1)

                def after_tile(t):
                    return tile_ready, t0 + (t + 1)

                def split_tmp(l, dst):
                    e.wait_ge(tmp_ready, m0 + (l + 1))
                    e.activation(dst, tmp[:, l % 2, :], ACT.Copy).then_inc(hi_ready, 1)

                wait_x(e, it, 0)
                for b in range(2):
                    split_w(b, b, BW, None)
                for k in range(KD):
                    square(x_tile(s, k), q0, k)
                root(n0, 0, q0, KD, D)
                for k in range(KD):
                    split_tmp(k, H_hi[:, k, :])

                for t in range(W_IN):
                    b = t + 2
                    split_w(b, b % 2, BW, after_tile(t))
                    if PT_Q <= t < PT_Z:
                        wait_tile_out(e, it, t)
                        e.activation(PRJ[:, t, :], PRJ[:, t, :], ACT.Silu).then_inc(silu_ready, 1)
                    elif t >= PT_Z:
                        e.activation(PRJ[:, t, :], bank[t % 2][:, :], ACT.Silu).then_inc(tile_free[t % 2], 1)

                for t in range(PT_Q):
                    wait_tile_out(e, it, t)
                for k in range(2):
                    square(PRJ[:, PT_QLAT + k, :], q0, Q_LAT + k)
                e.wait_ge(tmp_ready, m0 + KD)
                root(n0, N_LAT, q0, Q_LAT + 2, Q_LORA)
                for k in range(2):
                    split_tmp(L_LAT + k, QN_hi[:, k, :])
                square(PRJ[:, PT_KVLAT, :], q0, Q_LAT + 2)
                root(n0, N_LAT + 1, q0, Q_LAT + 3, KV_LORA)
                split_tmp(L_LAT + 2, QN_hi[:, 2, :])
                e.wait_ge(krope_parts, it * 3 + 3)
                e.activation(KH[64:96, :, :], RT[64:96, 0:1, :].to_broadcast([ROPE, HEADS, S]), ACT.Copy)\
                    .then_inc(krope_ready, 1)
                split_w(B_KV, 0, S, after_tile(T_Q + 3))
                split_w(B_KV + 1, 1, S, after_tile(T_Q + 7))
                split_w(B_OUT, 0, BW, after_tile(T_KN + 7))
                for t in range(T_V, T_V + S // P):
                    e.wait_ge(tile_ready, t0 + (t + 1))
                    e.activation(V[:, t - T_V, :], bank[t % 2][:, :], ACT.Copy).then_inc(tile_free[t % 2], 1)
                split_w(B_OUT + 1, 1, BW, after_tile(T_V + 3))

                with e.Fori(0, PAIRS) as hp:
                    for odd in range(2):
                        h4 = (it * HEADS + hp * 2 + odd) * 4

                        def evict(j):
                            e.wait_ge(pt_psum, h4 + (j + 1))
                            e.activation(PT[:, :, j * P:(j + 1) * P],
                                         bank[4 + j % 2][:, :].rearrange("p (k q) -> p k q", k=4), ACT.Copy)\
                                .then_inc(pt_ready, 1)

                        for j in range(4):
                            e.wait_ge(bias_ready, h4 + (j + 1))
                            if j >= 2:
                                e.wait_ge(pt_psum, h4 + (j - 1))
                            e.activation(PEXP[:, j % 2, :], bank[2 + j % 2][:, :], ACT.Exp, bias=stat[:, j, 1:2],
                                         scale=ATT_SCALE, accum_out=stat[:, j, 2:3]).then_inc(exp_ready, 1)
                            if j:
                                evict(j - 1)
                        evict(3)
                    e.wait_ge(pv_done[1], it * PAIRS + hp + 2)
                    alone(e)
                    e.activation(tile_of(H_hi, hp), bank[6][:, :], ACT.Copy).then_inc(yhi_ready, 1)

                e.wait_ge(par_loaded, it * 16 + 16)
                e.wait_ge(g_zero, it + 1)
                e.activation(G2[0:16, 0, :], PRJ[0:16, PT_MISC, :], ACT.Abs, bias=PAR[0:16, C_DT:C_DT + 1])\
                    .then_inc(gate_step, 1)
                e.wait_ge(gate_step, it * 5 + 1)
                e.activation(G2[0:16, 0, :], G2[0:16, 0, :], ACT.Exp, scale=-1.0).then_inc(gate_step, 1)
                e.wait_ge(gate_step, it * 5 + 2)
                e.activation(G2[0:16, 0, :], G2[0:16, 0, :], ACT.Ln, bias=c("ones")[0:16, 0:1])\
                    .then_inc(gate_step, 1)
                e.activation(NEGA[0:16, :], PAR[0:16, C_ALOG:C_ALOG + 1], ACT.Exp).then_inc(gate_step, 1)
                e.activation(G[32:48, :], PRJ[32:48, PT_MISC, :], ACT.Sigmoid).then_inc(gate_step, 1)
                e.wait_ge(silu_ready, it * 12 + 12)
                for t in range(8):
                    square(PRJ[:, PT_Q + t, :], q0, Q_L2 + t)
                    if t:
                        e.wait_ge(l2_ready, it * 8 + t)
                    root(n0, N_L2 + t, q0, Q_L2 + t + 1, 1)
                e.wait_ge(gt_psum, it + 1)
                e.activation(GT[:, :, :].rearrange("p n g -> p (n g)"), bank[2][:, 0:NCH * 16], ACT.Copy)\
                    .then_inc(gt_ready, 1)
                e.wait_ge(gt_ready, it + 1)
                e.wait_ge(l2_ready, it * 8 + 8)

                with e.Fori(0, NCH) as n:
                    st = e.snap(it * NCH + n)
                    chunk = [n, (NCH - 1) - n]
                    for d in range(2):
                        g, q = gdn[d], gs[d]
                        e.wait_ge(q["o_added"], st + 1)
                        alone(e)
                        for nm, t in (("kc", PT_K), ("qc", PT_Q), ("vc", PT_V)):
                            e.activation(pairs(g[nm][:, :]), PRJ[:, t:t + PAIRS, bass.ds(chunk[d] * CH, CH)], ACT.Copy)
                        for to, fr in ((4, 8), (12, 0)):
                            e.activation(g["col"][:, to:to + 4],
                                         GT[:, bass.ds(chunk[d], 1), fr + d * 4:fr + d * 4 + 4]
                                         .rearrange("p o g -> p (o g)"), ACT.Copy)\
                                .then_inc(q["staged"], 1)
                    for d in range(2):
                        g, q = gdn[d], gs[d]
                        e.wait_ge(q["decay_psum"], st + 1)
                        e.activation(g["dte"][:, :], B[d][0][:, :], ACT.Exp).then_inc(q["decay_exp"], 1)
                        e.wait_ge(q["cols_psum"], st + 1)
                        e.activation(g["col"][:, 0:4], B[d][2][:, 0:4], ACT.Exp)
                        e.activation(g["col"][:, 8:12], B[d][2][:, 4:8], ACT.Exp).then_inc(q["cols_exp"], 1)
                    for l in range(1, LEVELS):
                        for d in range(2):
                            g, q = gdn[d], gs[d]
                            e.wait_ge(q["y_psum"], st * 5 + l)
                            e.activation(g["ys"][:, :], B[d][0][:, 0:SW], ACT.Copy).then_inc(q["y_ready"], 1)
                    for d in range(2):
                        g, q = gdn[d], gs[d]
                        e.wait_ge(q["vn_psum"], st + 1)
                        e.activation(g["vn"][:, :], B[d][1][:, 0:SW], ACT.Copy).then_inc(q["vn_ready"], 1)

                for d in range(2):
                    e.wait_ge(gs[d]["o_added"], it * NCH + NCH + 1)
                for t in range(4):
                    square(O[:, t, :], q0, Q_Y + t)
                    if t:
                        e.wait_ge(gated_step, it * 4 + t)
                    root(n0, N_Y + t, q0, Q_Y + t + 1, DV)
                    split_tmp(L_Y + t, H_hi[:, 4 + t, :])

                with e.Fori(0, W_OUT // 2) as half:
                    i = half * 2
                    for j in range(2):
                        split_w(i + (B_OUT + 2 + j), j, BW, after_tile(i + (T_OUT + j)))
                wait_x(e, it, 1)
                for k in range(KD):
                    square(x_tile(s, k), q0, Q_FFN + k)
                root(n0, N_FFN, q0, Q_FFN + KD, D)
                for k in range(KD):
                    split_tmp(L_FFN + k, H_hi[:, k, :])

                def gate_up(f, last):
                    for j in range(2):
                        fj = f + j
                        for m in range(2):
                            if last and j:
                                split_w(B_DOWN + m, m, DOWN_K[m] * P, after_tile(T_DOWN - 2 + m))
                            else:
                                split_w(fj * 2 + (B_GU + 2 + m), m, BW, after_tile(fj * 2 + (T_GU + m)))
                            if m == 0:
                                e.activation(SG[:, j, :], bank[0][:, :], ACT.Silu).then_inc(tile_free[0], 1)
                        e.wait_ge(tile_free[1], it * (TILES // 2) + (fj + (T_GU // 2 + 2)))
                        alone(e)
                        e.activation(tile_of(A_hi, fj) if not last else A_hi[:, fj, :],
                                     tmp[:, (L_A + j) % 2, :], ACT.Copy).then_inc(hi_ready, 1)

                with e.Fori(0, NF // 2 - 1) as half:
                    f = half * 2
                    gate_up(f, False)
                gate_up(NF - 2, True)

                def down_w(j, r):
                    b = j * 3 + (B_DOWN + r)
                    if r == 0:
                        used = down_part, it * (2 * KD) + j * 2
                    elif r == 1:
                        used = tile_ready, t0 + (j + T_DOWN)
                    else:
                        used = down_part, it * (2 * KD) + (j * 2 + 1)
                    return b, used

                def down_split(j, jj, r):
                    b, used = down_w(j + jj, r)
                    split_w(b, (3 * jj + r) % 2, DOWN_K[r] * P, used)

                down_split(0, 0, 2)
                for r in range(3):
                    down_split(0, 1, r)
                with e.Fori(1, KD // 2) as half:
                    j = half * 2
                    for jj in range(2):
                        for r in range(3):
                            down_split(j, jj, r)

            wait_x(e, DEPTH * NSEQ, 0)
            for s in range(NSEQ):
                q0 = DEPTH * NSEQ * SQUARES + s * KD
                for k in range(KD):
                    square(X[:, s, k, :], q0, k)
                if s:
                    e.wait_ge(fin_ready, KD)
                root(DEPTH * NSEQ * SUMS, s, q0, KD, D)

        @block.gpsimd
        def _(e):
            e.wait_ge(const_loaded, 32)
            with e.Fori(0, DEPTH) as L, e.Fori(0, NSEQ) as s:
                it = e.snap(L * NSEQ + s)
                l0, b0, t0 = it * SPLITS, it * BLOCKS, it * TILES

                def low_w(b, slot, width):
                    e.wait_ge(w_hi, b0 + (b + 1))
                    e.tensor_tensor(Wlo[:, slot, 0:width], Wraw[:, slot, 0:width],
                                    Whi[:, slot, 0:width].bitcast(F32), ALU.subtract).then_inc(w_lo, 1)

                def low_tmp(l, parity, dst, hi):
                    e.wait_ge(hi_ready, l0 + (l + 1))
                    e.tensor_tensor(dst, tmp[:, parity, :], hi.bitcast(F32), ALU.subtract).then_inc(lo_ready, 1)

                for b in range(2):
                    low_w(b, b, BW)
                for k in range(KD):
                    low_tmp(k, k % 2, H_lo[:, k, :], H_hi[:, k, :])
                with e.Fori(0, W_IN // 2) as half:
                    i = half * 2
                    for j in range(2):
                        low_w(i + (2 + j), j, BW)
                for k in range(3):
                    low_tmp(L_LAT + k, (L_LAT + k) % 2, QN_lo[:, k, :], QN_hi[:, k, :])
                for b in range(2):
                    low_w(B_KV + b, b, S)
                for b in range(2):
                    low_w(B_OUT + b, b, BW)
                wait_tile_out(e, it, T_V + 2)
                wait_tile_out(e, it, T_V + 3)
                e.wait_ge(qrope_ready, it * HEADS + HEADS)
                alone(e)
                with e.Fori(0, PAIRS) as hp:
                    for odd in range(2):
                        e.wait_ge(pv_done[odd], it * PAIRS + hp + 1)
                        alone(e)
                        e.tensor_copy(RT[0:QK, odd, :], tile_of(QH, hp * 2 + odd, slice(0, QK))).then_inc(head_staged, 1)
                        e.tensor_copy(VS[:, odd, :, :], V[:, :, bass.ds((hp * 2 + odd) * DV, DV)])\
                            .then_inc(head_staged, 1)
                e.wait_ge(ylo_ready, it * PAIRS + PAIRS + 1)
                alone(e)
                e.memset(G[0:48, :], 0.0).then_inc(g_zero, 1)
                e.wait_ge(gate_step, it * 5 + 5)
                e.wait_ge(decay_step, it * 3 + 3)
                alone(e)
                e.memset(O, 0.0).then_inc(o_zero, 1)
                for d in range(2):
                    e.memset(gdn[d]["st"][:, :], 0.0).then_inc(gs[d]["state_new"], 1)
                with e.Fori(0, NCH) as n:
                    st = e.snap(it * NCH + n)
                    for d in range(2):
                        g, q = gdn[d], gs[d]
                        e.wait_ge(q["staged"], st * 2 + 2)
                        e.tensor_tensor(pairs(g["r1"][:, :]), spread(g["col"][:, 12:16], PAIRS),
                                        each(c(f"upto{d}")), ALU.mult).then_inc(q["decay_rhs"], 1)
                        e.tensor_tensor(pairs(g["rb"][:, :]), spread(g["col"][:, 4:8], PAIRS),
                                        each(c("eye_pair")), ALU.mult).then_inc(q["decay_rhs"], 1)
                    for l in range(LEVELS):
                        for d in range(2):
                            g, q = gdn[d], gs[d]
                            if l == 0:
                                e.wait_ge(q["mt_at"], st * 2 + 1)
                            elif l == 2:
                                e.wait_ge(q["t_ready"], st * 6 + 1)
                            elif l > 2:
                                e.wait_ge(q["y_psum"], st * 5 + (l - 2))
                            e.tensor_tensor(pairs(g["ml"][:, l % 2, :]), pairs(g["mt"][:, :]), each(c(f"join{d}{l}")),
                                            ALU.mult).then_inc(q["masked"], 1)
                    for d in range(2):
                        g, q = gdn[d], gs[d]
                        e.wait_ge(q["cols_exp"], st + 1)
                        e.wait_ge(q["state_new"], st + it + 1)
                        e.tensor_tensor(pairs(g["ssc"][:, :]), pairs(g["st"][:, :]), spread(g["col"][:, 8:12], PAIRS),
                                        ALU.mult).then_inc(q["scaled"], 1)
                for t in range(4):
                    low_tmp(L_Y + t, (L_Y + t) % 2, H_lo[:, 4 + t, :], H_hi[:, 4 + t, :])
                with e.Fori(0, W_OUT // 2) as half:
                    i = half * 2
                    for j in range(2):
                        low_w(i + (B_OUT + 2 + j), j, BW)
                for k in range(KD):
                    low_tmp(L_FFN + k, (L_FFN + k) % 2, H_lo[:, k, :], H_hi[:, k, :])

                def gate_up(f, last):
                    for j in range(2):
                        for m in range(2):
                            if last and j:
                                low_w(B_DOWN + m, m, DOWN_K[m] * P)
                            else:
                                low_w((f + j) * 2 + (B_GU + 2 + m), m, BW)
                        a = (lambda t: t[:, f + j, :]) if last else (lambda t: tile_of(t, f + j))
                        low_tmp(f + (L_A + j), (L_A + j) % 2, a(A_lo), a(A_hi))

                with e.Fori(0, NF // 2 - 1) as half:
                    f = half * 2
                    gate_up(f, False)
                gate_up(NF - 2, True)

                low_w(B_DOWN + 2, 0, DOWN_K[2] * P)
                for r in range(3):
                    low_w(B_DOWN + 3 + r, (3 + r) % 2, DOWN_K[r] * P)
                with e.Fori(1, KD // 2) as half:
                    j = half * 2
                    for jj in range(2):
                        for r in range(3):
                            low_w(j * 3 + (B_DOWN + 3 * jj + r), (3 * jj + r) % 2, DOWN_K[r] * P)

        @block.vector
        def _(e):
            e.wait_ge(const_loaded, 32)
            e.wait_ge(x_loaded, 16 * NSEQ)
            with e.Fori(0, DEPTH) as L, e.Fori(0, NSEQ) as s:
                it = e.snap(L * NSEQ + s)
                n0, l0, t0 = it * SUMS, it * SPLITS, it * TILES

                def tmp_free(l):
                    e.wait_ge(lo_ready, l0 + (l + 1 + (isinstance(l, int) and l == 0)))

                def normalise(inp, gain, n, l):
                    e.wait_ge(rstd_ready, n0 + (n + 1))
                    tmp_free(l)
                    e.scalar_tensor_tensor(tmp[:, l % 2, :], inp, gain, rstd[:, :], ALU.mult, ALU.mult)\
                        .then_inc(tmp_ready, 1)

                wait_x(e, it, 0)
                e.wait_ge(par_loaded, it * 16 + 16)
                for k in range(KD):
                    normalise(x_tile(s, k), PAR[:, C_NA + k:C_NA + k + 1], 0, k)

                for t in range(PT_Z):
                    e.wait_ge(tile_ready, t0 + (t + 1))
                    pb, free = bank[t % 2], tile_free[t % 2]
                    if t < PT_Q:
                        e.tensor_copy(PRJ[:, t, :], pb[:, :]).then_inc(free, 1)
                        continue
                    w = [PAR[:, C_CONV + 3 * (t - PT_Q) + i:C_CONV + 3 * (t - PT_Q) + i + 1] for i in range(3)]
                    y = PRJ[:, t, :]
                    e.tensor_scalar(y, pb[:, :], w[1], None, ALU.mult).then_inc(conv_step, 1)
                    e.wait_ge(conv_step, it * 24 + (2 * (t - PT_Q) + 1))
                    e.scalar_tensor_tensor(y[:, 1:S], pb[:, 0:S - 1], w[0], y[:, 1:S], ALU.mult, ALU.add)\
                        .then_inc(conv_step, 1)
                    e.wait_ge(conv_step, it * 24 + (2 * (t - PT_Q) + 2))
                    e.scalar_tensor_tensor(y[:, 0:S - 1], pb[:, 1:S], w[2], y[:, 0:S - 1], ALU.mult, ALU.add)\
                        .then_inc(free, 1)

                for k in range(2):
                    normalise(PRJ[:, PT_QLAT + k, :], PAR[:, C_QN + k:C_QN + k + 1], N_LAT, L_LAT + k)
                normalise(PRJ[:, PT_KVLAT, :], PAR[:, C_KVN:C_KVN + 1], N_LAT + 1, L_LAT + 2)

                r0, r1 = RT[64:96, 0, :], RT[64:96, 1, :]
                e.tensor_tensor(r0, PRJ[64:96, PT_MISC, :], c("rope", slice(64, 96)), ALU.mult).then_inc(krope_parts, 1)
                e.tensor_tensor(r1, PRJ[96:128, PT_MISC, :], c("rope", slice(96, 128)), ALU.mult)\
                    .then_inc(krope_parts, 1)
                e.wait_ge(krope_parts, it * 3 + 2)
                e.tensor_tensor(r0, r0, r1, ALU.add).then_inc(krope_parts, 1)
                e.wait_ge(krope_ready, it + 1)
                for h in range(HEADS):
                    t = T_Q + h
                    pb = bank[t % 2]
                    e.wait_ge(tile_ready, t0 + (t + 1))
                    if h:
                        e.wait_ge(qrope_ready, it * HEADS + h)
                    e.tensor_tensor(r0, pb[64:96, :], c("rope", slice(64, 96)), ALU.mult).then_inc(qrope_parts, 1)
                    e.tensor_tensor(r1, pb[96:128, :], c("rope", slice(96, 128)), ALU.mult).then_inc(qrope_parts, 1)
                    e.tensor_copy(QH[0:64, h, :], pb[0:64, :]).then_inc(tile_free[t % 2], 1)
                    e.wait_ge(qrope_parts, it * 16 + (2 * h + 2))
                    e.tensor_tensor(QH[64:96, h, :], r0, r1, ALU.add).then_inc(qrope_ready, 1)
                for h in range(HEADS):
                    t = T_KN + h
                    e.wait_ge(tile_ready, t0 + (t + 1))
                    e.tensor_copy(KH[0:64, h, :], bank[t % 2][0:64, :]).then_inc(tile_free[t % 2], 1)

                with e.Fori(0, PAIRS) as hp:
                    for odd in range(2):
                        h4 = (it * HEADS + hp * 2 + odd) * 4

                        def maximum(j):
                            e.wait_ge(sc_ready, h4 + (j + 1))
                            e.tensor_reduce(stat[:, j, 0:1], bank[2 + j % 2][:, :], AX_X, ALU.max)\
                                .then_inc(max_ready, 1)
                            e.wait_ge(max_ready, h4 + (j + 1))
                            e.tensor_scalar(stat[:, j, 1:2], stat[:, j, 0:1], -ATT_SCALE, None, ALU.mult)\
                                .then_inc(bias_ready, 1)

                        maximum(0)
                        for j in range(4):
                            if j < 3:
                                maximum(j + 1)
                            e.wait_ge(exp_ready, h4 + (j + 1))
                            e.reciprocal(stat[:, j, 3:4], stat[:, j, 2:3]).then_inc(rsum_ready, 1)
                            e.wait_ge(rsum_ready, h4 + (j + 1))
                            e.tensor_scalar(PEXP[:, j % 2, :], PEXP[:, j % 2, :], stat[:, j, 3:4], None, ALU.mult)\
                                .then_inc(prob_ready, 1)
                    e.wait_ge(yhi_ready, it * PAIRS + hp + 1)
                    e.tensor_tensor(tile_of(H_lo, hp), bank[6][:, :], tile_of(H_hi, hp).bitcast(F32), ALU.subtract)\
                        .then_inc(ylo_ready, 1)

                e.wait_ge(g_zero, it + 1)
                e.tensor_scalar(G2[0:16, 1, :], PRJ[0:16, PT_MISC, :], PAR[0:16, C_DT:C_DT + 1], 0.0, ALU.add, ALU.max)\
                    .then_inc(decay_step, 1)
                e.wait_ge(gate_step, it * 5 + 4)
                e.wait_ge(decay_step, it * 3 + 1)
                e.tensor_tensor(G2[0:16, 1, :], G2[0:16, 1, :], G2[0:16, 0, :], ALU.add).then_inc(decay_step, 1)
                e.wait_ge(decay_step, it * 3 + 2)
                e.tensor_scalar(G[0:16, :], G2[0:16, 1, :], NEGA[0:16, 0:1], -1.0, ALU.mult, ALU.mult)\
                    .then_inc(decay_step, 1)
                for t in range(8):
                    y = PRJ[:, PT_Q + t, :]
                    e.wait_ge(rstd_ready, n0 + (N_L2 + t + 1))
                    e.scalar_tensor_tensor(y, y, CH ** -0.5 if t < PAIRS else 1.0, rstd[:, :], ALU.mult, ALU.mult)\
                        .then_inc(l2_ready, 1)

                e.wait_ge(o_zero, it + 1)
                alone(e)
                with e.Fori(0, NCH) as n:
                    st = e.snap(it * NCH + n)
                    chunk = [n, (NCH - 1) - n]
                    for d in range(2):
                        g, q = gdn[d], gs[d]
                        e.wait_ge(q["decay_exp"], st + 1)
                        e.wait_ge(q["beta_psum"], st + 1)
                        e.tensor_tensor(pairs(g["dtm"][:, :]), pairs(g["dte"][:, 0:SW]), each(c(f"upto{d}")), ALU.mult)\
                            .then_inc(q["dtm"], 1)
                        e.tensor_tensor(g["wk"][:, :], g["dte"][:, SW:], B[d][1][:, 0:SW], ALU.mult)\
                            .then_inc(q["db"], 1)
                    for d in range(2):
                        g, q = gdn[d], gs[d]
                        e.wait_ge(q["dtm"], st + 1)
                        e.tensor_tensor(g["db"][:, :], g["dtm"][:, :], B[d][1][:, 0:SW], ALU.mult)\
                            .then_inc(q["db"], 1)
                    for d in range(2):
                        g, q = gdn[d], gs[d]
                        e.wait_ge(q["db"], st * 2 + 2)
                        e.wait_ge(q["staged"], st * 2 + 2)
                        e.tensor_tensor(g["kbe"][:, :], g["kc"][:, :], g["wk"][:, :], ALU.mult)\
                            .then_inc(q["kbe_qg"], 1)
                        e.tensor_tensor(g["qg"][:, :], g["qc"][:, :], g["dte"][:, SW:], ALU.mult)\
                            .then_inc(q["kbe_qg"], 1)
                    for d in range(2):
                        g, q = gdn[d], gs[d]
                        e.wait_ge(q["kk_psum"], st + 1)
                        e.tensor_tensor(g["mt"][:, :], B[d][2][:, 0:SW], g["db"][:, :], ALU.mult)\
                            .then_inc(q["mt_at"], 1)
                        e.tensor_tensor(g["at"][:, :], B[d][2][:, SW:], g["dtm"][:, :], ALU.mult)\
                            .then_inc(q["mt_at"], 1)
                    for d in range(2):
                        g, q = gdn[d], gs[d]
                        e.wait_ge(q["nat_psum"], st + 1)
                        e.wait_ge(q["cols_exp"], st + 1)
                        e.tensor_tensor(g["kv"][:, :].rearrange("p (q t) -> p q t", q=2 * PAIRS),
                                        B[d][0][:, :].rearrange("p (q t) -> p q t", q=2 * PAIRS),
                                        spread(g["col"][:, 0:8], 2 * PAIRS), ALU.mult).then_inc(q["kv"], 1)
                    for d in range(2):
                        g, q = gdn[d], gs[d]
                        e.wait_ge(q["b1_psum"], st + 1)
                        e.tensor_tensor(pairs(g["ttt"][:, 0, :]), each(c("eye_pair")), pairs(B[d][1][:, 0:SW]),
                                        ALU.subtract)
                        e.tensor_tensor(pairs(g["ttt"][:, 1, :]), each(c("eye_pair")), pairs(g["ml"][:, 0, :]),
                                        ALU.subtract).then_inc(q["t_ready"], 1)
                    for l in range(1, LEVELS):
                        for d in range(2):
                            g, q = gdn[d], gs[d]
                            e.wait_ge(q["z_psum"], st * 5 + l)
                            e.wait_ge(q["t_ready"], st * 6 + l)
                            if l < LEVELS - 1:
                                t2 = g["ttt"][:, :, :].rearrange("p a b -> p (a b)")
                                e.tensor_tensor(t2, t2, B[d][2][:, :], ALU.subtract).then_inc(q["t_ready"], 1)
                            else:
                                t2 = g["ttt"][:, 1, :]
                                e.tensor_tensor(t2, t2, B[d][2][:, SW:], ALU.subtract).then_inc(q["t_ready"], 1)
                    for d in range(2):
                        g, q = gdn[d], gs[d]
                        e.wait_ge(q["ks_psum"], st + 1)
                        e.wait_ge(q["kv"], st + 1)
                        e.tensor_tensor(g["r"][:, :], g["kv"][:, SW:], B[d][0][:, 0:SW], ALU.subtract)\
                            .then_inc(q["r_ready"], 1)
                    for d in range(2):
                        g, q = gdn[d], gs[d]
                        e.wait_ge(q["o_psum"], st + 1)
                        e.wait_ge(q["scaled"], st + 1)
                        e.tensor_tensor(g["st"][:, :], g["ssc"][:, :], B[d][2][:, 0:SW], ALU.add)\
                            .then_inc(q["state_new"], 1)
                        e.wait_ge(gs[1 - d]["o_added"], st + (1 + d))
                        alone(e)
                        oc = O[:, :, bass.ds(chunk[d] * CH, CH)]
                        e.tensor_tensor(oc, oc, pairs(B[d][0][:, 0:SW]), ALU.add).then_inc(q["o_added"], 1)

                for t in range(4):
                    e.wait_ge(rstd_ready, n0 + (N_Y + t + 1))
                    e.scalar_tensor_tensor(O[:, t, :], O[:, t, :], PAR[:, C_GN:C_GN + 1], rstd[:, :],
                                           ALU.mult, ALU.mult).then_inc(gated_step, 1)
                    e.wait_ge(gated_step, it * 4 + (t + 1))
                    tmp_free(L_Y + t)
                    if t == 0:
                        wait_tile_out(e, it, W_IN - 2)
                        wait_tile_out(e, it, W_IN - 1)
                    e.tensor_tensor(tmp[:, (L_Y + t) % 2, :], O[:, t, :], PRJ[:, PT_Z + t, :], ALU.mult)\
                        .then_inc(tmp_ready, 1)

                def residual(t, b, k):
                    e.wait_ge(tile_ready, t0 + t + 1)
                    xt = X[:, bass.ds(s, 1), bass.ds(k, 1), :].rearrange("p o k t -> p (o k t)")
                    e.tensor_tensor(xt, xt, bank[b][:, :], ALU.add).then_inc(tile_free[b], 1)

                with e.Fori(0, KD // 2) as half:
                    i = half * 2
                    for j in range(2):
                        residual(i + (T_OUT + j), j, i + j)
                wait_x(e, it, 1)
                for k in range(KD):
                    normalise(x_tile(s, k), PAR[:, C_NF + k:C_NF + k + 1], N_FFN, L_FFN + k)
                with e.Fori(0, NF // 2) as half:
                    f = half * 2
                    for j in range(2):
                        e.wait_ge(tile_ready, t0 + ((f + j) * 2 + (T_GU + 2)))
                        e.wait_ge(tile_free[0], it * (TILES // 2) + (f + j + (T_GU // 2 + 2)))
                        tmp_free(f + (L_A + j))
                        e.tensor_tensor(tmp[:, (L_A + j) % 2, :], SG[:, j, :], bank[1][:, :], ALU.mult)\
                            .then_inc(tile_free[1], 1)
                with e.Fori(0, KD // 2) as half:
                    i = half * 2
                    for j in range(2):
                        residual(i + (T_DOWN + j), j, i + j)

            wait_x(e, DEPTH * NSEQ, 0)
            for s in range(NSEQ):
                for k in range(KD):
                    n = s * KD + k
                    e.wait_ge(rstd_ready, DEPTH * NSEQ * SUMS + s + 1)
                    if n == 0:
                        e.wait_ge(lo_ready, DEPTH * NSEQ * SPLITS + 2)
                    if n >= 2:
                        e.wait_ge(out_written[k % 2], 16 * (n // 2))
                    e.scalar_tensor_tensor(tmp[:, k % 2, :], X[:, s, k, :], GFIN[:, k:k + 1], rstd[:, :],
                                           ALU.mult, ALU.mult).then_inc(fin_ready, 1)

        @block.tensor
        def _(e):
            e.wait_ge(const_loaded, 32)

            def sum_squares(ones, n_idx, q_idx, k, slot, first, last):
                e.wait_ge(sq_ready, q_idx + (k + 1))
                if first:
                    e.wait_ge(ln_ready, n_idx + 1)
                e.matmul(ss_bank[:, :], ones, sq[:, slot, :], start=first, stop=last).then_inc(sq_used, 1)

            with e.Fori(0, DEPTH) as L, e.Fori(0, NSEQ) as s:
                it = e.snap(L * NSEQ + s)
                n0, q0, l0 = it * SUMS, it * SQUARES, it * SPLITS
                b0, t0 = it * BLOCKS, it * TILES

                def bank_free(t, b):
                    e.wait_ge(tile_free[b], it * (TILES // 2) + ((t - b) // 2 + 1))

                def weights(b):
                    e.wait_ge(w_lo, b0 + (b + 3))

                def three(out_, w, a, first, last):
                    e.matmul(out_, w[0], a[0], start=first, stop=False)
                    e.matmul(out_, w[0], a[1], start=False, stop=False)
                    return e.matmul(out_, w[1], a[0], start=False, stop=last)

                def w_part(slot, a, n):
                    return Whi[:, slot, a:a + n], Wlo[:, slot, a:a + n]

                def dense(slot, b):
                    for k in range(KD):
                        mm = three(bank[b][:, :], w_part(slot, k * P, P), (H_hi[:, k, :], H_lo[:, k, :]),
                                   k == 0, k == KD - 1)
                    return mm

                for k in range(KD):
                    sum_squares(c("ones"), n0, q0, k, k % 2, k == 0, k == KD - 1)
                e.wait_ge(lo_ready, l0 + (KD + 2))
                alone(e)
                with e.Fori(0, W_IN // 2) as i:
                    for j in range(2):
                        weights(i * 2 + j)
                        e.wait_ge(tile_free[j], it * (TILES // 2) + (i + 1))
                        dense(j, j).then_inc(tile_ready, 1)
                for k in range(2):
                    sum_squares(c("ones"), n0 + N_LAT, q0, Q_LAT + k, (Q_LAT + k) % 2, k == 0, k == 1)
                sum_squares(c("ones"), n0 + N_LAT + 1, q0, Q_LAT + 2, (Q_LAT + 2) % 2, True, True)
                e.wait_ge(lo_ready, l0 + (L_LAT + 3 + 2))
                for h in range(HEADS):
                    t, slot = T_Q + h, h // PAIRS
                    if h % PAIRS == 0:
                        weights(B_Q + slot)
                    bank_free(t, t % 2)
                    for k in range(2):
                        mm = three(bank[t % 2][:, :], w_part(slot, k * S + (h % PAIRS) * P, P),
                                   (QN_hi[:, k, :], QN_lo[:, k, :]), k == 0, k == 1)
                    mm.then_inc(tile_ready, 1)
                weights(B_KV)
                for h in range(HEADS):
                    t = T_KN + h
                    bank_free(t, t % 2)
                    three(bank[t % 2][0:64, :], w_part(0, h * NOPE, NOPE), (QN_hi[:, 2, :], QN_lo[:, 2, :]),
                          True, True).then_inc(tile_ready, 1)
                weights(B_KV + 1)
                for k in range(S // P):
                    t = T_V + k
                    bank_free(t, t % 2)
                    wv = w_part(1, 0, S)
                    lat = [q[:, 2, k * P:(k + 1) * P] for q in (QN_hi, QN_lo)]
                    three(bank[t % 2][:, :], lat, wv, True, True).then_inc(tile_ready, 1)

                wait_tile_out(e, it, T_KN + 6)
                wait_tile_out(e, it, T_KN + 7)
                e.wait_ge(krope_ready, it + 1)
                alone(e)
                with e.Fori(0, PAIRS) as hp:
                    for odd in range(2):
                        h = it * HEADS + hp * 2 + odd
                        h4 = h * 4
                        e.wait_ge(head_staged, h * 2 + 2)

                        def scores(j):
                            if j >= 2:
                                e.wait_ge(exp_ready, h4 + (j - 1))
                            e.matmul(bank[2 + j % 2][:, :], RT[0:QK, odd, j * P:(j + 1) * P],
                                     tile_of(KH, hp * 2 + odd, slice(0, QK)), start=True, stop=True)\
                                .then_inc(sc_ready, 1)

                        def turn(j):
                            e.wait_ge(prob_ready, h4 + (j + 1))
                            if j >= 2:
                                e.wait_ge(pt_ready, h4 + (j - 1))
                            for k in range(4):
                                mm = e.transpose(bank[4 + j % 2][:, k * P:(k + 1) * P],
                                                 PEXP[:, j % 2, k * P:(k + 1) * P], c("eye"))
                            mm.then_inc(pt_psum, 1)

                        scores(0)
                        scores(1)
                        for j in range(4):
                            turn(j)
                            if j < 2:
                                scores(j + 2)
                        e.wait_ge(pt_ready, h4 + 4)
                        if not odd:
                            e.wait_ge(ylo_ready, it * PAIRS + hp + 1)
                        for k in range(4):
                            mm = e.matmul(bank[6][64 * odd:64 * odd + 64, :], VS[:, odd, k, :], PT[:, k, :],
                                          start=(k == 0), stop=(k == 3))
                        mm.then_inc(pv_done[odd], 1)

                e.wait_ge(decay_step, it * 3 + 3)
                e.wait_ge(gate_step, it * 5 + 5)
                alone(e)
                for n in range(NCH):
                    for p in range(2):
                        mm = e.matmul(bank[2][64 * p:64 * p + 64, n * 16:n * 16 + 16],
                                      G[0:48, n * CH:(n + 1) * CH], c(f"pick{p}", slice(0, 48)), start=True, stop=True)
                mm.then_inc(gt_psum, 1)
                for t in range(8):
                    sum_squares(c("ones_pair"), n0 + N_L2 + t, q0, Q_L2 + t, (Q_L2 + t) % 2, True, True)

                def stacked(dst, lhs, rhs, accumulate=None):
                    alone(e)
                    for p in range(PAIRS):
                        for r in (slice(0, 64), slice(64, 128)):
                            cols = slice(p * CH, (p + 1) * CH)
                            rr = rhs[r, cols] if rhs.shape[1] > CH else rhs[r, :]
                            mm = e.matmul(dst[r, cols], lhs[r, cols], rr, start=True, stop=accumulate is None)
                            if accumulate is not None:
                                mm = e.matmul(dst[r, cols], accumulate[0][r, cols], accumulate[1][r, cols],
                                              start=False, stop=True)
                    return mm

                with e.Fori(0, NCH) as n:
                    st = e.snap(it * NCH + n)
                    for d in range(2):
                        g, q = gdn[d], gs[d]
                        b_ = B[d]
                        e.wait_ge(q["decay_rhs"], st * 2 + 2)
                        e.matmul(b_[0][:, 0:SW], c(f"after{d}"), g["r1"][:, :], start=True, stop=True)
                        e.matmul(b_[0][:, SW:], c("ones_pair"), g["r1"][:, :], start=True, stop=True)\
                            .then_inc(q["decay_psum"], 1)
                        e.matmul(b_[1][:, 0:SW], c("ones_pair"), g["rb"][:, :], start=True, stop=True)\
                            .then_inc(q["beta_psum"], 1)
                        e.matmul(b_[2][:, 0:4], c(f"after{d}"), g["col"][:, 12:16], start=True, stop=True)
                        e.matmul(b_[2][:, 4:8], c("ones_pair"), g["col"][:, 12:16], start=True, stop=True)\
                            .then_inc(q["cols_psum"], 1)
                    for d in range(2):
                        g, q = gdn[d], gs[d]
                        e.wait_ge(q["cols_exp"], st + 1)
                        stacked(B[d][2][:, 0:SW], g["kc"], g["kc"])
                        stacked(B[d][2][:, SW:], g["kc"], g["qc"]).then_inc(q["kk_psum"], 1)
                    for d in range(2):
                        g, q = gdn[d], gs[d]
                        stacked(B[d][0][:, 0:SW], g["kc"], c("eye_pair"))
                        stacked(B[d][0][:, SW:], g["vc"], c("eye_pair")).then_inc(q["nat_psum"], 1)
                    for d in range(2):
                        g, q = gdn[d], gs[d]
                        e.wait_ge(q["masked"], st * 6 + 1)
                        stacked(B[d][1][:, 0:SW], g["ml"][:, 0, :], c("eye_pair")).then_inc(q["b1_psum"], 1)
                    for l in range(1, LEVELS):
                        for d in range(2):
                            g, q = gdn[d], gs[d]
                            e.wait_ge(q["t_ready"], st * 6 + l)
                            e.wait_ge(q["masked"], st * 6 + (l + 1))
                            if l == 1:
                                e.wait_ge(q["kv"], st + 1)
                            stacked(B[d][0][:, 0:SW], g["ml"][:, l % 2, :], g["ttt"][:, 0, :])\
                                .then_inc(q["y_psum"], 1)
                        for d in range(2):
                            g, q = gdn[d], gs[d]
                            e.wait_ge(q["y_ready"], st * 5 + l)
                            if l < LEVELS - 1:
                                stacked(B[d][2][:, 0:SW], g["ttt"][:, 1, :], g["ys"])
                            stacked(B[d][2][:, SW:], g["ys"], g["ttt"][:, 1, :]).then_inc(q["z_psum"], 1)
                    for d in range(2):
                        g, q = gdn[d], gs[d]
                        e.wait_ge(q["state_new"], st + it + 1)
                        e.wait_ge(q["kbe_qg"], st * 2 + 2)
                        stacked(B[d][0][:, 0:SW], g["kbe"], g["st"]).then_inc(q["ks_psum"], 1)
                    for d in range(2):
                        g, q = gdn[d], gs[d]
                        e.wait_ge(q["r_ready"], st + 1)
                        e.wait_ge(q["t_ready"], st * 6 + 6)
                        stacked(B[d][1][:, 0:SW], g["ttt"][:, 1, :], g["r"]).then_inc(q["vn_psum"], 1)
                    for d in range(2):
                        g, q = gdn[d], gs[d]
                        e.wait_ge(q["vn_ready"], st + 1)
                        stacked(B[d][2][:, 0:SW], g["kv"][:, 0:SW], g["vn"])
                        stacked(B[d][0][:, 0:SW], g["st"], g["qg"], (g["vn"], g["at"])).then_inc(q["o_psum"], 1)
                for t in range(4):
                    sum_squares(c("ones_pair"), n0 + N_Y + t, q0, Q_Y + t, (Q_Y + t) % 2, True, True)

                e.wait_ge(lo_ready, l0 + (L_Y + 4 + 2))
                e.wait_ge(ylo_ready, it * PAIRS + PAIRS + 1)
                alone(e)
                with e.Fori(0, W_OUT // 2) as i:
                    for j in range(2):
                        weights(i * 2 + (B_OUT + j))
                        e.wait_ge(tile_free[j], it * (TILES // 2) + (i + (T_OUT // 2 + 1)))
                        dense(j, j).then_inc(tile_ready, 1)
                for k in range(KD):
                    sum_squares(c("ones"), n0 + N_FFN, q0, Q_FFN + k, (Q_FFN + k) % 2, k == 0, k == KD - 1)
                e.wait_ge(lo_ready, l0 + (L_FFN + KD + 2))
                alone(e)
                with e.Fori(0, NF) as f:
                    for j in range(2):
                        weights(f * 2 + (B_GU + j))
                        e.wait_ge(tile_free[j], it * (TILES // 2) + (f + (T_GU // 2 + 1)))
                        dense(j, j).then_inc(tile_ready, 1)
                e.wait_ge(lo_ready, l0 + (SPLITS + 2))
                alone(e)
                with e.Fori(0, KD // 2) as i:
                    for j in range(2):
                        e.wait_ge(tile_free[j], it * (TILES // 2) + (i + (T_DOWN // 2 + 1)))
                        k0 = 0
                        for r, nk in enumerate(DOWN_K):
                            weights(i * 6 + (B_DOWN + 3 * j + r))
                            for k in range(nk):
                                mm = three(bank[j][:, :], w_part((3 * j + r) % 2, k * P, P),
                                           (A_hi[:, k0 + k, :], A_lo[:, k0 + k, :]), k0 + k == 0, k0 + k == NF - 1)
                            mm.then_inc(tile_ready if r == 2 else down_part, 1)
                            k0 += nk

            for s in range(NSEQ):
                n0, q0 = DEPTH * NSEQ * SUMS + s, DEPTH * NSEQ * SQUARES + s * KD
                for k in range(KD):
                    sum_squares(c("ones"), n0, q0, k, k % 2, k == 0, k == KD - 1)


def blocks(w, tiles):
    depth, k, n = w.shape
    w = w.reshape(depth, k // P, P, tiles, n // tiles)
    return np.ascontiguousarray(w.transpose(0, 3, 2, 1, 4).reshape(depth * tiles, P, -1))


def kernel(**inputs):
    import concourse.bacc as bacc
    from concourse.bass_utils import run_bass_kernel_spmd

    a = {k: np.asarray(v) for k, v in inputs.items()}
    swap = np.r_[ROPE // 2:ROPE, 0:ROPE // 2]
    w = a["w_in"]
    lat = Q_LORA + KV_LORA
    rope_, rest = w[:, :, lat:lat + ROPE], w[:, :, lat + ROPE:]
    qkvz, ab = rest[:, :, :2048], rest[:, :, 2048:]
    nothing = np.zeros_like(w[:, :, :16])
    w_in = np.concatenate([w[:, :, :lat], ab[:, :, :16], nothing, ab[:, :, 16:], nothing, rope_, rope_[:, :, swap],
                           qkvz], 2)
    wq = a["w_q_up"].reshape(DEPTH, Q_LORA, HEADS, QK)
    wq = np.concatenate([wq, wq[..., NOPE + swap]], 3).reshape(DEPTH, Q_LORA, HEADS * P)
    wkv = a["w_kv_up"].reshape(DEPTH, KV_LORA, HEADS, 2, NOPE)
    wkv = wkv.transpose(0, 3, 1, 2, 4).reshape(DEPTH * 2, KV_LORA, HEADS * NOPE)
    gu = np.stack([a["w_gate"].reshape(DEPTH, D, NF, P), a["w_up"].reshape(DEPTH, D, NF, P)], 3)
    gu = gu.reshape(DEPTH, D, 2 * FF)

    par = np.zeros((DEPTH, P, NPAR), np.float32)
    par[:, :, C_NA:C_NA + 8] = a["norm_attn"].reshape(DEPTH, KD, P).transpose(0, 2, 1)
    par[:, :, C_NF:C_NF + 8] = a["norm_ffn"].reshape(DEPTH, KD, P).transpose(0, 2, 1)
    par[:, :, C_QN:C_QN + 2] = a["q_norm"].reshape(DEPTH, 2, P).transpose(0, 2, 1)
    par[:, :, C_KVN] = a["kv_norm"]
    par[:, :, C_CONV:C_CONV + 36] = a["conv_w"].reshape(DEPTH, 3, 12, P).transpose(0, 3, 2, 1).reshape(DEPTH, P, 36)
    par[:, :16, C_DT] = a["dt_bias"].reshape(DEPTH, 16)
    par[:, :16, C_ALOG] = a["a_log"].reshape(DEPTH, 16)
    par[:, :, C_GN] = np.concatenate([a["gdn_norm"]] * 2, 1)

    arrays = {
        "xT": np.stack([a["x_prompt"][0], a["x_sample"][0]]).reshape(NSEQ, S, KD, P).transpose(0, 2, 3, 1),
        "w_in": blocks(w_in, W_IN), "w_q": blocks(wq, W_Q), "w_kv": wkv, "w_out": blocks(a["w_out"], W_OUT),
        "w_gu": blocks(gu, W_GU), "w_down": blocks(a["w_down"], KD), "par": par,
        "gfin": a["norm_final"].reshape(KD, P).T, "const": constants()[0],
    }
    arrays = {k: np.ascontiguousarray(v) for k, v in arrays.items()}
    nc = bacc.Bacc("TRN2", target_bir_lowering=False, num_devices=1)
    args = [nc.dram_tensor(k, v.shape, mybir.dt.from_np(v.dtype), kind="ExternalInput").ap() for k, v in arrays.items()]
    args.append(nc.dram_tensor("out", (NSEQ, KD, P, S), F32, kind="ExternalOutput").ap())
    build(nc, *args)
    got = run_bass_kernel_spmd(nc, [arrays], core_ids=[0]).results[0]["out"]
    y = got.reshape(NSEQ, D, S).transpose(0, 2, 1)
    return y[0:1], y[1:2]
```

```python
from contextlib import ExitStack

import numpy as np
import concourse.bass as bass
from concourse import mybir

F32 = mybir.dt.float32
F32R = mybir.dt.float32r
ALU = mybir.AluOpType
ACT = mybir.ActivationFunctionType
AX_X = mybir.AxisListType.X

P = 128
D = 1024
KD = D // P
S = 512
NSEQ = 2
DEPTH = 2
HEADS = 8
NOPE, ROPE, DV = 64, 32, 64
QK = NOPE + ROPE
Q_LORA, KV_LORA = 256, 128
FF = 2816
NF = FF // P
EPS = 1e-6
ATT_SCALE = float(QK) ** -0.5
CH = 64
NCH = S // CH
PAIRS = HEADS // 2
SW = PAIRS * CH
BD = PAIRS * P
LEVELS = 6
DOWN_K = (8, 7, 7)

W_IN, W_Q, W_KV, W_OUT, W_GU, W_DOWN = 20, 2, 2, KD, 2 * NF, 3 * KD
B_Q = W_IN
B_KV = B_Q + W_Q
B_OUT = B_KV + W_KV
B_GU = B_OUT + W_OUT
B_DOWN = B_GU + W_GU
BLOCKS = B_DOWN + W_DOWN
BW = KD * P

T_Q = W_IN
T_KN = T_Q + HEADS
T_V = T_KN + HEADS
T_OUT = T_V + S // P
T_GU = T_OUT + KD
T_DOWN = T_GU + 2 * NF
TILES = T_DOWN + KD

L_LAT, L_Y, L_FFN, L_A = KD, KD + 3, KD + 7, 2 * KD + 7
SPLITS = L_A + NF
TMPS = L_A

N_FFN, SUMS = 1, 2
Q_FFN, SQUARES = KD, 2 * KD

PT_QLAT, PT_KVLAT, PT_MISC, PT_Q, PT_K, PT_V, PT_Z = 0, 2, 3, 4, 8, 12, 16
LAT_SQ_AT, LAT_SUM_AT = 6, 10
ROW_B = 32

C_NA, C_NF, C_QN, C_KVN, C_CONV, C_DT, C_ALOG, C_GN = 0, 8, 16, 18, 19, 55, 56, 57
NPAR = 58


def constants():
    t = np.arange(CH)
    cols, at = [], {}

    def add(name, m):
        full = np.zeros((P, m.shape[1]), np.float32)
        full[:m.shape[0]] = m
        at[name] = (sum(c.shape[1] for c in cols), m.shape[1])
        cols.append(full)

    def two(m):
        return np.kron(np.eye(2), m)

    le, ge = t[:, None] <= t[None, :], t[:, None] >= t[None, :]
    gt, lt = t[:, None] > t[None, :], t[:, None] < t[None, :]
    add("ones", np.ones((P, P)))
    add("ones_pair", two(np.ones((CH, CH))))
    add("eye", np.eye(P))
    add("after0", two(gt))
    add("after1", two(lt))
    add("upto0", np.tile(le, (2, 1)))
    add("upto1", np.tile(ge, (2, 1)))
    add("eye_pair", np.tile(np.eye(CH), (2, 1)))
    for d in range(2):
        for l in range(LEVELS):
            s = 1 << l
            j, i = t[:, None], t[None, :]
            if d:
                j, i = i, j
            m = (i // (2 * s) == j // (2 * s)) & (i % (2 * s) >= s) & (j % (2 * s) < s)
            add(f"join{d}{l}", two(m))
    for p in range(2):
        m = np.zeros((48, 16))
        for d in range(2):
            for q in range(PAIRS):
                m[d * HEADS + 2 * q + p, d * PAIRS + q] = 1
                m[ROW_B + d * HEADS + 2 * q + p, 8 + d * PAIRS + q] = 1
        add(f"pick{p}", m)
    pos = np.arange(S, dtype=np.float32)
    inv = np.float32(10000.0) ** (-np.arange(0, ROPE, 2, dtype=np.float32) / np.float32(ROPE))
    ang = pos[:, None] * inv[None, :].astype(np.float32)
    cos, sin = np.cos(ang).T, np.sin(ang).T
    rope = np.zeros((P, S))
    rope[64:96] = np.concatenate([cos, cos])
    rope[96:128] = np.concatenate([-sin, sin])
    add("rope", rope)
    add("eps", np.full((P, 1), EPS))
    return np.concatenate(cols, 1).astype(np.float32), at


def build(nc, xT, w_in, w_q, w_kv, w_out, w_gu, w_down, par, gfin, const, out):
    _, at = constants()
    with ExitStack() as ctx:
        base = 17536
        total = (229344 - base) // 4
        pos = 0

        def take(name, shape, dt=F32):
            nonlocal pos
            n = int(np.prod(shape[1:]))
            assert pos + n <= total, (name, pos + n, total)
            t = nc.alloc_sbuf_tensor_at(name, shape, dt, offset=base + 4 * pos)
            pos += (n + 7) // 8 * 8
            return t

        X = take("X", [P, NSEQ, KD, S])
        h_at = pos
        H_hi = take("H_hi", [P, KD, S], F32R)
        H_lo = take("H_lo", [P, KD, S], F32R)
        Wraw = take("Wraw", [P, 2, BW])
        Whi = take("Whi", [P, 2, BW], F32R)
        Wlo = take("Wlo", [P, 2, BW], F32R)
        C = take("C", [P, const.shape[1]])
        PAR = take("PAR", [P, NPAR])
        GFIN = take("GFIN", [P, KD])
        NEGA = take("NEGA", [P, 1])
        stat = take("stat", [P, 4, 4])
        sq = take("sq", [P, 2, S])
        rstd = take("rstd", [P, S])
        tmp = take("tmp", [P, 2, S])
        region = pos
        PRJ = take("PRJ", [P, W_IN, S])
        O = PRJ[:, 0:4, :]
        work = pos
        QN_hi = take("QN_hi", [P, 3, S], F32R)
        QN_lo = take("QN_lo", [P, 3, S], F32R)
        here = pos
        LAT = take("LAT", [P, 5, S])
        pos = here
        KH = take("KH", [QK, HEADS, S])
        QH = take("QH", [QK, HEADS, S])
        V = take("V", [P, S // P, HEADS * DV])
        VS = take("VS", [P, 2, S // P, DV])
        here, pos = pos, h_at + PAIRS * S
        RT = take("RT", [P, 2, S])
        pos = here
        pos = work
        PEXP = take("PEXP", [P, 2, S])
        PT = take("PT", [P, S // P, S])
        pos = work
        GT = take("GT", [P, NCH, 16])
        G = take("G", [P, S])
        G2 = take("G2", [P, 2, S])
        here = pos
        SQ8 = take("SQ8", [P, 8, S])
        RS8 = take("RS8", [P, 8, S])
        pos = here
        gdn = []
        for d in range(2):
            g = {n: take(f"{n}{d}", [P, SW]) for n in "qg at".split()}
            g["r"] = take(f"r{d}", [P, BD])
            g["dtm"], g["db"] = g["r"][:, 0:SW], g["r"][:, SW:]
            g["ssc"] = take(f"ssc{d}", [P, BD])
            g["wk"], g["mt"] = g["ssc"][:, 0:SW], g["ssc"][:, SW:]
            g["rr"] = take(f"rr{d}", [P, 2 * SW])
            g["dte"] = take(f"dte{d}", [P, 2 * SW])
            g["kq"] = take(f"kq{d}", [P, PAIRS, 2, CH])
            for n in ("T", "TT", "kg", "bv"):
                g[n] = take(f"{n}{d}", [P, BD])
            g["ml"] = take(f"ml{d}", [P, 2, BD])
            g["col"] = take(f"col{d}", [P, 16])
            here, pos = pos, h_at + (d * KD + PAIRS) * S
            for n in ("kc", "vc", "kbe", "st"):
                g[n] = take(f"{n}{d}", [P, BD])
            pos = here
            g["vn"] = g["kbe"]
            g["ys"] = g["vc"]
            gdn.append(g)
        pos = region
        A_hi = take("A_hi", [P, NF, S], F32R)
        A_lo = take("A_lo", [P, NF, S], F32R)
        SG = take("SG", [P, 2, S])

        def c(name, rows=slice(0, P)):
            a, n = at[name]
            return C[rows, a:a + n]

        def pairs(ap):
            return ap.rearrange("p (q t) -> p q t", q=PAIRS)

        def halves(ap):
            return ap.rearrange("p (q h t) -> p q h t", q=PAIRS, h=2)

        def twice(ap):
            return pairs(ap).unsqueeze(2).to_broadcast([P, PAIRS, 2, CH])

        def spread(ap, n, w=CH):
            return ap.unsqueeze(2).to_broadcast([P, n, w])

        def each(ap, n=PAIRS, w=CH):
            return ap.unsqueeze(1).to_broadcast([P, n, w])

        def tile_of(t, i, rows=slice(0, P)):
            return t[rows, bass.ds(i, 1), :].rearrange("p o t -> p (o t)")

        def x_tile(s, k):
            return X[:, bass.ds(s, 1), k, :].rearrange("p o t -> p (o t)")

        bank = [ctx.enter_context(nc.psum_tensor(f"bank{i}", [P, S], F32)) for i in range(8)]
        ss_bank = bank[7]

        def sem(name):
            return ctx.enter_context(nc.semaphore(name))

        const_loaded, x_loaded, par_loaded = sem("const_loaded"), sem("x_loaded"), sem("par_loaded")
        out_written = [sem("out_written0"), sem("out_written1")]
        w_loaded = [sem("w_loaded0"), sem("w_loaded1")]
        w_hi, w_lo, down_part = sem("w_hi_ready"), sem("w_lo_ready"), sem("down_part_used")
        sq_ready, sq_used, ln_ready, rstd_ready = (
            sem("sq_ready"), sem("sq_used"), sem("ln_ready"), sem("rstd_ready"))
        tmp_ready, hi_ready, lo_ready = sem("tmp_ready"), sem("hi_ready"), sem("lo_ready")
        tile_ready = sem("tile_ready")
        tile_free = [sem("tile_free0"), sem("tile_free1")]
        conv_step, silu_ready = sem("conv_step"), sem("silu_ready")
        krope_parts, krope_ready = sem("krope_parts"), sem("krope_ready")
        qrope_parts, qrope_ready = sem("qrope_parts"), sem("qrope_ready")
        head_staged = sem("head_staged")
        sc_ready, max_ready, bias_ready, exp_ready, rsum_ready, prob_ready = (
            sem("scores_ready"), sem("max_ready"), sem("bias_ready"), sem("exp_ready"), sem("rsum_ready"),
            sem("prob_ready"))
        pt_psum, pt_ready, yhi_ready, ylo_ready = (
            sem("pt_psum_ready"), sem("pt_ready"), sem("yhi_ready"),
            sem("ylo_ready"))
        pv_done = [sem("pv_done_even"), sem("pv_done_odd")]
        g_zero, gate_step, decay_step = sem("g_zero"), sem("gate_step"), sem("decay_step")
        gt_psum, gt_ready, l2_ready, o_zero = sem("gt_psum_ready"), sem("gt_ready"), sem("l2_ready"), sem("o_zero")
        lat_sq, lat_sum, lat_ln, lat_rstd = sem("lat_sq_ready"), sem("lat_sum_ready"), sem("lat_ln"), sem("lat_rstd_ready")
        head_sq, head_sum, head_ln, head_rstd = (
            sem("head_sq_ready"), sem("head_sum_ready"), sem("head_ln"), sem("head_rstd_ready"))
        gated_step, fin_ready = sem("gated_step"), sem("fin_ready")
        idle = {str(x.engine): sem(f"idle_{i}") for i, x in enumerate((nc.tensor, nc.vector, nc.scalar, nc.gpsimd))}
        per_dir = ("staged kv_staged decay_rhs decay_psum beta_psum decay_exp cols_exp dtm db kbe_qg kk_psum "
                   "mt_at nat_psum kv masked b1_psum y_psum y_ready z_psum zt_psum t_ready tt_ready ks_psum r_ready vn_psum "
                   "vn_ready su_psum o_psum scaled state_new o_added").split()
        gs = [{n: sem(f"{n}{d}") for n in per_dir} for d in range(2)]
        B = [bank[0:3] + bank[6:7], bank[3:6] + bank[7:8]]


        def wait_x(e, it, half):
            for b in range(2):
                e.wait_ge(tile_free[b], it * (TILES // 2) + (half * (T_GU // 2) + 1))

        def wait_tile_out(e, it, t):
            e.wait_ge(tile_free[t % 2], it * (TILES // 2) + (t // 2 + 2))

        def alone(e):
            e.sem_inc(idle[str(e.engine)], 1)

        block = ctx.enter_context(nc.Block())

        @block.sync
        def _(e):
            for s_, n in ((lo_ready, 2), (w_lo, 2), (sq_used, 2), (tile_free[0], 1), (tile_free[1], 1),
                          (ln_ready, 1), (ylo_ready, 1), (pv_done[0], 1), (pv_done[1], 1), (gs[0]["o_added"], 1), (gs[1]["o_added"], 1)):
                e.sem_inc(s_, n)
            e.dma_start(C[:, :], const).then_inc(const_loaded, 16)
            e.dma_start(GFIN[:, :], gfin).then_inc(const_loaded, 16)
            for s in range(NSEQ):
                e.dma_start(X[:, s, :, :], xT[s].rearrange("k p t -> p k t")).then_inc(x_loaded, 16)
            with e.Fori(0, DEPTH) as L, e.Fori(0, NSEQ) as s:
                it = L * NSEQ + s
                wait_x(e, it, 0)
                e.dma_start(PAR[:, :], par[bass.ds(L, 1), :, :].rearrange("o p n -> p (o n)")).then_inc(par_loaded, 16)

                def load(b, slot, src, width):
                    e.wait_ge(w_lo, it * BLOCKS + (b + 1))
                    e.dma_start(Wraw[:, slot, 0:width], src).then_inc(w_loaded[slot], 16)

                def loads(b0, n, w, width):
                    with e.Fori(0, n // 2) as half:
                        i = half * 2
                        for j in range(2):
                            load(i + (b0 + j), j, w[bass.ds(L * n + i + j, 1), :, :].rearrange("o p n -> p (o n)"),
                                 width)

                loads(0, W_IN, w_in, BW)
                loads(B_Q, W_Q, w_q, BW)
                loads(B_KV, W_KV, w_kv, S)
                loads(B_OUT, W_OUT, w_out, BW)
                loads(B_GU, W_GU, w_gu, BW)
                with e.Fori(0, KD // 2) as half:
                    j = half * 2
                    for jj in range(2):
                        at_k = 0
                        for r, nk in enumerate(DOWN_K):
                            src = w_down[bass.ds(L * KD + j + jj, 1), :, at_k * P:(at_k + nk) * P]
                            load(j * 3 + (B_DOWN + 3 * jj + r), (3 * jj + r) % 2,
                                 src.rearrange("o p n -> p (o n)"), nk * P)
                            at_k += nk
            for s in range(NSEQ):
                for k in range(KD):
                    e.wait_ge(fin_ready, s * KD + k + 1)
                    e.dma_start(out[s, k], tmp[:, k % 2, :]).then_inc(out_written[k % 2], 16)
            for slot in range(2):
                e.wait_ge(out_written[slot], 16 * NSEQ * KD // 2)

        @block.scalar
        def _(e):
            e.wait_ge(const_loaded, 32)
            e.wait_ge(x_loaded, 16 * NSEQ)

            def square(inp, q0, k):
                e.wait_ge(sq_used, q0 + (k + 1 + (k == 0)))
                alone(e)
                e.activation(sq[:, k % 2, :], inp, ACT.Square).then_inc(sq_ready, 1)

            def root(n0, n, q0, k, width):
                e.wait_ge(sq_used, q0 + (k + 2))
                e.activation(rstd[:, :], ss_bank[:, :], ACT.Ln, scale=1.0 / width, bias=c("eps"))\
                    .then_inc(ln_ready, 1)
                e.wait_ge(ln_ready, n0 + (n + 2))
                e.activation(rstd[:, :], rstd[:, :], ACT.Exp, scale=-0.5).then_inc(rstd_ready, 1)

            with e.Fori(0, DEPTH) as L, e.Fori(0, NSEQ) as s:
                it = e.snap(L * NSEQ + s)
                n0, q0, l0, m0 = it * SUMS, it * SQUARES, it * SPLITS, it * TMPS
                b0, t0 = it * BLOCKS, it * TILES

                def split_w(b, slot, width, used):
                    e.wait_ge(w_loaded[slot], b0 * 8 + ((b - slot) * 8 + 16))
                    if used is not None:
                        e.wait_ge(used[0], used[1])
                    e.activation(Whi[:, slot, 0:width], Wraw[:, slot, 0:width], ACT.Copy).then_inc(w_hi, 1)

                def after_tile(t):
                    return tile_ready, t0 + (t + 1)

                def split_tmp(l, dst):
                    e.wait_ge(tmp_ready, m0 + (l + 1))
                    e.activation(dst, tmp[:, l % 2, :], ACT.Copy).then_inc(hi_ready, 1)

                wait_x(e, it, 0)
                for b in range(2):
                    split_w(b, b, BW, None)
                for k in range(KD):
                    square(x_tile(s, k), q0, k)
                root(n0, 0, q0, KD, D)
                for k in range(KD):
                    split_tmp(k, H_hi[:, k, :])

                for t in range(W_IN):
                    b = t + 2
                    split_w(b, b % 2, BW, after_tile(t))
                    if PT_Q <= t < PT_Z:
                        wait_tile_out(e, it, t)
                        e.activation(PRJ[:, t, :], PRJ[:, t, :], ACT.Silu).then_inc(silu_ready, 1)
                    elif t >= PT_Z:
                        e.activation(PRJ[:, t, :], bank[t % 2][:, :], ACT.Silu).then_inc(tile_free[t % 2], 1)
                    if t == LAT_SQ_AT:
                        for k in range(3):
                            wait_tile_out(e, it, PT_QLAT + k)
                        for k in range(3):
                            e.activation(LAT[:, k, :], PRJ[:, PT_QLAT + k, :], ACT.Square).then_inc(lat_sq, 1)
                    elif t == LAT_SUM_AT + 1:
                        for i, width in enumerate((Q_LORA, KV_LORA)):
                            e.wait_ge(lat_sum, it * 2 + (i + 1))
                            e.activation(LAT[:, 3 + i, :], bank[6 + i][:, :], ACT.Ln, scale=1.0 / width, bias=c("eps"))\
                                .then_inc(lat_ln, 1)
                        e.wait_ge(lat_ln, it * 2 + 2)
                        e.activation(LAT[:, 3:5, :], LAT[:, 3:5, :], ACT.Exp, scale=-0.5).then_inc(lat_rstd, 1)
                    elif t == W_IN - 3:
                        for k in range(2):
                            split_tmp(L_LAT + k, QN_hi[:, k, :])
                    elif t == W_IN - 2:
                        split_tmp(L_LAT + 2, QN_hi[:, 2, :])

                e.wait_ge(krope_parts, it * 3 + 3)
                e.activation(KH[64:96, :, :], RT[64:96, 0:1, :].to_broadcast([ROPE, HEADS, S]), ACT.Copy)\
                    .then_inc(krope_ready, 1)
                split_w(B_KV, 0, S, after_tile(T_Q + 3))
                split_w(B_KV + 1, 1, S, after_tile(T_Q + 7))
                split_w(B_OUT, 0, BW, after_tile(T_KN + 7))
                for t in range(T_V, T_V + S // P):
                    e.wait_ge(tile_ready, t0 + (t + 1))
                    e.activation(V[:, t - T_V, :], bank[t % 2][:, :], ACT.Copy).then_inc(tile_free[t % 2], 1)
                split_w(B_OUT + 1, 1, BW, after_tile(T_V + 3))

                with e.Fori(0, PAIRS) as hp:
                    for odd in range(2):
                        h4 = (it * HEADS + hp * 2 + odd) * 4

                        def evict(j):
                            e.wait_ge(pt_psum, h4 + (j + 1))
                            e.activation(PT[:, :, j * P:(j + 1) * P],
                                         bank[4 + j % 2][:, :].rearrange("p (k q) -> p k q", k=4), ACT.Copy)\
                                .then_inc(pt_ready, 1)

                        for j in range(4):
                            e.wait_ge(bias_ready, h4 + (j + 1))
                            if j >= 2:
                                e.wait_ge(pt_psum, h4 + (j - 1))
                            e.activation(PEXP[:, j % 2, :], bank[2 + j % 2][:, :], ACT.Exp, bias=stat[:, j, 1:2],
                                         scale=ATT_SCALE, accum_out=stat[:, j, 2:3]).then_inc(exp_ready, 1)
                            if j:
                                evict(j - 1)
                        evict(3)
                    e.wait_ge(pv_done[1], it * PAIRS + hp + 2)
                    alone(e)
                    e.activation(tile_of(H_hi, hp), bank[6][:, :], ACT.Copy).then_inc(yhi_ready, 1)

                e.wait_ge(par_loaded, it * 16 + 16)
                e.wait_ge(g_zero, it + 1)
                e.activation(G2[0:16, 0, :], PRJ[0:16, PT_MISC, :], ACT.Abs, bias=PAR[0:16, C_DT:C_DT + 1])\
                    .then_inc(gate_step, 1)
                e.wait_ge(gate_step, it * 5 + 1)
                e.activation(G2[0:16, 0, :], G2[0:16, 0, :], ACT.Exp, scale=-1.0).then_inc(gate_step, 1)
                e.activation(NEGA[0:16, :], PAR[0:16, C_ALOG:C_ALOG + 1], ACT.Exp).then_inc(gate_step, 1)
                e.activation(G[32:48, :], PRJ[32:48, PT_MISC, :], ACT.Sigmoid).then_inc(gate_step, 1)
                e.wait_ge(gate_step, it * 5 + 4)
                e.activation(G2[0:16, 0, :], G2[0:16, 0, :], ACT.Ln, bias=c("ones")[0:16, 0:1])\
                    .then_inc(gate_step, 1)

                def head_norms(done, n, b0, width):
                    for t in range(n):
                        e.wait_ge(head_sum, it * 12 + (done + t + 1))
                        e.activation(RS8[:, t, :], bank[b0 + t][:, :], ACT.Ln, scale=1.0 / width, bias=c("eps"))\
                            .then_inc(head_ln, 1)
                    for t in range(0, n, 2):
                        e.wait_ge(head_ln, it * 12 + (done + t + 2))
                        e.activation(RS8[:, t:t + 2, :], RS8[:, t:t + 2, :], ACT.Exp, scale=-0.5)\
                            .then_inc(head_rstd, 1)

                head_norms(0, 8, 0, 1)
                e.wait_ge(gt_psum, it + 1)
                e.activation(GT[:, :, :].rearrange("p n g -> p (n g)"), bank[2][:, 0:NCH * 16], ACT.Copy)\
                    .then_inc(gt_ready, 1)
                e.wait_ge(gt_ready, it + 1)
                e.wait_ge(l2_ready, it * 8 + 8)

                def chunk_of(d, n):
                    return (NCH - 1) - n if d else n

                def stage_cols(d, n):
                    for to, fr in ((4, 8), (12, 0)):
                        e.activation(gdn[d]["col"][:, to:to + 4],
                                     GT[:, bass.ds(chunk_of(d, n), 1), fr + d * 4:fr + d * 4 + 4]
                                     .rearrange("p o g -> p (o g)"), ACT.Copy).then_inc(gs[d]["staged"], 1)

                def stage_kq(d, n):
                    for i, t in enumerate((PT_K, PT_Q)):
                        e.activation(gdn[d]["kq"][:, :, i, :], PRJ[:, t:t + PAIRS, bass.ds(chunk_of(d, n) * CH, CH)],
                                     ACT.Copy)

                def stage_diagonal(d, n, nm, t):
                    for h in range(2):
                        rows = slice(h * CH, h * CH + CH)
                        cp = e.activation(halves(gdn[d][nm][:, :])[rows, :, h, :],
                                          PRJ[rows, t:t + PAIRS, bass.ds(chunk_of(d, n) * CH, CH)], ACT.Copy)
                    cp.then_inc(gs[d]["kv_staged"], 1)

                def decays(st):
                    for d in range(2):
                        g, q = gdn[d], gs[d]
                        e.wait_ge(q["decay_psum"], st + 1)
                        e.activation(g["dte"][:, :], B[d][3][:, :], ACT.Exp).then_inc(q["decay_exp"], 1)
                        e.wait_ge(q["beta_psum"], st + 1)
                        e.activation(g["col"][:, 0:4], B[d][1][:, SW:SW + 4], ACT.Exp)
                        e.activation(g["col"][:, 8:12], B[d][1][:, SW + 4:SW + 8], ACT.Exp).then_inc(q["cols_exp"], 1)

                def step(n, last):
                    st = e.snap(it * NCH + n)
                    for l in range(1, LEVELS):
                        for d in range(2):
                            g, q = gdn[d], gs[d]
                            e.wait_ge(q["y_psum"], st * 5 + l)
                            e.activation(g["ys"][:, :], B[d][0][:, :], ACT.Copy).then_inc(q["y_ready"], 1)
                        for d in range(0 if last else 2):
                            g, q = gdn[d], gs[d]
                            if l == 1:
                                e.wait_ge(q["kbe_qg"], st * 2 + 2)
                                alone(e)
                                stage_kq(d, n + 1)
                            elif l == 2:
                                stage_diagonal(d, n + 1, "kc", PT_K)
                            elif l == 4:
                                e.wait_ge(q["scaled"], st + 1)
                                alone(e)
                                stage_cols(d, n + 1)
                            elif l == 5:
                                e.wait_ge(q["zt_psum"], st * 5 + 5)
                                alone(e)
                                stage_diagonal(d, n + 1, "vc", PT_V)
                    for d in range(2):
                        g, q = gdn[d], gs[d]
                        e.wait_ge(q["vn_psum"], st + 1)
                        e.activation(g["vn"][:, :], B[d][1][:, :], ACT.Copy).then_inc(q["vn_ready"], 1)
                    if not last:
                        decays(st + 1)

                for d in range(2):
                    g, q = gdn[d], gs[d]
                    e.wait_ge(q["o_added"], it * NCH + 1)
                    e.wait_ge(q["state_new"], it * (NCH + 1) + 1)
                    alone(e)
                    stage_cols(d, 0)
                for d in range(2):
                    stage_kq(d, 0)
                    stage_diagonal(d, 0, "kc", PT_K)
                    stage_diagonal(d, 0, "vc", PT_V)
                decays(it * NCH)
                with e.Fori(0, NCH - 1) as n:
                    step(n, False)
                step(NCH - 1, True)

                head_norms(8, 4, 2, DV)
                for t in range(4):
                    split_tmp(L_Y + t, H_hi[:, 4 + t, :])

                with e.Fori(0, W_OUT // 2) as half:
                    i = half * 2
                    for j in range(2):
                        split_w(i + (B_OUT + 2 + j), j, BW, after_tile(i + (T_OUT + j)))
                wait_x(e, it, 1)
                for k in range(KD):
                    square(x_tile(s, k), q0, Q_FFN + k)
                root(n0, N_FFN, q0, Q_FFN + KD, D)
                for k in range(KD):
                    split_tmp(L_FFN + k, H_hi[:, k, :])

                def gate_up(f, last):
                    for j in range(2):
                        fj = f + j
                        for m in range(2):
                            if last and j:
                                split_w(B_DOWN + m, m, DOWN_K[m] * P, after_tile(T_DOWN - 2 + m))
                            else:
                                split_w(fj * 2 + (B_GU + 2 + m), m, BW, after_tile(fj * 2 + (T_GU + m)))
                            if m == 0:
                                e.activation(SG[:, j, :], bank[0][:, :], ACT.Silu).then_inc(tile_free[0], 1)
                        e.wait_ge(tile_free[1], it * (TILES // 2) + (fj + (T_GU // 2 + 2)))
                        alone(e)
                        e.activation(tile_of(A_hi, fj) if not last else A_hi[:, fj, :],
                                     tmp[:, (L_A + j) % 2, :], ACT.Copy).then_inc(hi_ready, 1)

                with e.Fori(0, NF // 2 - 1) as half:
                    f = half * 2
                    gate_up(f, False)
                gate_up(NF - 2, True)

                def down_w(j, r):
                    b = j * 3 + (B_DOWN + r)
                    if r == 0:
                        used = down_part, it * (2 * KD) + j * 2
                    elif r == 1:
                        used = tile_ready, t0 + (j + T_DOWN)
                    else:
                        used = down_part, it * (2 * KD) + (j * 2 + 1)
                    return b, used

                def down_split(j, jj, r):
                    b, used = down_w(j + jj, r)
                    split_w(b, (3 * jj + r) % 2, DOWN_K[r] * P, used)

                down_split(0, 0, 2)
                for r in range(3):
                    down_split(0, 1, r)
                with e.Fori(1, KD // 2) as half:
                    j = half * 2
                    for jj in range(2):
                        for r in range(3):
                            down_split(j, jj, r)

            wait_x(e, DEPTH * NSEQ, 0)
            for s in range(NSEQ):
                q0 = DEPTH * NSEQ * SQUARES + s * KD
                for k in range(KD):
                    square(X[:, s, k, :], q0, k)
                if s:
                    e.wait_ge(fin_ready, KD)
                root(DEPTH * NSEQ * SUMS, s, q0, KD, D)

        @block.gpsimd
        def _(e):
            e.wait_ge(const_loaded, 32)
            with e.Fori(0, DEPTH) as L, e.Fori(0, NSEQ) as s:
                it = e.snap(L * NSEQ + s)
                l0, b0, t0 = it * SPLITS, it * BLOCKS, it * TILES

                def low_w(b, slot, width):
                    e.wait_ge(w_hi, b0 + (b + 1))
                    e.tensor_tensor(Wlo[:, slot, 0:width], Wraw[:, slot, 0:width],
                                    Whi[:, slot, 0:width].bitcast(F32), ALU.subtract).then_inc(w_lo, 1)

                def low_tmp(l, parity, dst, hi):
                    e.wait_ge(hi_ready, l0 + (l + 1))
                    e.tensor_tensor(dst, tmp[:, parity, :], hi.bitcast(F32), ALU.subtract).then_inc(lo_ready, 1)

                for b in range(2):
                    low_w(b, b, BW)
                for k in range(KD):
                    low_tmp(k, k % 2, H_lo[:, k, :], H_hi[:, k, :])
                with e.Fori(0, W_IN // 2 - 1) as half:
                    i = half * 2
                    for j in range(2):
                        low_w(i + (2 + j), j, BW)
                for k in range(3):
                    low_tmp(L_LAT + k, (L_LAT + k) % 2, QN_lo[:, k, :], QN_hi[:, k, :])
                for j in range(2):
                    low_w(W_IN + j, j, BW)
                for b in range(2):
                    low_w(B_KV + b, b, S)
                for b in range(2):
                    low_w(B_OUT + b, b, BW)
                wait_tile_out(e, it, T_V + 2)
                wait_tile_out(e, it, T_V + 3)
                e.wait_ge(qrope_ready, it * HEADS + HEADS)
                alone(e)
                with e.Fori(0, PAIRS) as hp:
                    for odd in range(2):
                        e.wait_ge(pv_done[odd], it * PAIRS + hp + 1)
                        alone(e)
                        e.tensor_copy(RT[0:QK, odd, :], tile_of(QH, hp * 2 + odd, slice(0, QK))).then_inc(head_staged, 1)
                        e.tensor_copy(VS[:, odd, :, :], V[:, :, bass.ds((hp * 2 + odd) * DV, DV)])\
                            .then_inc(head_staged, 1)
                e.wait_ge(ylo_ready, it * PAIRS + PAIRS + 1)
                alone(e)
                e.memset(G[0:48, :], 0.0).then_inc(g_zero, 1)
                e.wait_ge(gate_step, it * 5 + 5)
                e.wait_ge(decay_step, it * 3 + 3)
                alone(e)
                e.memset(O, 0.0).then_inc(o_zero, 1)
                for d in range(2):
                    for n in ("kc", "vc", "st"):
                        ms = e.memset(gdn[d][n][:, :], 0.0)
                    ms.then_inc(gs[d]["state_new"], 1)
                def decay_rhs(st):
                    for d in range(2):
                        g, q = gdn[d], gs[d]
                        e.wait_ge(q["staged"], st * 2 + 2)
                        e.tensor_tensor(pairs(g["rr"][:, 0:SW]), spread(g["col"][:, 12:16], PAIRS),
                                        each(c(f"upto{d}")), ALU.mult).then_inc(q["decay_rhs"], 1)
                        e.tensor_tensor(pairs(g["rr"][:, SW:]), spread(g["col"][:, 4:8], PAIRS),
                                        each(c("eye_pair")), ALU.mult).then_inc(q["decay_rhs"], 1)

                def step(n, last):
                    st = e.snap(it * NCH + n)
                    for l in range(LEVELS):
                        for d in range(2):
                            g, q = gdn[d], gs[d]
                            if l == 0:
                                e.wait_ge(q["mt_at"], st * 2 + 1)
                            elif l == 2:
                                e.wait_ge(q["tt_ready"], st * 6 + 1)
                            elif l > 2:
                                e.wait_ge(q["y_psum"], st * 5 + (l - 2))
                            join = c(f"join{d}{l}").rearrange("p (h t) -> p h t", h=2).unsqueeze(1)
                            e.tensor_tensor(halves(g["ml"][:, l % 2, :]), twice(g["mt"]),
                                            join.to_broadcast([P, PAIRS, 2, CH]), ALU.mult).then_inc(q["masked"], 1)
                    for d in range(2):
                        g, q = gdn[d], gs[d]
                        e.wait_ge(q["cols_exp"], st + 1)
                        e.wait_ge(q["state_new"], st + it + 1)
                        e.wait_ge(q["kbe_qg"], st * 2 + 2)
                        e.wait_ge(q["masked"], st * 6 + 6)
                        e.tensor_tensor(pairs(g["ssc"][:, :]), pairs(g["st"][:, :]),
                                        spread(g["col"][:, 8:12], PAIRS, P), ALU.mult).then_inc(q["scaled"], 1)
                    if not last:
                        decay_rhs(st + 1)

                decay_rhs(it * NCH)
                with e.Fori(0, NCH - 1) as n:
                    step(n, False)
                step(NCH - 1, True)
                for t in range(4):
                    low_tmp(L_Y + t, (L_Y + t) % 2, H_lo[:, 4 + t, :], H_hi[:, 4 + t, :])
                with e.Fori(0, W_OUT // 2) as half:
                    i = half * 2
                    for j in range(2):
                        low_w(i + (B_OUT + 2 + j), j, BW)
                for k in range(KD):
                    low_tmp(L_FFN + k, (L_FFN + k) % 2, H_lo[:, k, :], H_hi[:, k, :])

                def gate_up(f, last):
                    for j in range(2):
                        for m in range(2):
                            if last and j:
                                low_w(B_DOWN + m, m, DOWN_K[m] * P)
                            else:
                                low_w((f + j) * 2 + (B_GU + 2 + m), m, BW)
                        a = (lambda t: t[:, f + j, :]) if last else (lambda t: tile_of(t, f + j))
                        low_tmp(f + (L_A + j), (L_A + j) % 2, a(A_lo), a(A_hi))

                with e.Fori(0, NF // 2 - 1) as half:
                    f = half * 2
                    gate_up(f, False)
                gate_up(NF - 2, True)

                low_w(B_DOWN + 2, 0, DOWN_K[2] * P)
                for r in range(3):
                    low_w(B_DOWN + 3 + r, (3 + r) % 2, DOWN_K[r] * P)
                with e.Fori(1, KD // 2) as half:
                    j = half * 2
                    for jj in range(2):
                        for r in range(3):
                            low_w(j * 3 + (B_DOWN + 3 * jj + r), (3 * jj + r) % 2, DOWN_K[r] * P)

        @block.vector
        def _(e):
            e.wait_ge(const_loaded, 32)
            e.wait_ge(x_loaded, 16 * NSEQ)
            with e.Fori(0, DEPTH) as L, e.Fori(0, NSEQ) as s:
                it = e.snap(L * NSEQ + s)
                n0, l0, t0 = it * SUMS, it * SPLITS, it * TILES

                def tmp_free(l):
                    e.wait_ge(lo_ready, l0 + (l + 1 + (isinstance(l, int) and l == 0)))

                def normalise(inp, gain, n, l, scale=None):
                    if scale is None:
                        scale = rstd[:, :]
                        e.wait_ge(rstd_ready, n0 + (n + 1))
                    tmp_free(l)
                    e.scalar_tensor_tensor(tmp[:, l % 2, :], inp, gain, scale, ALU.mult, ALU.mult)\
                        .then_inc(tmp_ready, 1)

                wait_x(e, it, 0)
                e.wait_ge(par_loaded, it * 16 + 16)
                for k in range(KD):
                    normalise(x_tile(s, k), PAR[:, C_NA + k:C_NA + k + 1], 0, k)

                for t in range(PT_Z):
                    e.wait_ge(tile_ready, t0 + (t + 1))
                    pb, free = bank[t % 2], tile_free[t % 2]
                    if t < PT_Q:
                        e.tensor_copy(PRJ[:, t, :], pb[:, :]).then_inc(free, 1)
                        continue
                    w = [PAR[:, C_CONV + 3 * (t - PT_Q) + i:C_CONV + 3 * (t - PT_Q) + i + 1] for i in range(3)]
                    y = PRJ[:, t, :]
                    e.tensor_scalar(y, pb[:, :], w[1], None, ALU.mult).then_inc(conv_step, 1)
                    e.wait_ge(conv_step, it * 24 + (2 * (t - PT_Q) + 1))
                    e.scalar_tensor_tensor(y[:, 1:S], pb[:, 0:S - 1], w[0], y[:, 1:S], ALU.mult, ALU.add)\
                        .then_inc(conv_step, 1)
                    e.wait_ge(conv_step, it * 24 + (2 * (t - PT_Q) + 2))
                    e.scalar_tensor_tensor(y[:, 0:S - 1], pb[:, 1:S], w[2], y[:, 0:S - 1], ALU.mult, ALU.add)\
                        .then_inc(free, 1)

                e.wait_ge(lat_rstd, it + 1)
                for k in range(2):
                    normalise(PRJ[:, PT_QLAT + k, :], PAR[:, C_QN + k:C_QN + k + 1], None, L_LAT + k, LAT[:, 3, :])
                normalise(PRJ[:, PT_KVLAT, :], PAR[:, C_KVN:C_KVN + 1], None, L_LAT + 2, LAT[:, 4, :])

                e.wait_ge(tile_ready, t0 + W_IN)
                alone(e)
                r0, r1 = RT[64:96, 0, :], RT[64:96, 1, :]
                e.tensor_tensor(r0, PRJ[64:96, PT_MISC, :], c("rope", slice(64, 96)), ALU.mult).then_inc(krope_parts, 1)
                e.tensor_tensor(r1, PRJ[96:128, PT_MISC, :], c("rope", slice(96, 128)), ALU.mult)\
                    .then_inc(krope_parts, 1)
                e.wait_ge(krope_parts, it * 3 + 2)
                e.tensor_tensor(r0, r0, r1, ALU.add).then_inc(krope_parts, 1)
                e.wait_ge(krope_ready, it + 1)
                for h in range(HEADS):
                    t = T_Q + h
                    pb = bank[t % 2]
                    e.wait_ge(tile_ready, t0 + (t + 1))
                    if h:
                        e.wait_ge(qrope_ready, it * HEADS + h)
                    e.tensor_tensor(r0, pb[64:96, :], c("rope", slice(64, 96)), ALU.mult).then_inc(qrope_parts, 1)
                    e.tensor_tensor(r1, pb[96:128, :], c("rope", slice(96, 128)), ALU.mult).then_inc(qrope_parts, 1)
                    e.tensor_copy(QH[0:64, h, :], pb[0:64, :]).then_inc(tile_free[t % 2], 1)
                    e.wait_ge(qrope_parts, it * 16 + (2 * h + 2))
                    e.tensor_tensor(QH[64:96, h, :], r0, r1, ALU.add).then_inc(qrope_ready, 1)
                for h in range(HEADS):
                    t = T_KN + h
                    e.wait_ge(tile_ready, t0 + (t + 1))
                    e.tensor_copy(KH[0:64, h, :], bank[t % 2][0:64, :]).then_inc(tile_free[t % 2], 1)

                with e.Fori(0, PAIRS) as hp:
                    for odd in range(2):
                        h4 = (it * HEADS + hp * 2 + odd) * 4

                        def maximum(j):
                            e.wait_ge(sc_ready, h4 + (j + 1))
                            e.tensor_reduce(stat[:, j, 0:1], bank[2 + j % 2][:, :], AX_X, ALU.max)\
                                .then_inc(max_ready, 1)
                            e.wait_ge(max_ready, h4 + (j + 1))
                            e.tensor_scalar(stat[:, j, 1:2], stat[:, j, 0:1], -ATT_SCALE, None, ALU.mult)\
                                .then_inc(bias_ready, 1)

                        maximum(0)
                        for j in range(4):
                            if j < 3:
                                maximum(j + 1)
                            e.wait_ge(exp_ready, h4 + (j + 1))
                            e.reciprocal(stat[:, j, 3:4], stat[:, j, 2:3]).then_inc(rsum_ready, 1)
                            e.wait_ge(rsum_ready, h4 + (j + 1))
                            e.tensor_scalar(PEXP[:, j % 2, :], PEXP[:, j % 2, :], stat[:, j, 3:4], None, ALU.mult)\
                                .then_inc(prob_ready, 1)
                    e.wait_ge(yhi_ready, it * PAIRS + hp + 1)
                    e.tensor_tensor(tile_of(H_lo, hp), bank[6][:, :], tile_of(H_hi, hp).bitcast(F32), ALU.subtract)\
                        .then_inc(ylo_ready, 1)

                e.wait_ge(silu_ready, it * 12 + 12)
                e.wait_ge(ylo_ready, it * PAIRS + PAIRS + 1)
                alone(e)
                for t in range(8):
                    y = PRJ[:, PT_Q + t, :]
                    e.tensor_tensor(SQ8[:, t, :], y, y, ALU.mult).then_inc(head_sq, 1)
                e.wait_ge(g_zero, it + 1)
                e.tensor_scalar(G2[0:16, 1, :], PRJ[0:16, PT_MISC, :], PAR[0:16, C_DT:C_DT + 1], 0.0, ALU.add, ALU.max)\
                    .then_inc(decay_step, 1)
                e.wait_ge(gate_step, it * 5 + 5)
                e.wait_ge(decay_step, it * 3 + 1)
                e.tensor_tensor(G2[0:16, 1, :], G2[0:16, 1, :], G2[0:16, 0, :], ALU.add).then_inc(decay_step, 1)
                e.wait_ge(decay_step, it * 3 + 2)
                e.tensor_scalar(G[0:16, :], G2[0:16, 1, :], NEGA[0:16, 0:1], -1.0, ALU.mult, ALU.mult)\
                    .then_inc(decay_step, 1)
                for t in range(8):
                    y = PRJ[:, PT_Q + t, :]
                    e.wait_ge(head_rstd, it * 6 + (t // 2 + 1))
                    e.scalar_tensor_tensor(y, y, CH ** -0.5 if t < PAIRS else 1.0, RS8[:, t, :], ALU.mult, ALU.mult)\
                        .then_inc(l2_ready, 1)

                def decays(st):
                    for d in range(2):
                        g, q = gdn[d], gs[d]
                        e.wait_ge(q["decay_exp"], st + 1)
                        e.tensor_tensor(pairs(g["dtm"]), pairs(g["dte"][:, 0:SW]), each(c(f"upto{d}")), ALU.mult)\
                            .then_inc(q["dtm"], 1)
                    for d in range(2):
                        g, q = gdn[d], gs[d]
                        e.wait_ge(q["cols_exp"], st + 1)
                        e.wait_ge(q["dtm"], st + 1)
                        e.tensor_tensor(g["db"], g["dtm"], B[d][1][:, 0:SW], ALU.mult).then_inc(q["db"], 1)

                def step(n, last):
                    st = e.snap(it * NCH + n)
                    chunk = [n, (NCH - 1) - n]
                    for d in range(2):
                        g, q = gdn[d], gs[d]
                        e.wait_ge(q["state_new"], st + it + 1)
                        e.tensor_tensor(g["wk"], g["dte"][:, SW:], B[d][1][:, 0:SW], ALU.mult).then_inc(q["db"], 1)
                    for d in range(2):
                        g, q = gdn[d], gs[d]
                        e.wait_ge(q["db"], st * 2 + 2)
                        e.wait_ge(q["kk_psum"], st + 1)
                        kk = halves(B[d][3][:, :])
                        e.tensor_tensor(pairs(g["mt"]), kk[:, :, 0, :], pairs(g["db"]), ALU.mult)\
                            .then_inc(q["mt_at"], 1)
                        e.tensor_tensor(pairs(g["at"][:, :]), kk[:, :, 1, :], pairs(g["dtm"]), ALU.mult)\
                            .then_inc(q["mt_at"], 1)
                    for d in range(2):
                        g, q = gdn[d], gs[d]
                        e.tensor_tensor(halves(g["kbe"][:, :]), halves(g["kc"][:, :]), twice(g["wk"]), ALU.mult)\
                            .then_inc(q["kbe_qg"], 1)
                        e.tensor_tensor(pairs(g["qg"][:, :]), g["kq"][:, :, 1, :], pairs(g["dte"][:, SW:]), ALU.mult)\
                            .then_inc(q["kbe_qg"], 1)
                    for d in range(2):
                        g, q = gdn[d], gs[d]
                        e.wait_ge(q["nat_psum"], st + 1)
                        e.wait_ge(q["cols_exp"], st + 1)
                        for i, (nm, b) in enumerate((("kg", 0), ("bv", 1))):
                            e.tensor_tensor(pairs(g[nm][:, :]), pairs(B[d][b][:, :]),
                                            spread(g["col"][:, 4 * i:4 * i + 4], PAIRS, P), ALU.mult)\
                                .then_inc(q["kv"], 1)
                    for d in range(2):
                        g, q = gdn[d], gs[d]
                        e.wait_ge(q["b1_psum"], st + 1)
                        eye = each(c("eye"), PAIRS, P)
                        e.tensor_tensor(pairs(g["T"][:, :]), eye, pairs(B[d][2][:, :]), ALU.subtract)\
                            .then_inc(q["t_ready"], 1)
                        e.tensor_tensor(pairs(g["TT"][:, :]), eye, pairs(g["ml"][:, 0, :]), ALU.subtract)\
                            .then_inc(q["tt_ready"], 1)
                    for l in range(1, LEVELS):
                        for d in range(2):
                            g, q = gdn[d], gs[d]
                            if l < LEVELS - 1:
                                e.wait_ge(q["z_psum"], st * 4 + l)
                                e.wait_ge(q["t_ready"], st * 5 + l)
                                e.tensor_tensor(g["T"][:, :], g["T"][:, :], B[d][1][:, :], ALU.subtract)\
                                    .then_inc(q["t_ready"], 1)
                            e.wait_ge(q["zt_psum"], st * 5 + l)
                            e.wait_ge(q["tt_ready"], st * 6 + l)
                            e.tensor_tensor(g["TT"][:, :], g["TT"][:, :], B[d][2][:, :], ALU.subtract)\
                                .then_inc(q["tt_ready"], 1)
                    for d in range(2):
                        g, q = gdn[d], gs[d]
                        e.wait_ge(q["ks_psum"], st + 1)
                        e.wait_ge(q["kv"], st * 2 + 2)
                        e.tensor_tensor(g["r"][:, :], g["bv"][:, :], B[d][0][:, :], ALU.subtract)\
                            .then_inc(q["r_ready"], 1)
                    if not last:
                        decays(st + 1)
                    for d in range(2):
                        g, q = gdn[d], gs[d]
                        e.wait_ge(q["o_psum"], st + 1)
                        e.wait_ge(q["scaled"], st + 1)
                        e.tensor_tensor(g["st"][:, :], g["ssc"][:, :], B[d][2][:, :], ALU.add)\
                            .then_inc(q["state_new"], 1)
                        e.wait_ge(gs[1 - d]["o_added"], st + (1 + d))
                        alone(e)
                        oc = O[:, :, bass.ds(chunk[d] * CH, CH)]
                        e.tensor_tensor(oc, oc, pairs(B[d][0][:, 0:SW]), ALU.add).then_inc(q["o_added"], 1)

                decays(it * NCH)
                e.wait_ge(o_zero, it + 1)
                alone(e)
                with e.Fori(0, NCH - 1) as n:
                    step(n, False)
                step(NCH - 1, True)

                for d in range(2):
                    e.wait_ge(gs[d]["o_added"], it * NCH + NCH + 1)
                alone(e)
                for t in range(4):
                    e.tensor_tensor(SQ8[:, t, :], O[:, t, :], O[:, t, :], ALU.mult).then_inc(head_sq, 1)
                for t in range(4):
                    e.wait_ge(head_rstd, it * 6 + (4 + t // 2 + 1))
                    e.scalar_tensor_tensor(O[:, t, :], O[:, t, :], PAR[:, C_GN:C_GN + 1], RS8[:, t, :],
                                           ALU.mult, ALU.mult).then_inc(gated_step, 1)
                    e.wait_ge(gated_step, it * 4 + (t + 1))
                    tmp_free(L_Y + t)
                    if t == 0:
                        wait_tile_out(e, it, W_IN - 2)
                        wait_tile_out(e, it, W_IN - 1)
                    e.tensor_tensor(tmp[:, (L_Y + t) % 2, :], O[:, t, :], PRJ[:, PT_Z + t, :], ALU.mult)\
                        .then_inc(tmp_ready, 1)

                def residual(t, b, k):
                    e.wait_ge(tile_ready, t0 + t + 1)
                    xt = X[:, bass.ds(s, 1), bass.ds(k, 1), :].rearrange("p o k t -> p (o k t)")
                    e.tensor_tensor(xt, xt, bank[b][:, :], ALU.add).then_inc(tile_free[b], 1)

                with e.Fori(0, KD // 2) as half:
                    i = half * 2
                    for j in range(2):
                        residual(i + (T_OUT + j), j, i + j)
                wait_x(e, it, 1)
                for k in range(KD):
                    normalise(x_tile(s, k), PAR[:, C_NF + k:C_NF + k + 1], N_FFN, L_FFN + k)
                with e.Fori(0, NF // 2) as half:
                    f = half * 2
                    for j in range(2):
                        e.wait_ge(tile_ready, t0 + ((f + j) * 2 + (T_GU + 2)))
                        e.wait_ge(tile_free[0], it * (TILES // 2) + (f + j + (T_GU // 2 + 2)))
                        tmp_free(f + (L_A + j))
                        e.tensor_tensor(tmp[:, (L_A + j) % 2, :], SG[:, j, :], bank[1][:, :], ALU.mult)\
                            .then_inc(tile_free[1], 1)
                with e.Fori(0, KD // 2) as half:
                    i = half * 2
                    for j in range(2):
                        residual(i + (T_DOWN + j), j, i + j)

            wait_x(e, DEPTH * NSEQ, 0)
            for s in range(NSEQ):
                for k in range(KD):
                    n = s * KD + k
                    e.wait_ge(rstd_ready, DEPTH * NSEQ * SUMS + s + 1)
                    if n == 0:
                        e.wait_ge(lo_ready, DEPTH * NSEQ * SPLITS + 2)
                    if n >= 2:
                        e.wait_ge(out_written[k % 2], 16 * (n // 2))
                    e.scalar_tensor_tensor(tmp[:, k % 2, :], X[:, s, k, :], GFIN[:, k:k + 1], rstd[:, :],
                                           ALU.mult, ALU.mult).then_inc(fin_ready, 1)

        @block.tensor
        def _(e):
            e.wait_ge(const_loaded, 32)

            def sum_squares(ones, n_idx, q_idx, k, slot, first, last):
                e.wait_ge(sq_ready, q_idx + (k + 1))
                if first:
                    e.wait_ge(ln_ready, n_idx + 1)
                e.matmul(ss_bank[:, :], ones, sq[:, slot, :], start=first, stop=last).then_inc(sq_used, 1)

            with e.Fori(0, DEPTH) as L, e.Fori(0, NSEQ) as s:
                it = e.snap(L * NSEQ + s)
                n0, q0, l0 = it * SUMS, it * SQUARES, it * SPLITS
                b0, t0 = it * BLOCKS, it * TILES

                def bank_free(t, b):
                    e.wait_ge(tile_free[b], it * (TILES // 2) + ((t - b) // 2 + 1))

                def weights(b):
                    e.wait_ge(w_lo, b0 + (b + 3))

                def three(out_, w, a, first, last):
                    e.matmul(out_, w[0], a[0], start=first, stop=False)
                    e.matmul(out_, w[0], a[1], start=False, stop=False)
                    return e.matmul(out_, w[1], a[0], start=False, stop=last)

                def w_part(slot, a, n):
                    return Whi[:, slot, a:a + n], Wlo[:, slot, a:a + n]

                def dense(slot, b, k0=KD, split=None):
                    for k in range(KD):
                        if k >= k0:
                            e.wait_ge(lo_ready, l0 + (split + k + 3))
                        mm = three(bank[b][:, :], w_part(slot, k * P, P), (H_hi[:, k, :], H_lo[:, k, :]),
                                   k == 0, k == KD - 1)
                    return mm

                for k in range(KD):
                    sum_squares(c("ones"), n0, q0, k, k % 2, k == 0, k == KD - 1)
                def dense_pair(i, b, t, k0=KD, split=None):
                    for j in range(2):
                        weights(i * 2 + (b + j))
                        e.wait_ge(tile_free[j], it * (TILES // 2) + (i + (t // 2 + 1)))
                        dense(j, j, KD if j else k0, split).then_inc(tile_ready, 1)

                dense_pair(0, 0, 0, 0, 0)
                with e.Fori(1, LAT_SUM_AT // 2) as i:
                    dense_pair(i, 0, 0)
                e.wait_ge(lat_sq, it * 3 + 3)
                alone(e)
                for k in range(3):
                    mm = e.matmul(bank[6 + k // 2][:, :], c("ones"), LAT[:, k, :], start=k != 1, stop=k != 0)
                    if k:
                        mm.then_inc(lat_sum, 1)
                with e.Fori(LAT_SUM_AT // 2, W_IN // 2) as i:
                    dense_pair(i, 0, 0)
                e.wait_ge(lo_ready, l0 + (L_LAT + 3 + 2))
                for h in range(HEADS):
                    t, slot = T_Q + h, h // PAIRS
                    if h % PAIRS == 0:
                        weights(B_Q + slot)
                    bank_free(t, t % 2)
                    for k in range(2):
                        mm = three(bank[t % 2][:, :], w_part(slot, k * S + (h % PAIRS) * P, P),
                                   (QN_hi[:, k, :], QN_lo[:, k, :]), k == 0, k == 1)
                    mm.then_inc(tile_ready, 1)
                weights(B_KV)
                for h in range(HEADS):
                    t = T_KN + h
                    bank_free(t, t % 2)
                    three(bank[t % 2][0:64, :], w_part(0, h * NOPE, NOPE), (QN_hi[:, 2, :], QN_lo[:, 2, :]),
                          True, True).then_inc(tile_ready, 1)
                weights(B_KV + 1)
                for k in range(S // P):
                    t = T_V + k
                    bank_free(t, t % 2)
                    wv = w_part(1, 0, S)
                    lat = [q[:, 2, k * P:(k + 1) * P] for q in (QN_hi, QN_lo)]
                    three(bank[t % 2][:, :], lat, wv, True, True).then_inc(tile_ready, 1)

                wait_tile_out(e, it, T_KN + 6)
                wait_tile_out(e, it, T_KN + 7)
                e.wait_ge(krope_ready, it + 1)
                alone(e)
                with e.Fori(0, PAIRS) as hp:
                    for odd in range(2):
                        h = it * HEADS + hp * 2 + odd
                        h4 = h * 4
                        e.wait_ge(head_staged, h * 2 + 2)

                        def scores(j):
                            if j >= 2:
                                e.wait_ge(exp_ready, h4 + (j - 1))
                            e.matmul(bank[2 + j % 2][:, :], RT[0:QK, odd, j * P:(j + 1) * P],
                                     tile_of(KH, hp * 2 + odd, slice(0, QK)), start=True, stop=True)\
                                .then_inc(sc_ready, 1)

                        def turn(j):
                            e.wait_ge(prob_ready, h4 + (j + 1))
                            if j >= 2:
                                e.wait_ge(pt_ready, h4 + (j - 1))
                            for k in range(4):
                                mm = e.transpose(bank[4 + j % 2][:, k * P:(k + 1) * P],
                                                 PEXP[:, j % 2, k * P:(k + 1) * P], c("eye"))
                            mm.then_inc(pt_psum, 1)

                        scores(0)
                        scores(1)
                        for j in range(4):
                            turn(j)
                            if j < 2:
                                scores(j + 2)
                        e.wait_ge(pt_ready, h4 + 4)
                        if not odd:
                            e.wait_ge(ylo_ready, it * PAIRS + hp + 1)
                        for k in range(4):
                            mm = e.matmul(bank[6][64 * odd:64 * odd + 64, :], VS[:, odd, k, :], PT[:, k, :],
                                          start=(k == 0), stop=(k == 3))
                        mm.then_inc(pv_done[odd], 1)

                def head_sums(done, n, b0):
                    for t in range(n):
                        e.wait_ge(head_sq, it * 12 + (done + t + 1))
                        alone(e)
                        e.matmul(bank[b0 + t][:, :], c("ones_pair"), SQ8[:, t, :], start=True, stop=True)\
                            .then_inc(head_sum, 1)

                wait_tile_out(e, it, T_V + 2)
                wait_tile_out(e, it, T_V + 3)
                head_sums(0, 8, 0)
                e.wait_ge(head_ln, it * 12 + 8)
                e.wait_ge(decay_step, it * 3 + 3)
                e.wait_ge(gate_step, it * 5 + 5)
                alone(e)
                for n in range(NCH):
                    for p in range(2):
                        mm = e.matmul(bank[2][64 * p:64 * p + 64, n * 16:n * 16 + 16],
                                      G[0:48, n * CH:(n + 1) * CH], c(f"pick{p}", slice(0, 48)), start=True, stop=True)
                mm.then_inc(gt_psum, 1)

                def heads(dst, lhs, rhs, start=True, stop=True):
                    w = dst.shape[1] // PAIRS
                    for p in range(PAIRS):
                        rr = rhs[:, p * w:(p + 1) * w] if rhs.shape[1] > w else rhs
                        mm = e.matmul(dst[:, p * w:(p + 1) * w], lhs[:, p * P:(p + 1) * P], rr,
                                      start=start, stop=stop)
                    return mm

                def decays(st):
                    for d in range(2):
                        g, q = gdn[d], gs[d]
                        e.wait_ge(q["decay_rhs"], st * 2 + 2)
                        alone(e)
                        e.matmul(B[d][3][:, 0:SW], c(f"after{d}"), g["rr"][:, 0:SW], start=True, stop=True)
                        e.matmul(B[d][3][:, SW:], c("ones_pair"), g["rr"][:, 0:SW], start=True, stop=True)\
                            .then_inc(q["decay_psum"], 1)

                def betas(d):
                    g, q = gdn[d], gs[d]
                    e.matmul(B[d][1][:, SW:SW + 4], c(f"after{d}"), g["col"][:, 12:16], start=True, stop=True)
                    e.matmul(B[d][1][:, SW + 4:SW + 8], c("ones_pair"), g["col"][:, 12:16], start=True, stop=True)
                    e.matmul(B[d][1][:, 0:SW], c("ones_pair"), g["rr"][:, SW:], start=True, stop=True)\
                        .then_inc(q["beta_psum"], 1)

                def step(n, last):
                    st = e.snap(it * NCH + n)
                    for d in range(2):
                        g, q = gdn[d], gs[d]
                        e.wait_ge(q["decay_exp"], st + 1)
                        e.wait_ge(q["kv_staged"], st * 2 + 1)
                        alone(e)
                        heads(B[d][3][:, :], g["kc"], g["kq"][:, :, :, :].rearrange("p q h t -> p (q h t)"))\
                            .then_inc(q["kk_psum"], 1)
                    for d in range(2):
                        g, q = gdn[d], gs[d]
                        e.wait_ge(q["o_added"], st + 1)
                        e.wait_ge(q["cols_exp"], st + 1)
                        e.wait_ge(q["db"], st * 2 + 2)
                        e.wait_ge(q["kv_staged"], st * 2 + 2)
                        alone(e)
                        heads(B[d][0][:, :], g["kc"], c("eye"))
                        heads(B[d][1][:, :], g["vc"], c("eye")).then_inc(q["nat_psum"], 1)
                    for d in range(2):
                        g, q = gdn[d], gs[d]
                        e.wait_ge(q["masked"], st * 6 + 1)
                        alone(e)
                        heads(B[d][2][:, :], g["ml"][:, 0, :], c("eye")).then_inc(q["b1_psum"], 1)
                    for l in range(1, LEVELS):
                        for d in range(2):
                            g, q = gdn[d], gs[d]
                            e.wait_ge(q["t_ready"], st * 5 + l)
                            e.wait_ge(q["masked"], st * 6 + (l + 1))
                            if l == 1:
                                e.wait_ge(q["kv"], st * 2 + 2)
                            alone(e)
                            heads(B[d][0][:, :], g["ml"][:, l % 2, :], g["T"]).then_inc(q["y_psum"], 1)
                        for d in range(2):
                            g, q = gdn[d], gs[d]
                            e.wait_ge(q["y_ready"], st * 5 + l)
                            e.wait_ge(q["tt_ready"], st * 6 + l)
                            alone(e)
                            if l < LEVELS - 1:
                                heads(B[d][1][:, :], g["TT"], g["ys"]).then_inc(q["z_psum"], 1)
                            heads(B[d][2][:, :], g["ys"], g["TT"]).then_inc(q["zt_psum"], 1)
                    for d in range(2):
                        g, q = gdn[d], gs[d]
                        e.wait_ge(q["state_new"], st + it + 1)
                        e.wait_ge(q["kbe_qg"], st * 2 + 2)
                        alone(e)
                        heads(B[d][0][:, :], g["kbe"], g["st"]).then_inc(q["ks_psum"], 1)
                    for d in range(2):
                        g, q = gdn[d], gs[d]
                        e.wait_ge(q["r_ready"], st + 1)
                        e.wait_ge(q["tt_ready"], st * 6 + 6)
                        alone(e)
                        heads(B[d][1][:, :], g["TT"], g["r"]).then_inc(q["vn_psum"], 1)
                    if not last:
                        for d in range(2):
                            e.wait_ge(gs[d]["mt_at"], st * 2 + 2)
                        decays(st + 1)
                    for d in range(2):
                        g, q = gdn[d], gs[d]
                        e.wait_ge(q["vn_ready"], st + 1)
                        alone(e)
                        if not last:
                            betas(d)
                        heads(B[d][2][:, :], g["kg"], g["vn"])
                        for p in range(PAIRS):
                            w = slice(p * P, (p + 1) * P)
                            t = slice(p * CH, (p + 1) * CH)
                            e.matmul(B[d][0][:, t], g["st"][:, w], g["qg"][:, t], start=True, stop=False)
                            mm = e.matmul(B[d][0][:, t], g["vn"][:, w], g["at"][:, t], start=False, stop=True)
                        mm.then_inc(q["o_psum"], 1)

                decays(it * NCH)
                for d in range(2):
                    betas(d)
                with e.Fori(0, NCH - 1) as n:
                    step(n, False)
                step(NCH - 1, True)
                head_sums(8, 4, 2)

                e.wait_ge(ylo_ready, it * PAIRS + PAIRS + 1)
                dense_pair(0, B_OUT, T_OUT, 4, L_Y - 4)
                with e.Fori(1, W_OUT // 2) as i:
                    dense_pair(i, B_OUT, T_OUT)
                for k in range(KD):
                    sum_squares(c("ones"), n0 + N_FFN, q0, Q_FFN + k, (Q_FFN + k) % 2, k == 0, k == KD - 1)
                dense_pair(0, B_GU, T_GU, 0, L_FFN)
                with e.Fori(1, NF) as f:
                    dense_pair(f, B_GU, T_GU)
                e.wait_ge(lo_ready, l0 + (SPLITS + 2))
                alone(e)
                with e.Fori(0, KD // 2) as i:
                    for j in range(2):
                        e.wait_ge(tile_free[j], it * (TILES // 2) + (i + (T_DOWN // 2 + 1)))
                        k0 = 0
                        for r, nk in enumerate(DOWN_K):
                            weights(i * 6 + (B_DOWN + 3 * j + r))
                            for k in range(nk):
                                mm = three(bank[j][:, :], w_part((3 * j + r) % 2, k * P, P),
                                           (A_hi[:, k0 + k, :], A_lo[:, k0 + k, :]), k0 + k == 0, k0 + k == NF - 1)
                            mm.then_inc(tile_ready if r == 2 else down_part, 1)
                            k0 += nk

            for s in range(NSEQ):
                n0, q0 = DEPTH * NSEQ * SUMS + s, DEPTH * NSEQ * SQUARES + s * KD
                for k in range(KD):
                    sum_squares(c("ones"), n0, q0, k, k % 2, k == 0, k == KD - 1)


def blocks(w, tiles):
    depth, k, n = w.shape
    w = w.reshape(depth, k // P, P, tiles, n // tiles)
    return np.ascontiguousarray(w.transpose(0, 3, 2, 1, 4).reshape(depth * tiles, P, -1))


def kernel(**inputs):
    import concourse.bacc as bacc
    from concourse.bass_utils import run_bass_kernel_spmd

    a = {k: np.asarray(v) for k, v in inputs.items()}
    swap = np.r_[ROPE // 2:ROPE, 0:ROPE // 2]
    w = a["w_in"]
    lat = Q_LORA + KV_LORA
    rope_, rest = w[:, :, lat:lat + ROPE], w[:, :, lat + ROPE:]
    qkvz, ab = rest[:, :, :2048], rest[:, :, 2048:]
    nothing = np.zeros_like(w[:, :, :16])
    w_in = np.concatenate([w[:, :, :lat], ab[:, :, :16], nothing, ab[:, :, 16:], nothing, rope_, rope_[:, :, swap],
                           qkvz], 2)
    wq = a["w_q_up"].reshape(DEPTH, Q_LORA, HEADS, QK)
    wq = np.concatenate([wq, wq[..., NOPE + swap]], 3).reshape(DEPTH, Q_LORA, HEADS * P)
    wkv = a["w_kv_up"].reshape(DEPTH, KV_LORA, HEADS, 2, NOPE)
    wkv = wkv.transpose(0, 3, 1, 2, 4).reshape(DEPTH * 2, KV_LORA, HEADS * NOPE)
    gu = np.stack([a["w_gate"].reshape(DEPTH, D, NF, P), a["w_up"].reshape(DEPTH, D, NF, P)], 3)
    gu = gu.reshape(DEPTH, D, 2 * FF)

    par = np.zeros((DEPTH, P, NPAR), np.float32)
    par[:, :, C_NA:C_NA + 8] = a["norm_attn"].reshape(DEPTH, KD, P).transpose(0, 2, 1)
    par[:, :, C_NF:C_NF + 8] = a["norm_ffn"].reshape(DEPTH, KD, P).transpose(0, 2, 1)
    par[:, :, C_QN:C_QN + 2] = a["q_norm"].reshape(DEPTH, 2, P).transpose(0, 2, 1)
    par[:, :, C_KVN] = a["kv_norm"]
    par[:, :, C_CONV:C_CONV + 36] = a["conv_w"].reshape(DEPTH, 3, 12, P).transpose(0, 3, 2, 1).reshape(DEPTH, P, 36)
    par[:, :16, C_DT] = a["dt_bias"].reshape(DEPTH, 16)
    par[:, :16, C_ALOG] = a["a_log"].reshape(DEPTH, 16)
    par[:, :, C_GN] = np.concatenate([a["gdn_norm"]] * 2, 1)

    arrays = {
        "xT": np.stack([a["x_prompt"][0], a["x_sample"][0]]).reshape(NSEQ, S, KD, P).transpose(0, 2, 3, 1),
        "w_in": blocks(w_in, W_IN), "w_q": blocks(wq, W_Q), "w_kv": wkv, "w_out": blocks(a["w_out"], W_OUT),
        "w_gu": blocks(gu, W_GU), "w_down": blocks(a["w_down"], KD), "par": par,
        "gfin": a["norm_final"].reshape(KD, P).T, "const": constants()[0],
    }
    arrays = {k: np.ascontiguousarray(v) for k, v in arrays.items()}
    nc = bacc.Bacc("TRN2", target_bir_lowering=False, num_devices=1)
    args = [nc.dram_tensor(k, v.shape, mybir.dt.from_np(v.dtype), kind="ExternalInput").ap() for k, v in arrays.items()]
    args.append(nc.dram_tensor("out", (NSEQ, KD, P, S), F32, kind="ExternalOutput").ap())
    build(nc, *args)
    got = run_bass_kernel_spmd(nc, [arrays], core_ids=[0]).results[0]["out"]
    y = got.reshape(NSEQ, D, S).transpose(0, 2, 1)
    return y[0:1], y[1:2]
```

```python
from contextlib import ExitStack

import numpy as np
import concourse.bass as bass
from concourse import mybir

F32 = mybir.dt.float32
F32R = mybir.dt.float32r
ALU = mybir.AluOpType
ACT = mybir.ActivationFunctionType
AX_X = mybir.AxisListType.X

P = 128
D = 1024
KD = D // P
S = 512
NSEQ = 2
DEPTH = 2
HEADS = 8
NOPE, ROPE, DV = 64, 32, 64
QK = NOPE + ROPE
Q_LORA, KV_LORA = 256, 128
FF = 2816
NF = FF // P
EPS = 1e-6
ATT_SCALE = float(QK) ** -0.5
CH = 64
NCH = S // CH
PAIRS = HEADS // 2
SW = PAIRS * CH
BD = PAIRS * P
LEVELS = 6
DOWN_K = (8, 7, 7)

W_IN, W_Q, W_KV, W_OUT, W_GU, W_DOWN = 20, 2, 2, KD, 2 * NF, 3 * KD
B_Q = W_IN
B_KV = B_Q + W_Q
B_OUT = B_KV + W_KV
B_GU = B_OUT + W_OUT
B_DOWN = B_GU + W_GU
BLOCKS = B_DOWN + W_DOWN
BW = KD * P

T_Q = W_IN
T_KN = T_Q + HEADS
T_V = T_KN + HEADS
T_OUT = T_V + S // P
T_GU = T_OUT + KD
T_DOWN = T_GU + 2 * NF
TILES = T_DOWN + KD

L_LAT, L_Y, L_FFN, L_A = KD, KD + 3, KD + 7, 2 * KD + 7
SPLITS = L_A + NF
TMPS = L_A

N_FFN, SUMS = 1, 2
Q_FFN, SQUARES = KD, 2 * KD

PT_QLAT, PT_KVLAT, PT_MISC, PT_Q, PT_K, PT_V, PT_Z = 0, 2, 3, 4, 8, 12, 16
LAT_SQ_AT, LAT_SUM_AT = 6, 10
ROW_B = 32

C_NF, C_QN, C_KVN, C_CONV, C_DT, C_ALOG, C_GN = 0, 8, 10, 11, 47, 48, 49
NPAR = 50


def constants():
    t = np.arange(CH)
    cols, at = [], {}

    def add(name, m):
        full = np.zeros((P, m.shape[1]), np.float32)
        full[:m.shape[0]] = m
        at[name] = (sum(c.shape[1] for c in cols), m.shape[1])
        cols.append(full)

    def two(m):
        return np.kron(np.eye(2), m)

    le, ge = t[:, None] <= t[None, :], t[:, None] >= t[None, :]
    gt, lt = t[:, None] > t[None, :], t[:, None] < t[None, :]
    add("ones", np.ones((P, P)))
    add("ones_pair", two(np.ones((CH, CH))))
    add("eye", np.eye(P))
    add("after0", two(gt))
    add("after1", two(lt))
    add("upto0", np.tile(le, (2, 1)))
    add("upto1", np.tile(ge, (2, 1)))
    add("eye_pair", np.tile(np.eye(CH), (2, 1)))
    for d in range(2):
        for l in range(LEVELS):
            s = 1 << l
            j, i = t[:, None], t[None, :]
            if d:
                j, i = i, j
            m = (i // (2 * s) == j // (2 * s)) & (i % (2 * s) >= s) & (j % (2 * s) < s)
            add(f"join{d}{l}", two(m))
    for p in range(2):
        m = np.zeros((48, 16))
        for d in range(2):
            for q in range(PAIRS):
                m[d * HEADS + 2 * q + p, d * PAIRS + q] = 1
                m[ROW_B + d * HEADS + 2 * q + p, 8 + d * PAIRS + q] = 1
        add(f"pick{p}", m)
    pos = np.arange(S, dtype=np.float32)
    inv = np.float32(10000.0) ** (-np.arange(0, ROPE, 2, dtype=np.float32) / np.float32(ROPE))
    ang = pos[:, None] * inv[None, :].astype(np.float32)
    cos, sin = np.cos(ang).T, np.sin(ang).T
    rope = np.zeros((P, S))
    rope[64:96] = np.concatenate([cos, cos])
    rope[96:128] = np.concatenate([-sin, sin])
    add("rope", rope)
    add("eps", np.full((P, 1), EPS))
    return np.concatenate(cols, 1).astype(np.float32), at


def build(nc, xT, w_in, w_q, w_kv, w_out, w_gu, w_down, par, gains, const, out):
    _, at = constants()
    with ExitStack() as ctx:
        base = 17536
        total = (229344 - base) // 4
        pos = 0

        def take(name, shape, dt=F32):
            nonlocal pos
            n = int(np.prod(shape[1:]))
            assert pos + n <= total, (name, pos + n, total)
            t = nc.alloc_sbuf_tensor_at(name, shape, dt, offset=base + 4 * pos)
            pos += (n + 7) // 8 * 8
            return t

        X = take("X", [P, NSEQ, KD, S])
        h_at = pos
        H_hi = take("H_hi", [P, KD, S], F32R)
        H_lo = take("H_lo", [P, KD, S], F32R)
        Wraw = take("Wraw", [P, 2, BW])
        Whi = take("Whi", [P, 2, BW], F32R)
        Wlo = take("Wlo", [P, 2, BW], F32R)
        C = take("C", [P, const.shape[1]])
        PAR = take("PAR", [P, NPAR])
        GAIN = take("GAIN", [P, DEPTH + 1, KD])
        NEGA = take("NEGA", [P, 1])
        stat = take("stat", [P, 4, 4])
        sq = take("sq", [P, 2, S])
        rstd = take("rstd", [P, S])
        tmp = take("tmp", [P, 2, S])
        region = pos
        PRJ = take("PRJ", [P, W_IN, S])
        O = PRJ[:, 0:4, :]
        work = pos
        QN_hi = take("QN_hi", [P, 3, S], F32R)
        QN_lo = take("QN_lo", [P, 3, S], F32R)
        here = pos
        LAT = take("LAT", [P, 5, S])
        pos = here
        KH = take("KH", [QK, HEADS, S])
        QH = take("QH", [QK, HEADS, S])
        V = take("V", [P, S // P, HEADS * DV])
        VS = take("VS", [P, 2, S // P, DV])
        here, pos = pos, h_at + PAIRS * S
        RT = take("RT", [P, 2, S])
        pos = here
        pos = work
        PEXP = take("PEXP", [P, 2, S])
        PT = take("PT", [P, S // P, S])
        pos = work
        GT = take("GT", [P, NCH, 16])
        G = take("G", [P, S])
        G2 = take("G2", [P, 2, S])
        here = pos
        SQ8 = take("SQ8", [P, 8, S])
        RS8 = take("RS8", [P, 8, S])
        pos = here
        gdn = []
        for d in range(2):
            g = {n: take(f"{n}{d}", [P, SW]) for n in "qg at".split()}
            g["r"] = take(f"r{d}", [P, BD])
            g["dtm"], g["db"] = g["r"][:, 0:SW], g["r"][:, SW:]
            g["ssc"] = take(f"ssc{d}", [P, BD])
            g["wk"], g["mt"] = g["ssc"][:, 0:SW], g["ssc"][:, SW:]
            g["rr"] = take(f"rr{d}", [P, 2 * SW])
            g["dte"] = take(f"dte{d}", [P, 2 * SW])
            g["kq"] = take(f"kq{d}", [P, PAIRS, 2, CH])
            for n in ("T", "TT", "kg", "bv"):
                g[n] = take(f"{n}{d}", [P, BD])
            g["ml"] = take(f"ml{d}", [P, 2, BD])
            g["col"] = take(f"col{d}", [P, 16])
            here, pos = pos, h_at + (d * KD + PAIRS) * S
            for n in ("kc", "vc", "kbe", "st"):
                g[n] = take(f"{n}{d}", [P, BD])
            pos = here
            g["vn"] = g["kbe"]
            g["ys"] = g["vc"]
            gdn.append(g)
        pos = region
        A_hi = take("A_hi", [P, NF, S], F32R)
        A_lo = take("A_lo", [P, NF, S], F32R)
        SG = take("SG", [P, 2, S])

        def c(name, rows=slice(0, P)):
            a, n = at[name]
            return C[rows, a:a + n]

        def pairs(ap):
            return ap.rearrange("p (q t) -> p q t", q=PAIRS)

        def halves(ap):
            return ap.rearrange("p (q h t) -> p q h t", q=PAIRS, h=2)

        def twice(ap):
            return pairs(ap).unsqueeze(2).to_broadcast([P, PAIRS, 2, CH])

        def spread(ap, n, w=CH):
            return ap.unsqueeze(2).to_broadcast([P, n, w])

        def each(ap, n=PAIRS, w=CH):
            return ap.unsqueeze(1).to_broadcast([P, n, w])

        def tile_of(t, i, rows=slice(0, P)):
            return t[rows, bass.ds(i, 1), :].rearrange("p o t -> p (o t)")

        def x_tile(s, k):
            return X[:, bass.ds(s, 1), k, :].rearrange("p o t -> p (o t)")

        bank = [ctx.enter_context(nc.psum_tensor(f"bank{i}", [P, S], F32)) for i in range(8)]
        ss_bank = bank[7]

        def sem(name):
            return ctx.enter_context(nc.semaphore(name))

        const_loaded, par_loaded = sem("const_loaded"), sem("par_loaded")
        x_loaded = [sem("x_loaded0"), sem("x_loaded1")]
        out_written = [sem("out_written0"), sem("out_written1")]
        w_loaded = [sem("w_loaded0"), sem("w_loaded1")]
        w_hi, w_lo, down_part = sem("w_hi_ready"), sem("w_lo_ready"), sem("down_part_used")
        sq_ready, sq_used, ln_ready, rstd_ready = (
            sem("sq_ready"), sem("sq_used"), sem("ln_ready"), sem("rstd_ready"))
        tmp_ready, hi_ready, lo_ready = sem("tmp_ready"), sem("hi_ready"), sem("lo_ready")
        tile_ready = sem("tile_ready")
        tile_free = [sem("tile_free0"), sem("tile_free1")]
        conv_step, silu_ready = sem("conv_step"), sem("silu_ready")
        krope_parts, krope_ready = sem("krope_parts"), sem("krope_ready")
        qrope_parts, qrope_ready, qnope_ready = sem("qrope_parts"), sem("qrope_ready"), sem("qnope_ready")
        head_staged = sem("head_staged")
        sc_ready, max_ready, bias_ready, exp_ready, rsum_ready, prob_ready = (
            sem("scores_ready"), sem("max_ready"), sem("bias_ready"), sem("exp_ready"), sem("rsum_ready"),
            sem("prob_ready"))
        pt_psum, pt_ready, yhi_ready, ylo_ready = (
            sem("pt_psum_ready"), sem("pt_ready"), sem("yhi_ready"),
            sem("ylo_ready"))
        pv_done = [sem("pv_done_even"), sem("pv_done_odd")]
        g_zero, gate_step, decay_step = sem("g_zero"), sem("gate_step"), sem("decay_step")
        gt_psum, gt_ready, l2_ready, o_zero = sem("gt_psum_ready"), sem("gt_ready"), sem("l2_ready"), sem("o_zero")
        lat_sq, lat_sum, lat_ln, lat_rstd = sem("lat_sq_ready"), sem("lat_sum_ready"), sem("lat_ln"), sem("lat_rstd_ready")
        head_sq, head_sum, head_ln, head_rstd = (
            sem("head_sq_ready"), sem("head_sum_ready"), sem("head_ln"), sem("head_rstd_ready"))
        gated_step, fin_ready = sem("gated_step"), sem("fin_ready")
        idle = {str(x.engine): sem(f"idle_{i}") for i, x in enumerate((nc.tensor, nc.vector, nc.scalar, nc.gpsimd))}
        per_dir = ("staged kv_staged decay_rhs decay_psum beta_psum decay_exp cols_exp dtm db kbe_qg kk_psum "
                   "mt_at nat_psum kg_ready bv_ready masked b1_psum y_psum y_ready z_psum zt_psum t_ready "
                   "tt_ready ks_psum r_ready vn_psum vn_ready o_psum scaled state_new o_added").split()
        gs = [{n: sem(f"{n}{d}") for n in per_dir} for d in range(2)]
        B = [bank[0:3] + bank[6:7], bank[3:6] + bank[7:8]]


        def wait_x(e, it, half):
            for b in range(2):
                e.wait_ge(tile_free[b], it * (TILES // 2) + (half * (T_GU // 2) + 1))

        def wait_tile_out(e, it, t):
            e.wait_ge(tile_free[t % 2], it * (TILES // 2) + (t // 2 + 2))

        def alone(e):
            e.sem_inc(idle[str(e.engine)], 1)

        block = ctx.enter_context(nc.Block())

        @block.sync
        def _(e):
            for s_, n in ((lo_ready, 2), (w_lo, 2), (sq_used, 2), (tile_free[0], 1), (tile_free[1], 1),
                          (ln_ready, 1), (ylo_ready, 1), (pv_done[0], 1), (pv_done[1], 1), (down_part, 1), (gs[0]["o_added"], 1), (gs[1]["o_added"], 1)):
                e.sem_inc(s_, n)
            e.dma_start(C[:, :], const).then_inc(const_loaded, 16)
            e.dma_start(GAIN[:, :, :], gains).then_inc(const_loaded, 16)
            e.dma_start(X[:, 0, :, :], xT[0].rearrange("k p t -> p k t")).then_inc(x_loaded[0], 16)
            with e.Fori(0, DEPTH) as L, e.Fori(0, NSEQ) as s:
                it = L * NSEQ + s

                def load(b, slot, src, width):
                    e.wait_ge(w_lo, it * BLOCKS + (b + 1))
                    e.dma_start(Wraw[:, slot, 0:width], src).then_inc(w_loaded[slot], 16)

                def load_pair(i, b0, n, w, width):
                    for j in range(2):
                        load(i + (b0 + j), j, w[bass.ds(L * n + i + j, 1), :, :].rearrange("o p n -> p (o n)"), width)

                def loads(b0, n, w, width, first=0):
                    with e.Fori(first, n // 2) as half:
                        load_pair(half * 2, b0, n, w, width)

                load_pair(0, 0, W_IN, w_in, BW)
                wait_x(e, it, 0)
                e.dma_start(PAR[:, :], par[bass.ds(L, 1), :, :].rearrange("o p n -> p (o n)")).then_inc(par_loaded, 16)
                loads(0, W_IN, w_in, BW, 1)
                loads(B_Q, W_Q, w_q, BW)
                loads(B_KV, W_KV, w_kv, S)
                loads(B_OUT, W_OUT, w_out, BW)
                loads(B_GU, W_GU, w_gu, BW)
                with e.Fori(0, KD // 2) as half:
                    j = half * 2
                    for jj in range(2):
                        at_k = 0
                        for r, nk in enumerate(DOWN_K):
                            src = w_down[bass.ds(L * KD + j + jj, 1), :, at_k * P:(at_k + nk) * P]
                            load(j * 3 + (B_DOWN + 3 * jj + r), (3 * jj + r) % 2,
                                 src.rearrange("o p n -> p (o n)"), nk * P)
                            at_k += nk
            for s in range(NSEQ):
                for k in range(KD):
                    e.wait_ge(fin_ready, s * KD + k + 1)
                    e.dma_start(out[s, k], tmp[:, k % 2, :]).then_inc(out_written[k % 2], 16)
            for slot in range(2):
                e.wait_ge(out_written[slot], 16 * NSEQ * KD // 2)

        @block.scalar
        def _(e):
            e.wait_ge(const_loaded, 32)
            e.wait_ge(x_loaded[0], 16)

            def square(inp, q0, k):
                e.wait_ge(sq_used, q0 + (k + 1 + (k == 0)))
                alone(e)
                e.activation(sq[:, k % 2, :], inp, ACT.Square).then_inc(sq_ready, 1)

            def root(n0, n, q0, k, width):
                e.wait_ge(sq_used, q0 + (k + 2))
                e.activation(rstd[:, :], ss_bank[:, :], ACT.Ln, scale=1.0 / width, bias=c("eps"))\
                    .then_inc(ln_ready, 1)
                e.wait_ge(ln_ready, n0 + (n + 2))
                e.activation(rstd[:, :], rstd[:, :], ACT.Exp, scale=-0.5).then_inc(rstd_ready, 1)

            def split_attn(m, k):
                e.wait_ge(tmp_ready, m + (k + 1))
                e.activation(H_hi[:, k, :], tmp[:, k % 2, :], ACT.Copy).then_inc(hi_ready, 1)

            for k in range(KD):
                square(X[:, 0, k, :], 0, k)
            root(0, 0, 0, KD, D)
            e.dma_start(X[:, 1, :, :], xT[1].rearrange("k p t -> p k t")).then_inc(x_loaded[1], 16)
            for k in range(KD):
                split_attn(0, k)

            with e.Fori(0, DEPTH) as L, e.Fori(0, NSEQ) as s:
                it = e.snap(L * NSEQ + s)
                n0, q0, l0, m0 = it * SUMS, it * SQUARES, it * SPLITS, it * TMPS
                b0, t0 = it * BLOCKS, it * TILES

                def split_w(b, slot, width, used):
                    e.wait_ge(w_loaded[slot], b0 * 8 + ((b - slot) * 8 + 16))
                    if used is not None:
                        e.wait_ge(used[0], used[1])
                    e.activation(Whi[:, slot, 0:width], Wraw[:, slot, 0:width], ACT.Copy).then_inc(w_hi, 1)

                def after_tile(t):
                    return tile_ready, t0 + (t + 1)

                def split_tmp(l, dst):
                    e.wait_ge(tmp_ready, m0 + (l + 1))
                    e.activation(dst, tmp[:, l % 2, :], ACT.Copy).then_inc(hi_ready, 1)

                split_w(0, 0, BW, (down_part, it * (2 * KD) + 1))
                wait_x(e, it, 0)
                split_w(1, 1, BW, None)

                for t in range(W_IN):
                    b = t + 2
                    split_w(b, b % 2, BW, after_tile(t))
                    if PT_Q <= t < PT_Z:
                        wait_tile_out(e, it, t)
                        e.activation(PRJ[:, t, :], PRJ[:, t, :], ACT.Silu).then_inc(silu_ready, 1)
                    elif t >= PT_Z:
                        e.activation(PRJ[:, t, :], bank[t % 2][:, :], ACT.Silu).then_inc(tile_free[t % 2], 1)
                    if t == LAT_SQ_AT:
                        for k in range(3):
                            wait_tile_out(e, it, PT_QLAT + k)
                        for k in range(3):
                            e.activation(LAT[:, k, :], PRJ[:, PT_QLAT + k, :], ACT.Square).then_inc(lat_sq, 1)
                    elif t == LAT_SUM_AT + 1:
                        for i, width in enumerate((Q_LORA, KV_LORA)):
                            e.wait_ge(lat_sum, it * 2 + (i + 1))
                            e.activation(LAT[:, 3 + i, :], bank[6 + i][:, :], ACT.Ln, scale=1.0 / width, bias=c("eps"))\
                                .then_inc(lat_ln, 1)
                        e.wait_ge(lat_ln, it * 2 + 2)
                        e.activation(LAT[:, 3:5, :], LAT[:, 3:5, :], ACT.Exp, scale=-0.5).then_inc(lat_rstd, 1)
                    elif t == W_IN - 3:
                        for k in range(2):
                            split_tmp(L_LAT + k, QN_hi[:, k, :])
                    elif t == W_IN - 2:
                        split_tmp(L_LAT + 2, QN_hi[:, 2, :])

                for h in range(HEADS):
                    e.wait_ge(tile_ready, t0 + (T_Q + h + 1))
                    e.activation(QH[0:64, h, :], bank[h % 2][0:64, :], ACT.Copy).then_inc(qnope_ready, 1)
                    if h % PAIRS == PAIRS - 1:
                        split_w(B_KV + h // PAIRS, h // PAIRS, S, None)
                e.wait_ge(krope_parts, it * 3 + 3)
                e.activation(KH[64:96, :, :], RT[64:96, 0:1, :].to_broadcast([ROPE, HEADS, S]), ACT.Copy)\
                    .then_inc(krope_ready, 1)
                for t in range(T_V, T_V + S // P):
                    e.wait_ge(tile_ready, t0 + (t + 1))
                    e.activation(V[:, t - T_V, :], bank[t % 2][:, :], ACT.Copy).then_inc(tile_free[t % 2], 1)

                def outputs_high(hp):
                    e.wait_ge(pv_done[1], it * PAIRS + hp + 2)
                    alone(e)
                    e.activation(tile_of(H_hi, hp), bank[6][:, :], ACT.Copy).then_inc(yhi_ready, 1)

                def attend(hp, first):
                    for odd in range(2):
                        h4 = (it * HEADS + hp * 2 + odd) * 4

                        def evict(j):
                            e.wait_ge(pt_psum, h4 + (j + 1))
                            e.activation(PT[:, :, j * P:(j + 1) * P],
                                         bank[4 + j % 2][:, :].rearrange("p (k q) -> p k q", k=4), ACT.Copy)\
                                .then_inc(pt_ready, 1)

                        for j in range(4):
                            e.wait_ge(bias_ready, h4 + (j + 1))
                            if j >= 2:
                                e.wait_ge(pt_psum, h4 + (j - 1))
                            e.activation(PEXP[:, j % 2, :], bank[2 + j % 2][:, :], ACT.Exp, bias=stat[:, j, 1:2],
                                         scale=ATT_SCALE, accum_out=stat[:, j, 2:3]).then_inc(exp_ready, 1)
                            if j:
                                evict(j - 1)
                            if j == 1 and not odd and not first:
                                outputs_high(hp - 1)
                        evict(3)

                attend(0, True)
                with e.Fori(1, PAIRS) as hp:
                    attend(hp, False)
                outputs_high(PAIRS - 1)
                for b in range(2):
                    split_w(B_OUT + b, b, BW, None)

                e.wait_ge(par_loaded, it * 16 + 16)
                e.wait_ge(g_zero, it + 1)
                e.activation(G2[0:16, 0, :], PRJ[0:16, PT_MISC, :], ACT.Abs, bias=PAR[0:16, C_DT:C_DT + 1])\
                    .then_inc(gate_step, 1)
                e.wait_ge(gate_step, it * 5 + 1)
                e.activation(G2[0:16, 0, :], G2[0:16, 0, :], ACT.Exp, scale=-1.0).then_inc(gate_step, 1)
                e.activation(NEGA[0:16, :], PAR[0:16, C_ALOG:C_ALOG + 1], ACT.Exp).then_inc(gate_step, 1)
                e.activation(G[32:48, :], PRJ[32:48, PT_MISC, :], ACT.Sigmoid).then_inc(gate_step, 1)
                e.wait_ge(gate_step, it * 5 + 4)
                e.activation(G2[0:16, 0, :], G2[0:16, 0, :], ACT.Ln, bias=c("ones")[0:16, 0:1])\
                    .then_inc(gate_step, 1)

                def head_norms(done, n, b0, width):
                    for t in range(n):
                        e.wait_ge(head_sum, it * 12 + (done + t + 1))
                        e.activation(RS8[:, t, :], bank[b0 + t][:, :], ACT.Ln, scale=1.0 / width, bias=c("eps"))\
                            .then_inc(head_ln, 1)
                    for t in range(0, n, 2):
                        e.wait_ge(head_ln, it * 12 + (done + t + 2))
                        e.activation(RS8[:, t:t + 2, :], RS8[:, t:t + 2, :], ACT.Exp, scale=-0.5)\
                            .then_inc(head_rstd, 1)

                head_norms(0, 8, 0, 1)
                e.wait_ge(gt_psum, it + 1)
                e.activation(GT[:, :, :].rearrange("p n g -> p (n g)"), bank[2][:, 0:NCH * 16], ACT.Copy)\
                    .then_inc(gt_ready, 1)
                e.wait_ge(gt_ready, it + 1)
                e.wait_ge(l2_ready, it * 8 + 8)

                def chunk_of(d, n):
                    return (NCH - 1) - n if d else n

                def stage_cols(d, n):
                    for to, fr in ((4, 8), (12, 0)):
                        e.activation(gdn[d]["col"][:, to:to + 4],
                                     GT[:, bass.ds(chunk_of(d, n), 1), fr + d * 4:fr + d * 4 + 4]
                                     .rearrange("p o g -> p (o g)"), ACT.Copy).then_inc(gs[d]["staged"], 1)

                def stage_kq(d, n):
                    for i, t in enumerate((PT_K, PT_Q)):
                        e.activation(gdn[d]["kq"][:, :, i, :], PRJ[:, t:t + PAIRS, bass.ds(chunk_of(d, n) * CH, CH)],
                                     ACT.Copy)

                def stage_diagonal(d, n, nm, t):
                    for h in range(2):
                        rows = slice(h * CH, h * CH + CH)
                        cp = e.activation(halves(gdn[d][nm][:, :])[rows, :, h, :],
                                          PRJ[rows, t:t + PAIRS, bass.ds(chunk_of(d, n) * CH, CH)], ACT.Copy)
                    cp.then_inc(gs[d]["kv_staged"], 1)

                def decays(st):
                    for d in range(2):
                        g, q = gdn[d], gs[d]
                        e.wait_ge(q["decay_psum"], st + 1)
                        e.activation(g["dte"][:, :], B[d][3][:, :], ACT.Exp).then_inc(q["decay_exp"], 1)
                        e.wait_ge(q["beta_psum"], st + 1)
                        e.activation(g["col"][:, 0:4], B[d][1][:, SW:SW + 4], ACT.Exp)
                        e.activation(g["col"][:, 8:12], B[d][1][:, SW + 4:SW + 8], ACT.Exp).then_inc(q["cols_exp"], 1)

                def step(n, last):
                    st = e.snap(it * NCH + n)
                    for d in range(2):
                        g, q = gdn[d], gs[d]
                        e.wait_ge(q["nat_psum"], st + 1)
                        alone(e)
                        for p in range(PAIRS):
                            w = slice(p * P, (p + 1) * P)
                            cp = e.activation(g["bv"][:, w], B[d][1][:, w], ACT.Copy, scale=g["col"][:, 4 + p:5 + p])
                        cp.then_inc(q["bv_ready"], 1)
                    for l in range(1, LEVELS):
                        for d in range(2):
                            g, q = gdn[d], gs[d]
                            e.wait_ge(q["y_psum"], st * 5 + l)
                            e.activation(g["ys"][:, :], B[d][0][:, :], ACT.Copy).then_inc(q["y_ready"], 1)
                        for d in range(0 if last else 2):
                            g, q = gdn[d], gs[d]
                            if l == 1:
                                e.wait_ge(q["kbe_qg"], st * 2 + 2)
                                alone(e)
                                stage_kq(d, n + 1)
                            elif l == 2:
                                stage_diagonal(d, n + 1, "kc", PT_K)
                            elif l == 4:
                                e.wait_ge(q["scaled"], st + 1)
                                alone(e)
                                stage_cols(d, n + 1)
                            elif l == 5:
                                e.wait_ge(q["zt_psum"], st * 5 + 5)
                                alone(e)
                                stage_diagonal(d, n + 1, "vc", PT_V)
                    for d in range(2):
                        g, q = gdn[d], gs[d]
                        e.wait_ge(q["vn_psum"], st + 1)
                        e.activation(g["vn"][:, :], B[d][1][:, :], ACT.Copy).then_inc(q["vn_ready"], 1)
                    if not last:
                        decays(st + 1)

                for d in range(2):
                    g, q = gdn[d], gs[d]
                    e.wait_ge(q["o_added"], it * NCH + 1)
                    e.wait_ge(q["state_new"], it * (NCH + 1) + 1)
                    alone(e)
                    stage_cols(d, 0)
                for d in range(2):
                    stage_kq(d, 0)
                    stage_diagonal(d, 0, "kc", PT_K)
                    stage_diagonal(d, 0, "vc", PT_V)
                decays(it * NCH)
                with e.Fori(0, NCH - 1) as n:
                    step(n, False)
                step(NCH - 1, True)

                head_norms(8, 4, 2, DV)
                for t in range(4):
                    split_tmp(L_Y + t, H_hi[:, 4 + t, :])

                with e.Fori(0, W_OUT // 2) as half:
                    i = half * 2
                    for j in range(2):
                        split_w(i + (B_OUT + 2 + j), j, BW, after_tile(i + (T_OUT + j)))
                    for j in range(2):
                        e.wait_ge(tile_free[j], it * (TILES // 2) + (half + (T_OUT // 2 + 2)))
                        e.wait_ge(sq_used, q0 + i + (Q_FFN + j + 1))
                        alone(e)
                        xt = X[:, bass.ds(s, 1), bass.ds(i + j, 1), :].rearrange("p o k t -> p (o k t)")
                        e.activation(sq[:, j, :], xt, ACT.Square).then_inc(sq_ready, 1)
                root(n0, N_FFN, q0, Q_FFN + KD, D)
                for k in range(KD):
                    split_tmp(L_FFN + k, H_hi[:, k, :])

                def gate_up(f, last):
                    for j in range(2):
                        fj = f + j
                        for m in range(2):
                            if last and j:
                                split_w(B_DOWN + m, m, DOWN_K[m] * P, after_tile(T_DOWN - 2 + m))
                            else:
                                split_w(fj * 2 + (B_GU + 2 + m), m, BW, after_tile(fj * 2 + (T_GU + m)))
                            if m == 0:
                                e.activation(SG[:, j, :], bank[0][:, :], ACT.Silu).then_inc(tile_free[0], 1)
                        e.wait_ge(tile_free[1], it * (TILES // 2) + (fj + (T_GU // 2 + 2)))
                        alone(e)
                        e.activation(tile_of(A_hi, fj) if not last else A_hi[:, fj, :],
                                     tmp[:, (L_A + j) % 2, :], ACT.Copy).then_inc(hi_ready, 1)

                with e.Fori(0, NF // 2 - 1) as half:
                    f = half * 2
                    gate_up(f, False)
                gate_up(NF - 2, True)

                def down_w(j, r):
                    b = j * 3 + (B_DOWN + r)
                    if r == 0:
                        used = down_part, it * (2 * KD) + (j * 2 + 1)
                    elif r == 1:
                        used = tile_ready, t0 + (j + T_DOWN)
                    else:
                        used = down_part, it * (2 * KD) + (j * 2 + 2)
                    return b, used

                for j in range(KD):
                    for r in range(3):
                        if j == 0 and r < 2:
                            continue
                        b, used = down_w(j, r)
                        split_w(b, (3 * j + r) % 2, DOWN_K[r] * P, used)
                        if r < 2 and 3 <= j < 7:
                            split_attn(m0 + TMPS, 2 * (j - 3) + r)
                        if (j, r) in ((1, 2), (2, 1)):
                            if j == 1:
                                e.wait_ge(x_loaded[1], 16)
                            for k in range(2) if j == 1 else range(2, KD):
                                square(x_tile(1 - s, k), q0 + SQUARES, k)
                            if j == 2:
                                root(n0 + SUMS, 0, q0 + SQUARES, KD, D)

            wait_x(e, DEPTH * NSEQ, 0)
            q0 = DEPTH * NSEQ * SQUARES + KD
            for k in range(KD):
                square(X[:, 1, k, :], q0, k)
            e.wait_ge(fin_ready, KD)
            root(DEPTH * NSEQ * SUMS, 1, q0, KD, D)

        @block.gpsimd
        def _(e):
            e.wait_ge(const_loaded, 32)

            def low_attn(l, k):
                e.wait_ge(hi_ready, l + (k + 1))
                e.tensor_tensor(H_lo[:, k, :], tmp[:, k % 2, :], H_hi[:, k, :].bitcast(F32), ALU.subtract)\
                    .then_inc(lo_ready, 1)

            for k in range(KD):
                low_attn(0, k)
            with e.Fori(0, DEPTH) as L, e.Fori(0, NSEQ) as s:
                it = e.snap(L * NSEQ + s)
                l0, b0, t0 = it * SPLITS, it * BLOCKS, it * TILES

                def low_w(b, slot, width):
                    e.wait_ge(w_hi, b0 + (b + 1))
                    e.tensor_tensor(Wlo[:, slot, 0:width], Wraw[:, slot, 0:width],
                                    Whi[:, slot, 0:width].bitcast(F32), ALU.subtract).then_inc(w_lo, 1)

                def low_tmp(l, parity, dst, hi):
                    e.wait_ge(hi_ready, l0 + (l + 1))
                    e.tensor_tensor(dst, tmp[:, parity, :], hi.bitcast(F32), ALU.subtract).then_inc(lo_ready, 1)

                for b in range(2):
                    low_w(b, b, BW)
                with e.Fori(0, W_IN // 2 - 1) as half:
                    i = half * 2
                    for j in range(2):
                        low_w(i + (2 + j), j, BW)
                for k in range(3):
                    low_tmp(L_LAT + k, (L_LAT + k) % 2, QN_lo[:, k, :], QN_hi[:, k, :])
                for j in range(2):
                    low_w(W_IN + j, j, BW)
                for b in range(2):
                    low_w(B_KV + b, b, S)
                e.wait_ge(qrope_ready, it * HEADS + HEADS)
                e.wait_ge(qnope_ready, it * HEADS + HEADS)
                e.wait_ge(krope_ready, it + 1)
                alone(e)
                def stage_pair(hp, first):
                    for odd in range(2):
                        e.wait_ge(pv_done[odd], it * PAIRS + hp + 1)
                        alone(e)
                        e.tensor_copy(RT[0:QK, odd, :], tile_of(QH, hp * 2 + odd, slice(0, QK))).then_inc(head_staged, 1)
                        if first and not odd:
                            wait_tile_out(e, it, T_V + 2)
                            wait_tile_out(e, it, T_V + 3)
                            alone(e)
                        e.tensor_copy(VS[:, odd, :, :], V[:, :, bass.ds((hp * 2 + odd) * DV, DV)])\
                            .then_inc(head_staged, 1)

                stage_pair(0, True)
                with e.Fori(1, PAIRS) as hp:
                    stage_pair(hp, False)
                e.wait_ge(ylo_ready, it * PAIRS + PAIRS + 1)
                alone(e)
                e.memset(G[0:48, :], 0.0).then_inc(g_zero, 1)
                for b in range(2):
                    low_w(B_OUT + b, b, BW)
                e.wait_ge(gate_step, it * 5 + 5)
                e.wait_ge(decay_step, it * 3 + 3)
                alone(e)
                e.memset(O, 0.0).then_inc(o_zero, 1)
                for d in range(2):
                    for n in ("kc", "vc", "st"):
                        ms = e.memset(gdn[d][n][:, :], 0.0)
                    ms.then_inc(gs[d]["state_new"], 1)
                def decay_rhs(st):
                    for d in range(2):
                        g, q = gdn[d], gs[d]
                        e.wait_ge(q["staged"], st * 2 + 2)
                        e.tensor_tensor(pairs(g["rr"][:, 0:SW]), spread(g["col"][:, 12:16], PAIRS),
                                        each(c(f"upto{d}")), ALU.mult).then_inc(q["decay_rhs"], 1)
                        e.tensor_tensor(pairs(g["rr"][:, SW:]), spread(g["col"][:, 4:8], PAIRS),
                                        each(c("eye_pair")), ALU.mult).then_inc(q["decay_rhs"], 1)

                def step(n, last):
                    st = e.snap(it * NCH + n)
                    for l in range(LEVELS):
                        for d in range(2):
                            g, q = gdn[d], gs[d]
                            if l == 0:
                                e.wait_ge(q["mt_at"], st * 2 + 1)
                            elif l == 2:
                                e.wait_ge(q["tt_ready"], st * 6 + 1)
                            elif l > 2:
                                e.wait_ge(q["y_psum"], st * 5 + (l - 2))
                            join = c(f"join{d}{l}").rearrange("p (h t) -> p h t", h=2).unsqueeze(1)
                            e.tensor_tensor(halves(g["ml"][:, l % 2, :]), twice(g["mt"]),
                                            join.to_broadcast([P, PAIRS, 2, CH]), ALU.mult).then_inc(q["masked"], 1)
                    for d in range(2):
                        g, q = gdn[d], gs[d]
                        e.wait_ge(q["cols_exp"], st + 1)
                        e.wait_ge(q["state_new"], st + it + 1)
                        e.wait_ge(q["kbe_qg"], st * 2 + 2)
                        e.wait_ge(q["masked"], st * 6 + 6)
                        e.tensor_tensor(pairs(g["ssc"][:, :]), pairs(g["st"][:, :]),
                                        spread(g["col"][:, 8:12], PAIRS, P), ALU.mult).then_inc(q["scaled"], 1)
                    if not last:
                        decay_rhs(st + 1)

                decay_rhs(it * NCH)
                with e.Fori(0, NCH - 1) as n:
                    step(n, False)
                step(NCH - 1, True)
                for t in range(4):
                    low_tmp(L_Y + t, (L_Y + t) % 2, H_lo[:, 4 + t, :], H_hi[:, 4 + t, :])
                with e.Fori(0, W_OUT // 2) as half:
                    i = half * 2
                    for j in range(2):
                        low_w(i + (B_OUT + 2 + j), j, BW)
                for k in range(KD):
                    low_tmp(L_FFN + k, (L_FFN + k) % 2, H_lo[:, k, :], H_hi[:, k, :])

                def gate_up(f, last):
                    for j in range(2):
                        for m in range(2):
                            if last and j:
                                low_w(B_DOWN + m, m, DOWN_K[m] * P)
                            else:
                                low_w((f + j) * 2 + (B_GU + 2 + m), m, BW)
                        a = (lambda t: t[:, f + j, :]) if last else (lambda t: tile_of(t, f + j))
                        low_tmp(f + (L_A + j), (L_A + j) % 2, a(A_lo), a(A_hi))

                with e.Fori(0, NF // 2 - 1) as half:
                    f = half * 2
                    gate_up(f, False)
                gate_up(NF - 2, True)

                for j in range(KD):
                    for r in range(3):
                        if j or r == 2:
                            low_w(3 * j + (B_DOWN + r), (3 * j + r) % 2, DOWN_K[r] * P)
                        if r < 2 and 3 <= j < 7:
                            low_attn(l0 + SPLITS, 2 * (j - 3) + r)

        @block.vector
        def _(e):
            e.wait_ge(const_loaded, 32)
            e.wait_ge(x_loaded[0], 16)

            def normalise_attn(inp, gain, n, l, k):
                e.wait_ge(rstd_ready, n + 1)
                e.wait_ge(lo_ready, l + (k + 1 + (k == 0)))
                alone(e)
                e.scalar_tensor_tensor(tmp[:, k % 2, :], inp, gain, rstd[:, :], ALU.mult, ALU.mult)\
                    .then_inc(tmp_ready, 1)

            for k in range(KD):
                normalise_attn(X[:, 0, k, :], GAIN[:, 0, k:k + 1], 0, 0, k)
            with e.Fori(0, DEPTH) as L, e.Fori(0, NSEQ) as s:
                it = e.snap(L * NSEQ + s)
                n0, l0, t0 = it * SUMS, it * SPLITS, it * TILES

                def tmp_free(l):
                    e.wait_ge(lo_ready, l0 + (l + 1 + (isinstance(l, int) and l == 0)))

                def normalise(inp, gain, n, l, scale=None):
                    if scale is None:
                        scale = rstd[:, :]
                        e.wait_ge(rstd_ready, n0 + (n + 1))
                    tmp_free(l)
                    e.scalar_tensor_tensor(tmp[:, l % 2, :], inp, gain, scale, ALU.mult, ALU.mult)\
                        .then_inc(tmp_ready, 1)

                e.wait_ge(par_loaded, it * 16 + 16)

                for t in range(PT_Z):
                    e.wait_ge(tile_ready, t0 + (t + 1))
                    pb, free = bank[t % 2], tile_free[t % 2]
                    if t < PT_Q:
                        e.tensor_copy(PRJ[:, t, :], pb[:, :]).then_inc(free, 1)
                        continue
                    w = [PAR[:, C_CONV + 3 * (t - PT_Q) + i:C_CONV + 3 * (t - PT_Q) + i + 1] for i in range(3)]
                    y = PRJ[:, t, :]
                    e.tensor_scalar(y, pb[:, :], w[1], None, ALU.mult).then_inc(conv_step, 1)
                    e.wait_ge(conv_step, it * 24 + (2 * (t - PT_Q) + 1))
                    e.scalar_tensor_tensor(y[:, 1:S], pb[:, 0:S - 1], w[0], y[:, 1:S], ALU.mult, ALU.add)\
                        .then_inc(conv_step, 1)
                    e.wait_ge(conv_step, it * 24 + (2 * (t - PT_Q) + 2))
                    e.scalar_tensor_tensor(y[:, 0:S - 1], pb[:, 1:S], w[2], y[:, 0:S - 1], ALU.mult, ALU.add)\
                        .then_inc(free, 1)

                e.wait_ge(lat_rstd, it + 1)
                for k in range(2):
                    normalise(PRJ[:, PT_QLAT + k, :], PAR[:, C_QN + k:C_QN + k + 1], None, L_LAT + k, LAT[:, 3, :])
                normalise(PRJ[:, PT_KVLAT, :], PAR[:, C_KVN:C_KVN + 1], None, L_LAT + 2, LAT[:, 4, :])

                e.wait_ge(tile_ready, t0 + W_IN)
                alone(e)
                r0, r1 = RT[64:96, 0, :], RT[64:96, 1, :]
                e.tensor_tensor(r0, PRJ[64:96, PT_MISC, :], c("rope", slice(64, 96)), ALU.mult).then_inc(krope_parts, 1)
                e.tensor_tensor(r1, PRJ[96:128, PT_MISC, :], c("rope", slice(96, 128)), ALU.mult)\
                    .then_inc(krope_parts, 1)
                e.wait_ge(krope_parts, it * 3 + 2)
                e.tensor_tensor(r0, r0, r1, ALU.add).then_inc(krope_parts, 1)
                r0, r1 = sq[64:96, 0, :], sq[64:96, 1, :]
                for h in range(HEADS):
                    t = T_Q + h
                    pb = bank[t % 2]
                    e.wait_ge(tile_ready, t0 + (t + 1))
                    if h:
                        e.wait_ge(qrope_ready, it * HEADS + h)
                    e.tensor_tensor(r0, pb[64:96, :], c("rope", slice(64, 96)), ALU.mult).then_inc(qrope_parts, 1)
                    e.tensor_tensor(r1, pb[96:128, :], c("rope", slice(96, 128)), ALU.mult).then_inc(tile_free[t % 2], 1)
                    e.wait_ge(qrope_parts, it * HEADS + (h + 1))
                    wait_tile_out(e, it, t)
                    e.tensor_tensor(QH[64:96, h, :], r0, r1, ALU.add).then_inc(qrope_ready, 1)
                for h in range(HEADS):
                    t = T_KN + h
                    e.wait_ge(tile_ready, t0 + (t + 1))
                    e.tensor_copy(KH[0:64, h, :], bank[t % 2][0:64, :]).then_inc(tile_free[t % 2], 1)

                def outputs_low(hp):
                    e.wait_ge(yhi_ready, it * PAIRS + hp + 1)
                    e.tensor_tensor(tile_of(H_lo, hp), bank[6][:, :], tile_of(H_hi, hp).bitcast(F32), ALU.subtract)\
                        .then_inc(ylo_ready, 1)

                def maximum(h4, j):
                    e.wait_ge(sc_ready, h4 + (j + 1))
                    j = j % 4
                    e.tensor_reduce(stat[:, j, 0:1], bank[2 + j % 2][:, :], AX_X, ALU.max).then_inc(max_ready, 1)

                def bias(h4, j):
                    e.wait_ge(max_ready, h4 + (j + 1))
                    j = j % 4
                    e.tensor_scalar(stat[:, j, 1:2], stat[:, j, 0:1], -ATT_SCALE, None, ALU.mult)\
                        .then_inc(bias_ready, 1)

                def attend(hp, first, last):
                    for odd in range(2):
                        h4 = (it * HEADS + hp * 2 + odd) * 4
                        if first and not odd:
                            for j in range(2):
                                maximum(h4, j)
                                bias(h4, j)
                        for j in range(4):
                            e.wait_ge(exp_ready, h4 + (j + 1))
                            e.reciprocal(stat[:, j, 3:4], stat[:, j, 2:3]).then_inc(rsum_ready, 1)
                            e.wait_ge(rsum_ready, h4 + (j + 1))
                            e.tensor_scalar(PEXP[:, j % 2, :], PEXP[:, j % 2, :], stat[:, j, 3:4], None, ALU.mult)\
                                .then_inc(prob_ready, 1)
                            if j < 2 or not (last and odd):
                                maximum(h4, j + 2)
                                bias(h4, j + 2)
                            if j == 1 and not odd and not first:
                                outputs_low(hp - 1)

                attend(0, True, False)
                with e.Fori(1, PAIRS - 1) as hp:
                    attend(hp, False, False)
                attend(PAIRS - 1, False, True)
                outputs_low(PAIRS - 1)

                e.wait_ge(silu_ready, it * 12 + 12)
                e.wait_ge(ylo_ready, it * PAIRS + PAIRS + 1)
                alone(e)
                for t in range(8):
                    y = PRJ[:, PT_Q + t, :]
                    e.tensor_tensor(SQ8[:, t, :], y, y, ALU.mult).then_inc(head_sq, 1)
                e.wait_ge(g_zero, it + 1)
                e.tensor_scalar(G2[0:16, 1, :], PRJ[0:16, PT_MISC, :], PAR[0:16, C_DT:C_DT + 1], 0.0, ALU.add, ALU.max)\
                    .then_inc(decay_step, 1)
                e.wait_ge(gate_step, it * 5 + 5)
                e.wait_ge(decay_step, it * 3 + 1)
                e.tensor_tensor(G2[0:16, 1, :], G2[0:16, 1, :], G2[0:16, 0, :], ALU.add).then_inc(decay_step, 1)
                e.wait_ge(decay_step, it * 3 + 2)
                e.tensor_scalar(G[0:16, :], G2[0:16, 1, :], NEGA[0:16, 0:1], -1.0, ALU.mult, ALU.mult)\
                    .then_inc(decay_step, 1)
                for t in range(8):
                    y = PRJ[:, PT_Q + t, :]
                    e.wait_ge(head_rstd, it * 6 + (t // 2 + 1))
                    e.scalar_tensor_tensor(y, y, CH ** -0.5 if t < PAIRS else 1.0, RS8[:, t, :], ALU.mult, ALU.mult)\
                        .then_inc(l2_ready, 1)

                def decays(st):
                    for d in range(2):
                        g, q = gdn[d], gs[d]
                        e.wait_ge(q["decay_exp"], st + 1)
                        e.tensor_tensor(pairs(g["dtm"]), pairs(g["dte"][:, 0:SW]), each(c(f"upto{d}")), ALU.mult)\
                            .then_inc(q["dtm"], 1)
                    for d in range(2):
                        g, q = gdn[d], gs[d]
                        e.wait_ge(q["cols_exp"], st + 1)
                        e.wait_ge(q["dtm"], st + 1)
                        e.tensor_tensor(g["db"], g["dtm"], B[d][1][:, 0:SW], ALU.mult).then_inc(q["db"], 1)

                def step(n, last):
                    st = e.snap(it * NCH + n)
                    chunk = [n, (NCH - 1) - n]
                    for d in range(2):
                        g, q = gdn[d], gs[d]
                        e.wait_ge(q["state_new"], st + it + 1)
                        e.tensor_tensor(g["wk"], g["dte"][:, SW:], B[d][1][:, 0:SW], ALU.mult).then_inc(q["db"], 1)
                    for d in range(2):
                        g, q = gdn[d], gs[d]
                        e.wait_ge(q["db"], st * 2 + 2)
                        e.wait_ge(q["kk_psum"], st + 1)
                        e.tensor_tensor(pairs(g["mt"]), halves(B[d][3][:, :])[:, :, 0, :], pairs(g["db"]), ALU.mult)\
                            .then_inc(q["mt_at"], 1)
                    for d in range(2):
                        g, q = gdn[d], gs[d]
                        e.tensor_tensor(pairs(g["at"][:, :]), halves(B[d][3][:, :])[:, :, 1, :], pairs(g["dtm"]), ALU.mult)\
                            .then_inc(q["mt_at"], 1)
                    for d in range(2):
                        g, q = gdn[d], gs[d]
                        e.wait_ge(q["nat_psum"], st + 1)
                        e.wait_ge(q["cols_exp"], st + 1)
                        e.tensor_tensor(pairs(g["kg"][:, :]), pairs(B[d][0][:, :]),
                                        spread(g["col"][:, 0:4], PAIRS, P), ALU.mult).then_inc(q["kg_ready"], 1)
                        e.wait_ge(q["b1_psum"], st + 1)
                        eye = each(c("eye"), PAIRS, P)
                        e.tensor_tensor(pairs(g["T"][:, :]), eye, pairs(B[d][2][:, :]), ALU.subtract)\
                            .then_inc(q["t_ready"], 1)
                        e.tensor_tensor(pairs(g["TT"][:, :]), eye, pairs(g["ml"][:, 0, :]), ALU.subtract)\
                            .then_inc(q["tt_ready"], 1)
                    for d in range(2):
                        g, q = gdn[d], gs[d]
                        e.tensor_tensor(halves(g["kbe"][:, :]), halves(g["kc"][:, :]), twice(g["wk"]), ALU.mult)\
                            .then_inc(q["kbe_qg"], 1)
                        e.tensor_tensor(pairs(g["qg"][:, :]), g["kq"][:, :, 1, :], pairs(g["dte"][:, SW:]), ALU.mult)\
                            .then_inc(q["kbe_qg"], 1)
                    for l in range(1, LEVELS):
                        for d in range(2):
                            g, q = gdn[d], gs[d]
                            if l < LEVELS - 1:
                                e.wait_ge(q["z_psum"], st * 4 + l)
                                e.wait_ge(q["t_ready"], st * 5 + l)
                                e.tensor_tensor(g["T"][:, :], g["T"][:, :], B[d][1][:, :], ALU.subtract)\
                                    .then_inc(q["t_ready"], 1)
                            e.wait_ge(q["zt_psum"], st * 5 + l)
                            e.wait_ge(q["tt_ready"], st * 6 + l)
                            e.tensor_tensor(g["TT"][:, :], g["TT"][:, :], B[d][2][:, :], ALU.subtract)\
                                .then_inc(q["tt_ready"], 1)
                    for d in range(2):
                        g, q = gdn[d], gs[d]
                        e.wait_ge(q["ks_psum"], st + 1)
                        e.wait_ge(q["bv_ready"], st + 1)
                        e.tensor_tensor(g["r"][:, :], g["bv"][:, :], B[d][0][:, :], ALU.subtract)\
                            .then_inc(q["r_ready"], 1)
                    if not last:
                        decays(st + 1)
                    for d in range(2):
                        g, q = gdn[d], gs[d]
                        e.wait_ge(q["o_psum"], st + 1)
                        e.wait_ge(q["scaled"], st + 1)
                        e.tensor_tensor(g["st"][:, :], g["ssc"][:, :], B[d][2][:, :], ALU.add)\
                            .then_inc(q["state_new"], 1)
                        e.wait_ge(gs[1 - d]["o_added"], st + (1 + d))
                        alone(e)
                        oc = O[:, :, bass.ds(chunk[d] * CH, CH)]
                        e.tensor_tensor(oc, oc, pairs(B[d][0][:, 0:SW]), ALU.add).then_inc(q["o_added"], 1)

                decays(it * NCH)
                e.wait_ge(o_zero, it + 1)
                alone(e)
                with e.Fori(0, NCH - 1) as n:
                    step(n, False)
                step(NCH - 1, True)

                for d in range(2):
                    e.wait_ge(gs[d]["o_added"], it * NCH + NCH + 1)
                alone(e)
                for t in range(4):
                    e.tensor_tensor(SQ8[:, t, :], O[:, t, :], O[:, t, :], ALU.mult).then_inc(head_sq, 1)
                for t in range(4):
                    e.wait_ge(head_rstd, it * 6 + (4 + t // 2 + 1))
                    e.scalar_tensor_tensor(O[:, t, :], O[:, t, :], PAR[:, C_GN:C_GN + 1], RS8[:, t, :],
                                           ALU.mult, ALU.mult).then_inc(gated_step, 1)
                    e.wait_ge(gated_step, it * 4 + (t + 1))
                    tmp_free(L_Y + t)
                    if t == 0:
                        wait_tile_out(e, it, W_IN - 2)
                        wait_tile_out(e, it, W_IN - 1)
                    e.tensor_tensor(tmp[:, (L_Y + t) % 2, :], O[:, t, :], PRJ[:, PT_Z + t, :], ALU.mult)\
                        .then_inc(tmp_ready, 1)

                def residual(t, b, k):
                    e.wait_ge(tile_ready, t0 + t + 1)
                    xt = X[:, bass.ds(s, 1), bass.ds(k, 1), :].rearrange("p o k t -> p (o k t)")
                    e.tensor_tensor(xt, xt, bank[b][:, :], ALU.add).then_inc(tile_free[b], 1)

                with e.Fori(0, KD // 2) as half:
                    i = half * 2
                    for j in range(2):
                        residual(i + (T_OUT + j), j, i + j)
                wait_x(e, it, 1)
                for k in range(KD):
                    normalise(x_tile(s, k), PAR[:, C_NF + k:C_NF + k + 1], N_FFN, L_FFN + k)
                with e.Fori(0, NF // 2) as half:
                    f = half * 2
                    for j in range(2):
                        e.wait_ge(tile_ready, t0 + ((f + j) * 2 + (T_GU + 2)))
                        e.wait_ge(tile_free[0], it * (TILES // 2) + (f + j + (T_GU // 2 + 2)))
                        tmp_free(f + (L_A + j))
                        e.tensor_tensor(tmp[:, (L_A + j) % 2, :], SG[:, j, :], bank[1][:, :], ALU.mult)\
                            .then_inc(tile_free[1], 1)
                for j in range(KD):
                    if 3 <= j < 7:
                        for k in range(2 * (j - 3), 2 * (j - 3) + 2):
                            normalise_attn(x_tile(1 - s, k),
                                           GAIN[:, bass.ds(L + s, 1), k:k + 1].rearrange("p o k -> p (o k)"),
                                           n0 + SUMS, l0 + SPLITS, k)
                    residual(T_DOWN + j, j % 2, j)

            wait_x(e, DEPTH * NSEQ, 0)
            for s in range(NSEQ):
                for k in range(KD):
                    n = s * KD + k
                    e.wait_ge(rstd_ready, DEPTH * NSEQ * SUMS + s + 1)
                    if n == 0:
                        e.wait_ge(lo_ready, DEPTH * NSEQ * SPLITS + KD + 2)
                    if n >= 2:
                        e.wait_ge(out_written[k % 2], 16 * (n // 2))
                    e.scalar_tensor_tensor(tmp[:, k % 2, :], X[:, s, k, :], GAIN[:, DEPTH, k:k + 1], rstd[:, :],
                                           ALU.mult, ALU.mult).then_inc(fin_ready, 1)

        @block.tensor
        def _(e):
            e.wait_ge(const_loaded, 32)

            def sum_squares(ones, n_idx, q_idx, k, slot, first, last):
                e.wait_ge(sq_ready, q_idx + (k + 1))
                if first:
                    e.wait_ge(ln_ready, n_idx + 1)
                e.matmul(ss_bank[:, :], ones, sq[:, slot, :], start=first, stop=last).then_inc(sq_used, 1)

            for k in range(KD):
                sum_squares(c("ones"), 0, 0, k, k % 2, k == 0, k == KD - 1)
            with e.Fori(0, DEPTH) as L, e.Fori(0, NSEQ) as s:
                it = e.snap(L * NSEQ + s)
                n0, q0, l0 = it * SUMS, it * SQUARES, it * SPLITS
                b0, t0 = it * BLOCKS, it * TILES

                def bank_free(t, b):
                    e.wait_ge(tile_free[b], it * (TILES // 2) + ((t - b) // 2 + 1))

                def weights(b):
                    e.wait_ge(w_lo, b0 + (b + 3))

                def three(out_, w, a, first, last):
                    e.matmul(out_, w[0], a[0], start=first, stop=False)
                    e.matmul(out_, w[0], a[1], start=False, stop=False)
                    return e.matmul(out_, w[1], a[0], start=False, stop=last)

                def w_part(slot, a, n):
                    return Whi[:, slot, a:a + n], Wlo[:, slot, a:a + n]

                def dense(slot, b, k0=KD, split=None):
                    for k in range(KD):
                        if k >= k0:
                            e.wait_ge(lo_ready, l0 + (split + k + 3))
                        mm = three(bank[b][:, :], w_part(slot, k * P, P), (H_hi[:, k, :], H_lo[:, k, :]),
                                   k == 0, k == KD - 1)
                    return mm

                def dense_pair(i, b, t, k0=KD, split=None):
                    for j in range(2):
                        weights(i * 2 + (b + j))
                        e.wait_ge(tile_free[j], it * (TILES // 2) + (i + (t // 2 + 1)))
                        dense(j, j, KD if j else k0, split).then_inc(tile_ready, 1)

                dense_pair(0, 0, 0, 0, 0)
                with e.Fori(1, LAT_SUM_AT // 2) as i:
                    dense_pair(i, 0, 0)
                e.wait_ge(lat_sq, it * 3 + 3)
                alone(e)
                for k in range(3):
                    mm = e.matmul(bank[6 + k // 2][:, :], c("ones"), LAT[:, k, :], start=k != 1, stop=k != 0)
                    if k:
                        mm.then_inc(lat_sum, 1)
                with e.Fori(LAT_SUM_AT // 2, W_IN // 2) as i:
                    dense_pair(i, 0, 0)
                e.wait_ge(lo_ready, l0 + (L_LAT + 3 + 2))
                for h in range(HEADS):
                    t, slot = T_Q + h, h // PAIRS
                    if h % PAIRS == 0:
                        weights(B_Q + slot)
                    bank_free(t, t % 2)
                    if h >= 2:
                        e.wait_ge(qnope_ready, it * HEADS + (h - 1))
                        alone(e)
                    for k in range(2):
                        mm = three(bank[t % 2][:, :], w_part(slot, k * S + (h % PAIRS) * P, P),
                                   (QN_hi[:, k, :], QN_lo[:, k, :]), k == 0, k == 1)
                    mm.then_inc(tile_ready, 1)
                weights(B_KV)
                for h in range(HEADS):
                    t = T_KN + h
                    bank_free(t, t % 2)
                    if h < 2:
                        e.wait_ge(qnope_ready, it * HEADS + (HEADS - 1 + h))
                        alone(e)
                    three(bank[t % 2][0:64, :], w_part(0, h * NOPE, NOPE), (QN_hi[:, 2, :], QN_lo[:, 2, :]),
                          True, True).then_inc(tile_ready, 1)
                weights(B_KV + 1)
                for k in range(S // P):
                    t = T_V + k
                    bank_free(t, t % 2)
                    wv = w_part(1, 0, S)
                    lat = [q[:, 2, k * P:(k + 1) * P] for q in (QN_hi, QN_lo)]
                    three(bank[t % 2][:, :], lat, wv, True, True).then_inc(tile_ready, 1)

                wait_tile_out(e, it, T_KN + 6)
                wait_tile_out(e, it, T_KN + 7)
                e.wait_ge(krope_ready, it + 1)
                alone(e)
                def scores(hp, odd, j, first=False):
                    h = it * HEADS + hp * 2 + odd
                    if j == 0:
                        e.wait_ge(head_staged, h * 2 + 1)
                    if not first:
                        e.wait_ge(exp_ready, h * 4 + (j - 1))
                    e.matmul(bank[2 + j % 2][:, :], RT[0:QK, odd, j * P:(j + 1) * P],
                             tile_of(KH, hp * 2 + odd, slice(0, QK)), start=True, stop=True).then_inc(sc_ready, 1)

                def attend(hp, last):
                    for odd in range(2):
                        h4 = (it * HEADS + hp * 2 + odd) * 4
                        for j in range(4):
                            if j < 2:
                                scores(hp, odd, j + 2)
                            elif j == 2 and not (last and odd):
                                scores(hp + odd, 1 - odd, 0)
                            e.wait_ge(prob_ready, h4 + (j + 1))
                            if j >= 2:
                                e.wait_ge(pt_ready, h4 + (j - 1))
                            for k in range(4):
                                mm = e.transpose(bank[4 + j % 2][:, k * P:(k + 1) * P],
                                                 PEXP[:, j % 2, k * P:(k + 1) * P], c("eye"))
                            mm.then_inc(pt_psum, 1)
                            if j == 3 and not (last and odd):
                                scores(hp + odd, 1 - odd, 1)
                        e.wait_ge(pt_ready, h4 + 4)
                        e.wait_ge(head_staged, (it * HEADS + hp * 2 + odd) * 2 + 2)
                        if not odd:
                            e.wait_ge(ylo_ready, it * PAIRS + hp + 1)
                            alone(e)
                        for k in range(4):
                            mm = e.matmul(bank[6][64 * odd:64 * odd + 64, :], VS[:, odd, k, :], PT[:, k, :],
                                          start=(k == 0), stop=(k == 3))
                        mm.then_inc(pv_done[odd], 1)

                for j in range(2):
                    scores(0, 0, j, first=True)
                with e.Fori(0, PAIRS - 1) as hp:
                    attend(hp, False)
                attend(PAIRS - 1, True)

                def head_sums(done, n, b0):
                    for t in range(n):
                        e.wait_ge(head_sq, it * 12 + (done + t + 1))
                        alone(e)
                        e.matmul(bank[b0 + t][:, :], c("ones_pair"), SQ8[:, t, :], start=True, stop=True)\
                            .then_inc(head_sum, 1)

                wait_tile_out(e, it, T_V + 2)
                wait_tile_out(e, it, T_V + 3)
                head_sums(0, 8, 0)
                e.wait_ge(head_ln, it * 12 + 8)
                e.wait_ge(decay_step, it * 3 + 3)
                e.wait_ge(gate_step, it * 5 + 5)
                alone(e)
                for n in range(NCH):
                    for p in range(2):
                        mm = e.matmul(bank[2][64 * p:64 * p + 64, n * 16:n * 16 + 16],
                                      G[0:48, n * CH:(n + 1) * CH], c(f"pick{p}", slice(0, 48)), start=True, stop=True)
                mm.then_inc(gt_psum, 1)

                def heads(dst, lhs, rhs):
                    for p in range(PAIRS):
                        w = slice(p * P, (p + 1) * P)
                        mm = e.matmul(dst[:, w], lhs[:, w], rhs[:, w], start=True, stop=True)
                    return mm

                def turned(dst, src):
                    for p in range(PAIRS):
                        w = slice(p * P, (p + 1) * P)
                        mm = e.transpose(dst[:, w], src[:, w], c("eye"))
                    return mm

                def decays(st):
                    for d in range(2):
                        g, q = gdn[d], gs[d]
                        e.wait_ge(q["decay_rhs"], st * 2 + 2)
                        alone(e)
                        e.matmul(B[d][3][:, 0:SW], c(f"after{d}"), g["rr"][:, 0:SW], start=True, stop=True)
                        e.matmul(B[d][3][:, SW:], c("ones_pair"), g["rr"][:, 0:SW], start=True, stop=True)\
                            .then_inc(q["decay_psum"], 1)

                def betas(d):
                    g, q = gdn[d], gs[d]
                    e.matmul(B[d][1][:, SW:SW + 4], c(f"after{d}"), g["col"][:, 12:16], start=True, stop=True)
                    e.matmul(B[d][1][:, SW + 4:SW + 8], c("ones_pair"), g["col"][:, 12:16], start=True, stop=True)
                    e.matmul(B[d][1][:, 0:SW], c("ones_pair"), g["rr"][:, SW:], start=True, stop=True)\
                        .then_inc(q["beta_psum"], 1)

                def step(n, last):
                    st = e.snap(it * NCH + n)
                    for d in range(2):
                        g, q = gdn[d], gs[d]
                        e.wait_ge(q["decay_exp"], st + 1)
                        e.wait_ge(q["kv_staged"], st * 2 + 1)
                        alone(e)
                        heads(B[d][3][:, :], g["kc"], g["kq"][:, :, :, :].rearrange("p q h t -> p (q h t)"))\
                            .then_inc(q["kk_psum"], 1)
                    for d in range(2):
                        g, q = gdn[d], gs[d]
                        e.wait_ge(q["o_added"], st + 1)
                        e.wait_ge(q["cols_exp"], st + 1)
                        e.wait_ge(q["db"], st * 2 + 2)
                        e.wait_ge(q["kv_staged"], st * 2 + 2)
                        alone(e)
                        turned(B[d][0], g["kc"])
                        turned(B[d][1], g["vc"]).then_inc(q["nat_psum"], 1)
                    for d in range(2):
                        g, q = gdn[d], gs[d]
                        e.wait_ge(q["masked"], st * 6 + 1)
                        alone(e)
                        turned(B[d][2], g["ml"][:, 0, :]).then_inc(q["b1_psum"], 1)
                    for l in range(1, LEVELS):
                        for d in range(2):
                            g, q = gdn[d], gs[d]
                            e.wait_ge(q["t_ready"], st * 5 + l)
                            e.wait_ge(q["masked"], st * 6 + (l + 1))
                            if l == 1:
                                e.wait_ge(q["kg_ready"], st + 1)
                            alone(e)
                            heads(B[d][0][:, :], g["ml"][:, l % 2, :], g["T"]).then_inc(q["y_psum"], 1)
                        for d in range(2):
                            g, q = gdn[d], gs[d]
                            e.wait_ge(q["y_ready"], st * 5 + l)
                            e.wait_ge(q["tt_ready"], st * 6 + l)
                            if l == 1:
                                e.wait_ge(q["bv_ready"], st + 1)
                            alone(e)
                            if l < LEVELS - 1:
                                heads(B[d][1][:, :], g["TT"], g["ys"]).then_inc(q["z_psum"], 1)
                            heads(B[d][2][:, :], g["ys"], g["TT"]).then_inc(q["zt_psum"], 1)
                    for d in range(2):
                        g, q = gdn[d], gs[d]
                        e.wait_ge(q["state_new"], st + it + 1)
                        e.wait_ge(q["kbe_qg"], st * 2 + 2)
                        alone(e)
                        heads(B[d][0][:, :], g["kbe"], g["st"]).then_inc(q["ks_psum"], 1)
                    for d in range(2):
                        g, q = gdn[d], gs[d]
                        e.wait_ge(q["r_ready"], st + 1)
                        e.wait_ge(q["tt_ready"], st * 6 + 6)
                        alone(e)
                        heads(B[d][1][:, :], g["TT"], g["r"]).then_inc(q["vn_psum"], 1)
                    if not last:
                        for d in range(2):
                            e.wait_ge(gs[d]["mt_at"], st * 2 + 2)
                        decays(st + 1)
                    for d in range(2):
                        g, q = gdn[d], gs[d]
                        e.wait_ge(q["vn_ready"], st + 1)
                        alone(e)
                        if not last:
                            betas(d)
                        heads(B[d][2][:, :], g["kg"], g["vn"])
                        for p in range(PAIRS):
                            w = slice(p * P, (p + 1) * P)
                            t = slice(p * CH, (p + 1) * CH)
                            e.matmul(B[d][0][:, t], g["st"][:, w], g["qg"][:, t], start=True, stop=False)
                            mm = e.matmul(B[d][0][:, t], g["vn"][:, w], g["at"][:, t], start=False, stop=True)
                        mm.then_inc(q["o_psum"], 1)

                decays(it * NCH)
                for d in range(2):
                    betas(d)
                with e.Fori(0, NCH - 1) as n:
                    step(n, False)
                step(NCH - 1, True)
                head_sums(8, 4, 2)

                e.wait_ge(ylo_ready, it * PAIRS + PAIRS + 1)
                dense_pair(0, B_OUT, T_OUT, 4, L_Y - 4)
                dense_pair(1, B_OUT, T_OUT)

                def ffn_sums(i, first=False, last=False):
                    for j in range(2):
                        sum_squares(c("ones"), n0 + N_FFN, q0, i * 2 + (Q_FFN + j), j,
                                    first and j == 0, last and j == 1)

                ffn_sums(0, first=True)
                with e.Fori(2, W_OUT // 2) as i:
                    dense_pair(i, B_OUT, T_OUT)
                    ffn_sums(i - 1)
                ffn_sums(W_OUT // 2 - 1, last=True)
                dense_pair(0, B_GU, T_GU, 0, L_FFN)
                with e.Fori(1, NF) as f:
                    dense_pair(f, B_GU, T_GU)
                def down_pair(i):
                    for j in range(2):
                        e.wait_ge(tile_free[j], it * (TILES // 2) + (i + (T_DOWN // 2 + 1)))
                        k0 = 0
                        for r, nk in enumerate(DOWN_K):
                            weights(i * 6 + (B_DOWN + 3 * j + r))
                            e.wait_ge(lo_ready, l0 + (L_A + k0 + nk + 2))
                            for k in range(nk):
                                mm = three(bank[j][:, :], w_part((3 * j + r) % 2, k * P, P),
                                           (A_hi[:, k0 + k, :], A_lo[:, k0 + k, :]), k0 + k == 0, k0 + k == NF - 1)
                            mm.then_inc(tile_ready if r == 2 else down_part, 1)
                            k0 += nk

                down_pair(0)
                for k in range(KD):
                    sum_squares(c("ones"), n0 + SUMS, q0 + SQUARES, k, k % 2, k == 0, k == KD - 1)
                with e.Fori(1, KD // 2) as i:
                    down_pair(i)

            n0, q0 = DEPTH * NSEQ * SUMS + 1, DEPTH * NSEQ * SQUARES + KD
            for k in range(KD):
                sum_squares(c("ones"), n0, q0, k, k % 2, k == 0, k == KD - 1)


def blocks(w, tiles):
    depth, k, n = w.shape
    w = w.reshape(depth, k // P, P, tiles, n // tiles)
    return np.ascontiguousarray(w.transpose(0, 3, 2, 1, 4).reshape(depth * tiles, P, -1))


def kernel(**inputs):
    import concourse.bacc as bacc
    from concourse.bass_utils import run_bass_kernel_spmd

    a = {k: np.asarray(v) for k, v in inputs.items()}
    swap = np.r_[ROPE // 2:ROPE, 0:ROPE // 2]
    w = a["w_in"]
    lat = Q_LORA + KV_LORA
    rope_, rest = w[:, :, lat:lat + ROPE], w[:, :, lat + ROPE:]
    qkvz, ab = rest[:, :, :2048], rest[:, :, 2048:]
    nothing = np.zeros_like(w[:, :, :16])
    w_in = np.concatenate([w[:, :, :lat], ab[:, :, :16], nothing, ab[:, :, 16:], nothing, rope_, rope_[:, :, swap],
                           qkvz], 2)
    wq = a["w_q_up"].reshape(DEPTH, Q_LORA, HEADS, QK)
    wq = np.concatenate([wq, wq[..., NOPE + swap]], 3).reshape(DEPTH, Q_LORA, HEADS * P)
    wkv = a["w_kv_up"].reshape(DEPTH, KV_LORA, HEADS, 2, NOPE)
    wkv = wkv.transpose(0, 3, 1, 2, 4).reshape(DEPTH * 2, KV_LORA, HEADS * NOPE)
    gu = np.stack([a["w_gate"].reshape(DEPTH, D, NF, P), a["w_up"].reshape(DEPTH, D, NF, P)], 3)
    gu = gu.reshape(DEPTH, D, 2 * FF)

    par = np.zeros((DEPTH, P, NPAR), np.float32)
    par[:, :, C_NF:C_NF + 8] = a["norm_ffn"].reshape(DEPTH, KD, P).transpose(0, 2, 1)
    par[:, :, C_QN:C_QN + 2] = a["q_norm"].reshape(DEPTH, 2, P).transpose(0, 2, 1)
    par[:, :, C_KVN] = a["kv_norm"]
    par[:, :, C_CONV:C_CONV + 36] = a["conv_w"].reshape(DEPTH, 3, 12, P).transpose(0, 3, 2, 1).reshape(DEPTH, P, 36)
    par[:, :16, C_DT] = a["dt_bias"].reshape(DEPTH, 16)
    par[:, :16, C_ALOG] = a["a_log"].reshape(DEPTH, 16)
    par[:, :, C_GN] = np.concatenate([a["gdn_norm"]] * 2, 1)

    arrays = {
        "xT": np.stack([a["x_prompt"][0], a["x_sample"][0]]).reshape(NSEQ, S, KD, P).transpose(0, 2, 3, 1),
        "w_in": blocks(w_in, W_IN), "w_q": blocks(wq, W_Q), "w_kv": wkv, "w_out": blocks(a["w_out"], W_OUT),
        "w_gu": blocks(gu, W_GU), "w_down": blocks(a["w_down"], KD), "par": par,
        "gains": np.concatenate([a["norm_attn"], a["norm_final"][None]]).reshape(DEPTH + 1, KD, P).transpose(2, 0, 1),
        "const": constants()[0],
    }
    arrays = {k: np.ascontiguousarray(v) for k, v in arrays.items()}
    nc = bacc.Bacc("TRN2", target_bir_lowering=False, num_devices=1)
    args = [nc.dram_tensor(k, v.shape, mybir.dt.from_np(v.dtype), kind="ExternalInput").ap() for k, v in arrays.items()]
    args.append(nc.dram_tensor("out", (NSEQ, KD, P, S), F32, kind="ExternalOutput").ap())
    build(nc, *args)
    got = run_bass_kernel_spmd(nc, [arrays], core_ids=[0]).results[0]["out"]
    y = got.reshape(NSEQ, D, S).transpose(0, 2, 1)
    return y[0:1], y[1:2]
```
